# Optimizing a Trainium2 kernel written in Bass

```python
import math, functools
import jax, jax.numpy as jnp
from jax import lax
import numpy as np

D_MODEL = 2048
BATCH = 1
SEQ = 256
DEPTH = 1
DEC_BATCH = 8
DEC_SEQ = 4
PAST_LEN = 256
PAGE_SIZE = 128

MIX_W = D_MODEL
HG_W = MIX_W // 2
SB_W = MIX_W - HG_W
HG_DK = 128
HG_HEADS = HG_W // HG_DK
HG_DV = HG_W // HG_HEADS
SB_DH = 128
SB_HEADS = SB_W // SB_DH
IN_W = 4 * HG_W + 3 * SB_W
HG_CHUNK = 64
SB_QBLOCK = 128
SB_SCALE = 1.0 / math.sqrt(SB_DH)
SB_BIAS_INIT = -6.0
N_GROUPS = 4
EXPERTS_PER_GROUP = 8
N_EXPERTS = N_GROUPS * EXPERTS_PER_GROUP
TOP_K = 2
EXPERT_FF = D_MODEL // 4
ALPHA = (2.0 * DEPTH) ** 0.25
BETA = (8.0 * DEPTH) ** -0.25
LN_EPS = 1e-5
RMS_EPS = 1e-6

kernel_name = 'hymba_hgrn2_stickbreak_hmoe_step'

def layer_norm(x, g, b):
    xf = x.astype(jnp.float32)
    mu = jnp.mean(xf, axis=-1, keepdims=True)
    var = jnp.mean(jnp.square(xf - mu), axis=-1, keepdims=True)
    return ((xf - mu) * lax.rsqrt(var + LN_EPS) * g + b).astype(x.dtype)

def rms_norm(x, g):
    xf = x.astype(jnp.float32)
    return xf * lax.rsqrt(jnp.mean(jnp.square(xf), axis=-1, keepdims=True) + RMS_EPS) * g

def hgrn2_chunked(q, log_f, k, v, s0, chunk):
    B, T, H, _ = q.shape
    n = T // chunk

    def to_chunks(a):
        return a.reshape(B, n, chunk, H, a.shape[-1]).transpose(1, 0, 3, 2, 4)

    tri = jnp.tril(jnp.ones((chunk, chunk), bool))

    def step(S, inp):
        qc, gc, kc, vc = inp
        b = jnp.cumsum(gc, axis=2)
        o_inter = jnp.einsum('bhtk,bhkv->bhtv', qc * jnp.exp(b), S)
        diff = b[:, :, :, None, :] - b[:, :, None, :, :]
        decay = jnp.exp(jnp.where(tri[:, :, None], diff, -jnp.inf))
        a = jnp.einsum('bhtk,bhsk,bhtsk->bhts', qc, kc, decay)
        o_intra = jnp.einsum('bhts,bhsv->bhtv', a, vc)
        b_last = b[:, :, -1]
        S_new = jnp.exp(b_last)[..., None] * S + jnp.einsum(
            'bhsk,bhsv->bhkv', kc * jnp.exp(b_last[:, :, None] - b), vc)
        return S_new, o_inter + o_intra

    s_fin, o = lax.scan(step, s0, (to_chunks(q), to_chunks(log_f), to_chunks(k), to_chunks(v)))
    o = o.transpose(1, 0, 3, 2, 4).reshape(B, T, H, v.shape[-1])
    return o, s_fin

def stick_breaking(q, k, v, bias, q_pos, k_pos):
    z = (jnp.einsum('bqhd,bkhd->bhqk', q, k) * SB_SCALE
         + bias.astype(jnp.float32)[None, :, None, None])
    mask = k_pos[None, :] < q_pos[:, None]
    log_1mb = jnp.where(mask, jax.nn.log_sigmoid(-z), 0.0)
    later = lax.cumsum(log_1mb, axis=3, reverse=True) - log_1mb
    a = jnp.where(mask, jnp.exp(jax.nn.log_sigmoid(z) + later), 0.0)
    return jnp.einsum('bhqk,bkhd->bqhd', a, v)

def sb_prompt(q, k, v, bias):
    B, T, H, Dh = q.shape
    nb = T // SB_QBLOCK
    qb = q.reshape(B, nb, SB_QBLOCK, H, Dh).transpose(1, 0, 2, 3, 4)
    k_pos = jnp.arange(T)

    def one(args):
        q_blk, start = args
        return stick_breaking(q_blk, k, v, bias, start + jnp.arange(SB_QBLOCK), k_pos)

    o = lax.map(one, (qb, jnp.arange(nb) * SB_QBLOCK))
    return o.transpose(1, 0, 2, 3, 4).reshape(B, T, H, Dh)

def sb_sample(q, k, v, bias, cache_k_l, cache_v_l, page_table):
    DB, S, H, Dh = q.shape
    past = page_table.shape[1] * cache_k_l.shape[1]
    pk = cache_k_l[page_table].reshape(DB, past, H, Dh).astype(jnp.float32)
    pv = cache_v_l[page_table].reshape(DB, past, H, Dh).astype(jnp.float32)
    keys = jnp.concatenate([pk, k], axis=1)
    vals = jnp.concatenate([pv, v], axis=1)
    return stick_breaking(q, keys, vals, bias, past + jnp.arange(S), jnp.arange(past + S))

def hier_moe(u, w_gr, b_gr, w_er, b_er, w_gate, w_up, w_down):
    B, T, D = u.shape
    h = u.reshape(B * T, D)
    g_logits = (h @ w_gr + b_gr).astype(jnp.float32)
    g_idx = jnp.argmax(g_logits, axis=-1)
    g_w = jnp.take_along_axis(jax.nn.softmax(g_logits, axis=-1), g_idx[:, None], axis=-1)
    e_logits = (jnp.einsum('nd,dge->nge', h, w_er) + b_er).astype(jnp.float32)
    e_sel = jnp.take_along_axis(e_logits, g_idx[:, None, None], axis=1)[:, 0]
    top_val, top_idx = lax.top_k(e_sel, TOP_K)
    gate = g_w * jax.nn.softmax(top_val, axis=-1)
    eid = g_idx[:, None] * EXPERTS_PER_GROUP + top_idx
    dense_gate = jnp.sum(jax.nn.one_hot(eid, N_EXPERTS, dtype=jnp.float32) * gate[..., None], axis=1)
    y = jnp.zeros((B * T, D), jnp.float32)
    for e in range(N_EXPERTS):
        hid = jax.nn.silu(h @ w_gate[e]) * (h @ w_up[e])
        y = y + dense_gate[:, e:e + 1] * (hid @ w_down[e])
    return y.reshape(B, T, D).astype(u.dtype)

def decoder_layer(x, c, s0, sb_attend, lb, w_ada, b_ada, w_in, hg_norm, sb_norm, sb_bias, w_o,
                  ln1_g, ln1_b, w_gr, b_gr, w_er, b_er, w_gate, w_up, w_down, ln2_g, ln2_b):
    B, T, _ = x.shape
    ada = jnp.einsum('bd,de->be', jax.nn.silu(c), w_ada) + b_ada
    sh1, sc1, g1, sh2, sc2, g2 = jnp.split(ada[:, None, :], 6, axis=-1)
    u = x * (1 + sc1) + sh1
    proj = (u @ w_in).astype(jnp.float32)
    hq, hf, hi, hg, sq, sk, sv = jnp.split(proj, np.cumsum([HG_W] * 4 + [SB_W] * 2).tolist(), axis=-1)
    f = lb + (1.0 - lb) * jax.nn.sigmoid(hf)
    hshape = (B, T, HG_HEADS, HG_DK)
    chunk = math.gcd(HG_CHUNK, T)
    o_h, s_fin = hgrn2_chunked(jax.nn.silu(hq).reshape(hshape), jnp.log(f).reshape(hshape),
                               (1.0 - f).reshape(hshape), hi.reshape(B, T, HG_HEADS, HG_DV),
                               s0.astype(jnp.float32), chunk)
    o_h = rms_norm(o_h, hg_norm) * jax.nn.silu(hg.reshape(B, T, HG_HEADS, HG_DV))
    sshape = (B, T, SB_HEADS, SB_DH)
    k_sb = sk.reshape(sshape)
    v_sb = sv.reshape(sshape)
    o_s = rms_norm(sb_attend(sq.reshape(sshape), k_sb, v_sb, sb_bias), sb_norm)
    mix = jnp.concatenate([o_h.reshape(B, T, HG_W), o_s.reshape(B, T, SB_W)], axis=-1).astype(u.dtype) @ w_o
    x = layer_norm(ALPHA * x + g1 * mix, ln1_g, ln1_b)
    u2 = x * (1 + sc2) + sh2
    x = layer_norm(ALPHA * x + g2 * hier_moe(u2, w_gr, b_gr, w_er, b_er, w_gate, w_up, w_down), ln2_g, ln2_b)
    return x, s_fin, k_sb, v_sb

def setup_inputs(seed: int = 0) -> dict:
    key = jax.random.key(seed)
    ks = jax.random.split(key, 27)
    f32 = jnp.float32
    n_pages = PAST_LEN // PAGE_SIZE
    n_used = DEC_BATCH * n_pages
    n_phys = n_used + max(1, n_used // 4)
    L = DEPTH

    def nrm(k, shape, s):
        return jax.random.normal(k, shape, f32) * s

    col_scale = jnp.concatenate([jnp.ones(HG_W), jnp.ones(HG_W), jnp.full(HG_W, BETA), jnp.ones(HG_W),
                                 jnp.ones(SB_W), jnp.ones(SB_W), jnp.full(SB_W, BETA)]).astype(f32)
    page_table = jax.random.permutation(ks[5], n_phys)[:n_used].reshape(DEC_BATCH, n_pages).astype(jnp.int32)
    return {
        'x_prompt': nrm(ks[0], (BATCH, SEQ, D_MODEL), 1.0),
        'x_sample': nrm(ks[1], (DEC_BATCH, DEC_SEQ, D_MODEL), 1.0),
        'cache_k': nrm(ks[2], (L, n_phys, PAGE_SIZE, SB_HEADS, SB_DH), 1.0),
        'cache_v': nrm(ks[3], (L, n_phys, PAGE_SIZE, SB_HEADS, SB_DH), 1.0),
        'state_hgrn': nrm(ks[4], (L, DEC_BATCH, HG_HEADS, HG_DK, HG_DV), 0.5),
        'page_table': page_table,
        'c_prompt': nrm(ks[6], (BATCH, D_MODEL), 1.0),
        'c_sample': nrm(ks[7], (DEC_BATCH, D_MODEL), 1.0),
        'hg_lb_logits': nrm(ks[8], (L + 1, HG_W), 0.5),
        'w_ada': nrm(ks[9], (L, D_MODEL, 6 * D_MODEL), 0.5 * D_MODEL ** -0.5),
        'b_ada': nrm(ks[10], (L, 6 * D_MODEL), 0.02),
        'w_in': nrm(ks[11], (L, D_MODEL, IN_W), D_MODEL ** -0.5) * col_scale,
        'hg_norm': 1.0 + nrm(ks[12], (L, HG_DV), 0.05),
        'sb_norm': 1.0 + nrm(ks[13], (L, SB_DH), 0.05),
        'sb_bias': SB_BIAS_INIT + nrm(ks[26], (L, SB_HEADS), 0.3),
        'w_o': nrm(ks[14], (L, MIX_W, D_MODEL), BETA * MIX_W ** -0.5),
        'ln1_g': 1.0 + nrm(ks[15], (L, D_MODEL), 0.05),
        'ln1_b': nrm(ks[16], (L, D_MODEL), 0.01),
        'w_gr': nrm(ks[17], (L, D_MODEL, N_GROUPS), D_MODEL ** -0.5),
        'b_gr': nrm(ks[18], (L, N_GROUPS), 0.01),
        'w_er': nrm(ks[19], (L, D_MODEL, N_GROUPS, EXPERTS_PER_GROUP), D_MODEL ** -0.5),
        'b_er': nrm(ks[20], (L, N_GROUPS, EXPERTS_PER_GROUP), 0.01),
        'w_gate': nrm(ks[21], (L, N_EXPERTS, D_MODEL, EXPERT_FF), D_MODEL ** -0.5),
        'w_up': nrm(ks[22], (L, N_EXPERTS, D_MODEL, EXPERT_FF), D_MODEL ** -0.5),
        'w_down': nrm(ks[23], (L, N_EXPERTS, EXPERT_FF, D_MODEL), BETA * EXPERT_FF ** -0.5),
        'ln2_g': 1.0 + nrm(ks[24], (L, D_MODEL), 0.05),
        'ln2_b': nrm(ks[25], (L, D_MODEL), 0.01),
    }

def reference(x_prompt, x_sample, cache_k, cache_v, state_hgrn, page_table, c_prompt, c_sample,
              hg_lb_logits, w_ada, b_ada, w_in, hg_norm, sb_norm, sb_bias, w_o, ln1_g, ln1_b,
              w_gr, b_gr, w_er, b_er, w_gate, w_up, w_down, ln2_g, ln2_b):
    lower_bounds = jnp.cumsum(jax.nn.softmax(hg_lb_logits.astype(jnp.float32), axis=0), axis=0)
    hp, hs = x_prompt, x_sample
    s0_prompt = jnp.zeros((x_prompt.shape[0], HG_HEADS, HG_DK, HG_DV), jnp.float32)
    kp_l, vp_l, sp_l, ks_l, vs_l, ss_l = [], [], [], [], [], []
    for l in range(DEPTH):
        lw = (lower_bounds[l], w_ada[l], b_ada[l], w_in[l], hg_norm[l], sb_norm[l], sb_bias[l], w_o[l],
              ln1_g[l], ln1_b[l], w_gr[l], b_gr[l], w_er[l], b_er[l], w_gate[l], w_up[l],
              w_down[l], ln2_g[l], ln2_b[l])
        hp, sp, kp, vp = decoder_layer(hp, c_prompt, s0_prompt, sb_prompt, *lw)
        attend = functools.partial(sb_sample, cache_k_l=cache_k[l], cache_v_l=cache_v[l],
                                   page_table=page_table)
        hs, ss, ksm, vsm = decoder_layer(hs, c_sample, state_hgrn[l], attend, *lw)
        kp_l.append(kp)
        vp_l.append(vp)
        sp_l.append(sp)
        ks_l.append(ksm)
        vs_l.append(vsm)
        ss_l.append(ss)
    return (hp, hs, jnp.stack(kp_l), jnp.stack(vp_l), jnp.stack(sp_l),
            jnp.stack(ks_l), jnp.stack(vs_l), jnp.stack(ss_l))


_drawn_inputs = setup_inputs


def setup_inputs(seed=0):
    import zlib

    import numpy as np

    out = dict(_drawn_inputs(seed))
    spreads = {}
    factors = {'hg_norm': 8.0,
     'sb_norm': 8.0,
     'sb_bias': 8.0,
     'ln1_b': 5.545,
     'b_gr': 104.411,
     'b_er': 50.911,
     'ln2_b': 5.471}
    for name, (base, spread) in spreads.items():
        noise = np.random.default_rng([zlib.crc32(name.encode()), seed]).standard_normal(out[name].shape)
        drawn = base * np.exp(spread * noise) if base else spread * noise
        out[name] = __import__('jax').numpy.asarray(drawn.astype(out[name].dtype))
    for name, factor in factors.items():
        out[name] = (out[name] * factor).astype(out[name].dtype)
    return out
```

```python
from contextlib import ExitStack

import concourse.bass as bass
from concourse import mybir

F32 = mybir.dt.float32
I32 = mybir.dt.int32
U32 = mybir.dt.uint32
ACT = mybir.ActivationFunctionType
ALU = mybir.AluOpType
AX = mybir.AxisListType.X

P = 128
D = 2048
KC = D // P
TP, NSEQ, SS = 256, 8, 4
TS = NSEQ * SS
T = TP + TS
H = 8
R = 1 + NSEQ
PAST, PAGE = 256, 128
NPG = PAST // PAGE
NPHYS = 20
SCALE = 128 ** -0.5
ALPHA = 2.0 ** 0.25
LN_EPS, RMS_EPS = 1e-5, 1e-6
NG, NEG, NE, FF = 4, 8, 32, 512
NL = NG + NE
B = 64
NBLK = NE + (2 * T) // B - 1
CH = 32
SLOTS = 8
MOE_CHUNKS = 12
TILES = [(0, 128), (128, 128), (256, 32)]
NEG_BIG = -1.0e30


def layer(nc, xT, cT, w_ada, b_adaT, b_g2, w_in, w_o, w_r, b_r, lb_logits, norms, sb_bias,
          ln1, ln2, cache_k, cache_v, page_table, state, w_gate, w_up, w_down,
          y_p, y_s, k_p, v_p, s_p, k_s, v_s, s_s, u2_rows, y_rows):
    with ExitStack() as ctx:
        def sb(name, shape, dt=F32):
            return ctx.enter_context(nc.sbuf_tensor(name, shape, dt))

        def sem(name):
            return ctx.enter_context(nc.semaphore(name))

        ps = ctx.enter_context(nc.psum_tensor("ps", [P, 8, 512], F32))
        ring = sb("ring", [P, SLOTS, D])

        ident = sb("ident", [P, P])
        tri = sb("tri", [P, P])
        ones = sb("ones", [P, P])
        causal = sb("causal", [P, 384])
        negmask = sb("negmask", [P, 384])
        chunkmask = sb("chunkmask", [P, P])
        strict4 = sb("strict4", [TS, TS])
        neg4 = sb("neg4", [TS, TS])
        incl4 = sb("incl4", [TS, TS])
        seqmask = sb("seqmask", [TS, NSEQ])
        rowsel = sb("rowsel", [P, P + TS])
        silu_c = sb("silu_c", [P, KC, 32])
        ctmp = sb("ctmp", [P, KC * R])
        cin = sb("cin", [P, KC * R])
        adaT = sb("adaT", [P, 5, KC, R])
        badaT = sb("badaT", [P, 5, KC])
        ada_rows = sb("ada_rows", [P, 512])
        bg2 = sb("bg2", [P, 512])
        lbt = sb("lbt", [P, 4, H])
        normw = sb("normw", [P, 2])
        biasb = sb("biasb", [P, H])
        ln1t = sb("ln1t", [P, 2, KC])
        epsr = sb("epsr", [P, 2])
        wr = sb("wr", [P, KC, NL])
        br = sb("br", [P, NL])
        pages = sb("pages", [1, NSEQ * NPG], I32)

        ARENA = 30700
        arena = sb("arena", [P, ARENA])

        def area(at, *shape, parts=P):
            n = 1
            for s in shape:
                n *= s
            assert at + n <= ARENA, (at, shape)
            v = arena[0:parts, at:at + n]
            if len(shape) == 1:
                return v
            names = "abcde"[:len(shape)]
            return v.rearrange(f"p ({' '.join(names)}) -> p {' '.join(names)}",
                               **{k: s for k, s in zip(names, shape)})

        uT = area(0, KC, T)
        mixT = uT
        SQ = 4608
        projT = area(SQ, 5 * H, T)
        sqT, skT = projT[:, 0:H, :], projT[:, H:2 * H, :]
        hq, hf, hg = (projT[:, (2 + i) * H:(3 + i) * H, :] for i in range(3))
        TOK = SQ + 5 * H * T
        tok = area(TOK, 6, 1024)
        TMP = TOK + 6 * 1024
        kstage = area(TMP, 3, 1024)
        zeros = area(TMP, D)
        zz = [area(TMP + 3072 + 1920 * i, 384) for i in range(2)]
        ee = [area(TMP + 3072 + 1920 * i + 384, 384) for i in range(2)]
        spl = [area(TMP + 3072 + 1920 * i + 768, 384) for i in range(2)]
        zn = [area(TMP + 3072 + 1920 * i + 1152, 384) for i in range(2)]
        aa = [area(TMP + 3072 + 1920 * i + 1536, 384) for i in range(2)]
        keyT = area(TMP, H, PAST)
        zrow = area(TMP + 2048, 512)
        apad = area(TMP, NPG, NSEQ, H, TS)
        zP = area(TMP + 4096, NPG * NSEQ, H, SS)
        eP = area(TMP + 4608, NPG * NSEQ, H, SS)
        sP = area(TMP + 5120, NPG * NSEQ, H, SS)
        dP = area(TMP + 5632, NPG * NSEQ, H, SS)
        zN = area(TMP + 6144, H, TS, parts=TS)
        eN = area(TMP + 6400, H, TS, parts=TS)
        sN = area(TMP + 6656, H, TS, parts=TS)
        dN = area(TMP + 6912, H, TS, parts=TS)
        aN = area(TMP + 7168, H, TS, parts=TS)
        orow = area(TMP + 7424, 2, P)
        qhat = area(SQ, H, T)
        khat = area(SQ + H * T, H, T)
        shist = area(SQ, 8, 4, P)
        bcum = area(TMP, H, T)
        t1 = area(TMP + 2304, H, T)
        reset = area(TMP + 4608, 4 * T)
        abuf = area(TMP + 5760, 2, H, P)
        abufs = area(TMP + 7808, H, TS, parts=TS)
        dec = area(TMP + 8064, H, 16)
        vblk = area(TMP + 4608, NSEQ, P, parts=TS)
        kdt = area(TMP + 2304, 2, 4, P)
        kdts = area(TMP + 3328, 4, P, parts=TS)
        qpad = area(TMP, 4, NSEQ, TS)
        s0 = [area(TOK + 1024 * i, NSEQ, P) for i in range(2)]
        snew = area(TOK + 2048, NSEQ, P)
        osr = area(TMP + 3840, P)
        sqo = [area(TMP + 4608 + T * i, T) for i in range(2)]
        rst = [area(TMP + 4608 + T * (2 + i), T) for i in range(2)]
        xa = area(4608, KC, T)
        rT = area(9216, KC, T)
        r2 = [area(13824 + T * i, T) for i in range(4)]
        mu = area(14976, T)
        rstd = area(15264, T)
        lt1 = area(15552, T)
        u2T = area(4608, KC, T)
        urow = [area(16384 + 2048 * i, D) for i in range(3)]
        RT = 28700
        mslot = [area(0 + D * i, D) for i in range(4)]
        xres = area(22528, 3, D)
        xg = area(8192, D, parts=B)
        xgT = area(10240, KC, B)
        hid = area(11264, 256)
        hsil = area(11520, 256)
        hT = area(11776, 2, P)
        yout = area(12032, 1024)
        g2p = area(13056, D)
        g2s = area(15104, D)
        ln2b = area(17152, 2, D)
        ya = [area(0, D), area(2048, D), area(4096, D)]
        yb = [area(6144, D), area(8192, D), area(10240, D)]

        slot_loaded = [sem(f"slot_loaded{i}") for i in range(SLOTS)]
        moe_loaded = [sem(f"moe_loaded{i}") for i in range(MOE_CHUNKS)]
        ring_used = sem("ring_used")
        moe_used = sem("moe_used")
        (x_loaded, c_loaded, small_loaded, late_loaded, pages_loaded, xa_loaded, kv_stored, sprompt_stored,
         ssample_stored, u2_stored, gathered, y_stored, out_stored) = (sem(n) for n in (
             "x_loaded", "c_loaded", "small_loaded", "late_loaded", "pages_loaded", "xa_loaded", "kv_stored",
             "sprompt_stored", "ssample_stored", "u2_stored", "gathered", "y_stored", "out_stored"))
        s0_loaded = [sem(f"s0_loaded{i}") for i in range(2)]
        fin_gather = [sem(f"fin_gather{i}") for i in range(3)]
        pool_step, dve_step, act_step = sem("pool_step"), sem("dve_step"), sem("act_step")
        consts_ready, expc_ready, silu_c_ready = sem("consts_ready"), sem("expc_ready"), sem("silu_c_ready")
        rows_copied, rows_turned, ada_ready = sem("rows_copied"), sem("rows_turned"), sem("ada_ready")
        u_ready, evac_act, evac_dve = sem("u_ready"), sem("evac_act"), sem("evac_dve")
        kout_pe, kout_evac = sem("kout_pe"), sem("kout_evac")
        (z_pe, z_dve, soft_act, sp_ready, c_pe, d_dve, a_ready, o_pe, o_evac) = (sem(n) for n in (
            "z_pe", "z_dve", "soft_act", "sp_ready", "c_pe", "d_dve", "a_ready", "o_pe", "o_evac"))
        kT_pe, kT_act, kT_dve, zr_pe, zr_dve, zt_pe, zt_dve = (
            sem(n) for n in ("kT_pe", "kT_act", "kT_dve", "zr_pe", "zr_dve", "zt_pe", "zt_dve"))
        ss_pe, ss_dve, ss_act = sem("ss_pe"), sem("ss_dve"), sem("ss_act")
        hg_pe, hg_dve, hg_act, vblk_ready, lb_act = (sem(n) for n in ("hg_pe", "hg_dve", "hg_act", "vblk_ready", "lb_act"))
        kd_pe, kd_act, u_pe, u_dve = sem("kd_pe"), sem("kd_act"), sem("u_pe"), sem("u_dve")
        us_pe, us_dve, os_pe = sem("us_pe"), sem("us_dve"), sem("os_pe")
        qpad_ready, osr_dve, osr_pe, osm_dve = (sem(n) for n in ("qpad_ready", "osr_dve", "osr_pe", "osm_dve"))
        hgo_pe, hgo_act = sem("hgo_pe"), sem("hgo_act")
        nsq_act, nm_pe, nrs_act, nm_dve = sem("nsq_act"), sem("nm_pe"), sem("nrs_act"), sem("nm_dve")
        xa_ready, wo_dve, wo_act, st_pe = sem("xa_ready"), sem("wo_dve"), sem("wo_act"), sem("st_pe")
        ln_dve, rstd_act, x1_act, u2_dve = sem("ln_dve"), sem("rstd_act"), sem("x1_act"), sem("u2_dve")
        rt_pe, rt_dve, rt_act, tt_pe, tt_act = (sem(n) for n in ("rt_pe", "rt_dve", "rt_act", "tt_pe", "tt_act"))
        plan_ready, idx_ready = sem("plan_ready"), sem("idx_ready")
        x_turned, x_copied = sem("x_turned"), sem("x_copied")
        sil_act, hid_dve, hT_pe, hT_dve, y_evac = (sem(n) for n in ("sil_act", "hid_dve", "hT_pe", "hT_dve", "y_evac"))
        g2_pe, g2_act = sem("g2_pe"), sem("g2_act")
        zeros_ready, y_zeroed = sem("zeros_ready"), sem("y_zeroed")
        wait_carrier = sem("wait_carrier")
        fin_dve, fin_act = sem("fin_dve"), sem("fin_act")

        def rta(at, *shape, parts=P):
            return area(RT + at, *shape, parts=parts)
        lg = rta(0, 3, NL)
        vm = rta(108, 3)
        gmax = rta(111, 3)
        gone = rta(114, 3, NG)
        gexp = rta(126, 3, NG)
        gw = rta(138, 3)
        pick = rta(141, 3, NG, NEG)
        esel = rta(237, 3, NEG)
        e1 = rta(261, 3, NEG)
        e2 = rta(285, 3, NEG)
        m1 = rta(309, 3)
        m2 = rta(312, 3)
        cand = rta(315, 3, NEG)
        oneh = [rta(339 + 96 * k, 3, NG, NEG) for k in range(2)]
        both = rta(531, 3, NE)
        rank = rta(627, 3, NE)
        cnt = rta(723, NE)
        nb = rta(755, NE)
        cum = rta(787, NE)
        base = rta(819, NE)
        tmp32 = rta(851, 3, NE)
        rk = rta(947, 3)
        blkr = rta(950, 3)
        sl = rta(953, 3)
        blk = rta(956, 3)
        tmp3 = rta(959, 3)
        onesNE = rta(962, NE)
        rsel = [rta(994 + 192 * k, 3, B) for k in range(2)]
        NB1 = NBLK + 1
        bsel = [rta(1378 + 123 * k, 3, NB1) for k in range(2)]
        eid = rta(1624, NB1, parts=1)
        ecmp = area(13824, NB1, NE, parts=1)
        gate2 = sb("gate2", [P, 2, 3])
        tokid = sb("tokid", [P, 3])
        iotab = sb("iotab", [P, B])
        rev4 = sb("rev4", [P, NEG])
        rowidx = sb("rowidx", [P, 2, 3], I32)
        gslot = sb("gslot", [P, 2, 3])
        lgT = sb("lgT", [NL, T])
        bnst = sb("bnst", [P, 4, 6])
        bnag = sb("bnag", [P, 2])
        rs1 = sb("rs1", [P, 1])
        plan = sb("plan", [1, NB1 + 1], I32)
        idxs = sb("idxs", [B, NB1], I32)
        idx1 = sb("idx1", [B, 1], I32)
        stri = sb("stri", [P, P])

        block = ctx.enter_context(nc.Block())

        def bc(ap, at, n):
            v = ap.unsqueeze(at)
            return v.to_broadcast([*v.shape[:at], n, *v.shape[at + 1:]])

        N_ADA01, N_PROJ, N_ADA23, N_K, N_V, N_ADA45, N_WO = 0, 32, 88, 120, 128, 136, 168
        N_END = 184

        def used(n):
            return SLOTS + n + 1

        def loaded(n):
            r = n // SLOTS
            return 16 * (r + 1 + (r >= N_K // SLOTS) + (r >= N_V // SLOTS))

        @block.sync
        def _(sp):
            def put(n_wait, slot, src):
                sp.wait_ge(ring_used, n_wait)
                sp.dma_start(ring[:, slot, :], src).then_inc(slot_loaded[slot], 16)

            def ada_sixths(first, last, n0):
                with sp.Fori(first, last) as g:
                    for t in range(KC):
                        put((g - first) * KC + (n0 + t + 1), t % SLOTS,
                            w_ada[bass.ds(g, 1), t].rearrange("g p n -> p (g n)"))

            sp.dma_start(cin[:], cT.rearrange("p m r -> p (m r)")).then_inc(c_loaded, 16)
            sp.dma_start(pages[:], page_table[:]).then_inc(pages_loaded, 16)
            ada_sixths(0, 2, N_ADA01)
            with sp.Fori(0, 7) as g:
                for c in range(SLOTS):
                    put(g * SLOTS + (N_PROJ + c + 1), c, w_in[bass.ds(g, 1), c].rearrange("g p n -> p (g n)"))
            ada_sixths(2, 4, N_ADA23)
            sp.wait_ge(pages_loaded, 16)
            for n0, cache in ((N_K, cache_k), (N_V, cache_v)):
                for b in range(NSEQ):
                    sp.wait_ge(ring_used, n0 + b + 1)
                    for pg in range(NPG):
                        i = b * NPG + pg
                        page = sp.value_load(pages[0:1, i:i + 1], min_val=0, max_val=NPHYS - 1)
                        sp.dma_start(ring[:, b, pg * 1024:(pg + 1) * 1024],
                                     cache[bass.ds(page, 1)].rearrange("g p n -> p (g n)")
                                     ).then_inc(slot_loaded[b], 16)
            ada_sixths(4, 6, N_ADA45)
            with sp.Fori(0, 2) as g:
                for c in range(SLOTS):
                    put(g * SLOTS + (N_WO + c + 1), c, w_o[bass.ds(g, 1), c].rearrange("g p n -> p (g n)"))
            sp.wait_ge(plan_ready, 1)
            nblocks = sp.value_load(plan[0:1, NB1:NB1 + 1], min_val=0, max_val=NBLK)
            with sp.Fori(0, NBLK) as i:
                with sp.If(i < nblocks):
                    e = sp.value_load(plan[0:1, bass.ds(i, 1)], min_val=0, max_val=NE - 1)
                    for c in range(MOE_CHUNKS):
                        dst = ring[:, c, :] if c < SLOTS else mslot[c - SLOTS]
                        if c < 8:
                            w, q = (w_gate, w_up)[c // 4], c % 4
                            src = w[bass.ds(e, 1)].rearrange("e (p t) n -> p (e t) n", p=P)[:, 4 * q:4 * q + 4, :]
                            dst = dst.rearrange("p (t n) -> p t n", t=4)
                        else:
                            q = c - 8
                            src = w_down[bass.ds(e, 1)].rearrange("e f n -> (e f) n")[P * q:P * (q + 1), :]
                        sp.wait_ge(moe_used, i * MOE_CHUNKS + (c + 1))
                        sp.dma_start(dst, src).then_inc(moe_loaded[c], 16)
            sp.wait_ge(y_stored, nblocks * 32 + 32)
            sp.sem_inc(wait_carrier, 1)
            sp.wait_ge(kv_stored, 6 * 16)
            sp.wait_ge(sprompt_stored, 2 * 16)
            sp.wait_ge(ssample_stored, H * 16)
            sp.wait_ge(u2_stored, 3 * 16)
            sp.wait_ge(out_stored, 3 * 16)

        @block.gpsimd
        def _(pool):
            count = [0]

            def link(ins):
                count[0] += 1
                ins.then_inc(pool_step, 1)
                pool.wait_ge(pool_step, count[0])

            def keep(view, pattern, base_, cm, fill, op=ALU.is_ge):
                link(nc.gpsimd.affine_select(out=view, in_=view, pattern=pattern, compare_op=op, fill=fill,
                                             base=base_, channel_multiplier=cm))

            pool.dma_start(uT, xT[:]).then_inc(x_loaded, 16)
            pool.dma_start(badaT[:], b_adaT[:]).then_inc(small_loaded, 16)
            pool.dma_start(lbt[:, 0:2, :], lb_logits[:]).then_inc(small_loaded, 16)
            pool.dma_start(normw[:], norms[:]).then_inc(small_loaded, 16)
            pool.dma_start(biasb[:], sb_bias.partition_broadcast(P)).then_inc(small_loaded, 16)
            pool.dma_start(ln1t[:], ln1[:]).then_inc(small_loaded, 16)
            pool.dma_start(wr[:], w_r[:]).then_inc(small_loaded, 16)
            pool.dma_start(br[:], b_r.partition_broadcast(P)).then_inc(small_loaded, 16)
            for j in range(4):
                pool.dma_start(bg2[32 * j:32 * j + 32, :], b_g2[j].partition_broadcast(32)).then_inc(small_loaded, 16)

            g = nc.gpsimd
            g.memset(ones[:], 1.0)
            g.memset(ident[:], 0.0)
            g.memset(tri[:], 1.0)
            g.memset(stri[:], 1.0)
            g.memset(causal[:], 1.0)
            g.memset(negmask[:], 0.0)
            g.memset(chunkmask[:], 1.0)
            g.memset(strict4[:], 1.0)
            g.memset(incl4[:], 1.0)
            g.memset(neg4[:], 0.0)
            g.memset(seqmask[:], 1.0)
            g.memset(rowsel[:], 0.0)
            g.iota(tokid[:], [[P, 3]], base=0, channel_multiplier=1, allow_small_or_imprecise_dtypes=True)
            g.iota(iotab[:], [[1, B]], base=0, channel_multiplier=0, allow_small_or_imprecise_dtypes=True)
            g.iota(rev4[:], [[-1, NEG]], base=NEG, channel_multiplier=0, allow_small_or_imprecise_dtypes=True)
            g.memset(epsr[:, 0:1], RMS_EPS)
            link(g.memset(epsr[:, 1:2], LN_EPS))
            keep(ident[:], [[-1, P]], 0, 1, 1.0, ALU.not_equal)
            keep(tri[:], [[-1, P]], 0, 1, 0.0)
            keep(stri[:], [[1, P]], -1, -1, 0.0)
            for v, fill in ((causal, 0.0), (negmask, NEG_BIG)):
                keep(v[:, 0:128], [[1, P]], -1, -1, fill)
                keep(v[:, 256:384], [[1, P]], -1, -1, fill)
            keep(chunkmask[:], [[1, P]], 0, -1, 0.0)
            v = chunkmask[:].rearrange("p (a b) -> p a b", b=CH)
            keep(v, [[-CH, P // CH], [0, CH]], 0, 1, 0.0)
            for m, lo, fill in ((strict4, -1, 0.0), (neg4, -1, NEG_BIG), (incl4, 0, 0.0)):
                keep(m[:], [[1, TS]], lo, -1, fill)
                v = m[:].rearrange("p (a b) -> p a b", b=SS)
                keep(v, [[-SS, NSEQ], [0, SS]], 0, 1, fill)
            keep(seqmask[:], [[-SS, NSEQ]], 0, 1, 0.0)
            keep(seqmask[:], [[SS, NSEQ]], SS - 1, -1, 0.0)
            link(g.memset(rowsel[0:1, 0:P], 1.0))
            link(g.memset(rowsel[0:TS, P:P + TS], 1.0))
            v = rowsel[0:TS, P:P + TS].rearrange("p (a b) -> p a b", b=SS)
            keep(v, [[-1, NSEQ], [0, SS]], -1, 1, 0.0, ALU.is_equal)
            for j in range(1, 4):
                link(g.tensor_copy(rowsel[32 * j:32 * j + 32, :], rowsel[0:32, :]))
            pool.sem_inc(consts_ready, 1)

            g.memset(zeros, 0.0).then_inc(zeros_ready, 1)
            pool.wait_ge(zeros_ready, 1)
            pool.wait_ge(u_ready, 1)
            pool.dma_start(y_rows.rearrange("(n p) d -> p n d", p=P), bc(zeros, 1, NBLK * B // P)
                           ).then_inc(y_zeroed, 16)

            pool.wait_ge(evac_act, 2 + 8 + 1)
            pool.wait_ge(evac_dve, 2 + 8 + 1)
            for i, (t0, tn) in enumerate(TILES):
                dst = v_p[t0:t0 + tn, :] if i < 2 else v_s[:]
                pool.dma_start(dst, tok[0:tn, i, :]).then_inc(kv_stored, 16)
            for i, (t0, tn) in enumerate(TILES):
                pool.wait_ge(kout_evac, i + 1)
                dst = k_p[t0:t0 + tn, :] if i < 2 else k_s[:]
                pool.dma_start(dst, kstage[0:tn, i, :]).then_inc(kv_stored, 16)

            pool.wait_ge(ss_pe, 3)
            pool.wait_ge(kv_stored, 6 * 16)
            for h in range(2):
                pool.dma_start(s0[h], state[:, h].rearrange("b p v -> p b v")).then_inc(s0_loaded[h], 16)
            pool.wait_ge(hg_dve, 2)
            for h in range(H):
                if h >= 1:
                    pool.wait_ge(us_pe, 2 * h)
                nc.gpsimd.tensor_tensor(vblk, bc(tok[0:TS, 5, h * P:(h + 1) * P], 1, NSEQ),
                                        bc(seqmask[:], 2, P), ALU.mult).then_inc(vblk_ready, 1)
                if h % 4 == 3:
                    pool.wait_ge(u_dve, 8 * (h // 4 + 1))
                    pool.dma_start(s_p[h - 3:h + 1].rearrange("h p v -> p h v"), shist[:, 7, :, :]
                                   ).then_inc(sprompt_stored, 16)
                pool.wait_ge(us_dve, 3 * (h + 1))
                pool.dma_start(s_s[:, h].rearrange("b p v -> p b v"), snew).then_inc(ssample_stored, 16)
                if h + 2 < H:
                    pool.wait_ge(os_pe, h + 1)
                    pool.dma_start(s0[h % 2], state[:, h + 2].rearrange("b p v -> p b v")
                                   ).then_inc(s0_loaded[h % 2], 16)

            pool.wait_ge(hgo_pe, 2)
            pool.wait_ge(sprompt_stored, 2 * 16)
            pool.dma_start(xa, xT[:]).then_inc(xa_loaded, 16)
            pool.wait_ge(xa_loaded, 16)
            nc.gpsimd.tensor_scalar(xa, xa, ALPHA, 0.0, ALU.mult, ALU.add).then_inc(xa_ready, 1)

            for i, (t0, tn) in enumerate(TILES):
                pool.wait_ge(tt_act, 4 * (i + 1))
                pool.dma_start(u2_rows[t0:t0 + tn, :], urow[i][0:tn, :]).then_inc(u2_stored, 16)
            pool.wait_ge(plan_ready, 2)
            nblocks = pool.value_load(plan[0:1, NB1:NB1 + 1], min_val=0, max_val=NBLK)
            pool.wait_ge(u2_stored, 3 * 16)

            def gather(n):
                pool.wait_ge(idx_ready, n)
                pool.sem_inc(wait_carrier, 1)
                nc.gpsimd.indirect_dma_start(out=xg, out_offset=None, in_=u2_rows[:],
                                             in_offset=bass.IndirectOffsetOnAxis(idx1[:, 0:1], 0)
                                             ).then_inc(gathered, 16)

            nc.gpsimd.tensor_copy(idx1[:], idxs[:, 0:1]).then_inc(idx_ready, 1)
            pool.wait_ge(tt_act, 24)
            gather(1)
            pool.dma_start(ln2b, ln2.partition_broadcast(P)).then_inc(late_loaded, 16)
            with pool.Fori(0, NBLK) as i:
                with pool.If(i < nblocks):
                    pool.wait_ge(gathered, i * 16 + 16)
                    nc.gpsimd.tensor_copy(idx1[:], idxs[:, bass.ds(i + 1, 1)]).then_inc(idx_ready, 1)
                    pool.wait_ge(x_turned, i + 1)
                    gather(i + 2)
            pool.wait_ge(y_stored, nblocks * 32 + 32)
            pool.wait_ge(gathered, nblocks * 16 + 16)
            pool.wait_ge(x_copied, nblocks + 1)
            pool.sem_inc(wait_carrier, 1)
            for i, (t0, tn) in enumerate(TILES):
                for k, dst in enumerate((ya, yb)):
                    nc.gpsimd.indirect_dma_start(out=dst[i][0:tn, :], out_offset=None, in_=y_rows[:],
                                                 in_offset=bass.IndirectOffsetOnAxis(rowidx[0:tn, k, i:i + 1], 0)
                                                 ).then_inc(fin_gather[i], 16)

        @block.tensor
        def _(pe):
            mm = nc.tensor.matmul

            def ada_chunk(n, six, t):
                pe.wait_ge(slot_loaded[n % SLOTS], loaded(n))
                if t == 0 and six >= 1:
                    pe.wait_ge(rows_copied, six)
                for j in range(4):
                    last = mm(ps[32 * j:32 * j + 32, 0, :], silu_c[:, t, :], ring[:, n % SLOTS, 512 * j:512 * (j + 1)],
                              start=(t == 0), stop=(t == KC - 1))
                last.then_inc(ring_used, 1)

            def ada_turn(six):
                pe.wait_ge(rows_copied, six + 1)
                if six >= 1:
                    pe.wait_ge(ada_ready, six)
                for c in range(4):
                    last = nc.tensor.transpose(ps[:, 1, P * c:P * (c + 1)], ada_rows[:, P * c:P * (c + 1)], ident[:])
                last.then_inc(rows_turned, 1)

            pe.sem_inc(ring_used, SLOTS)
            pe.sem_inc(hT_pe, 1)
            pe.wait_ge(silu_c_ready, 1)
            pe.wait_ge(consts_ready, 1)
            for six in range(2):
                for t in range(KC):
                    ada_chunk(N_ADA01 + six * KC + t, six, t)
                ada_turn(six)

            pe.wait_ge(u_ready, 1)

            def heads_feature_major(trips, n0, done):
                with pe.Fori(0, trips) as g:
                    for c in range(SLOTS):
                        pe.wait_ge(slot_loaded[c], g * 16 + loaded(n0 + c))
                        pe.wait_ge((evac_act, evac_dve)[c % 2], g * 4 + (done + c // 2 - 1))
                        for t in range(KC):
                            last = mm(ps[:, 4 + c % 4, 0:T], ring[:, c, P * t:P * (t + 1)], uT[:, t, :],
                                      start=(t == 0), stop=(t == KC - 1))
                        last.then_inc(ring_used, 1)

            heads_feature_major(2, N_PROJ, 2)
            with pe.Fori(0, 2) as g:
                for s, banks in enumerate(((4, 5, 6), (7, 2, 3))):
                    pe.wait_ge(evac_act, g + 10)
                    pe.wait_ge(evac_dve, g + 10)
                    for q in range(4):
                        c = 4 * s + q
                        pe.wait_ge(slot_loaded[c], g * 16 + loaded(N_PROJ + 2 * SLOTS + c))
                        for t in range(4):
                            for (t0, tn), bank in zip(TILES, banks):
                                last = mm(ps[0:tn, bank, :], uT[:, 4 * q + t, t0:t0 + tn],
                                          ring[:, c, 512 * t:512 * (t + 1)],
                                          start=(q == 0 and t == 0), stop=(q == 3 and t == 3))
                        last.then_inc(ring_used, 1)
            pe.wait_ge(evac_act, 12)
            pe.wait_ge(evac_dve, 12)
            heads_feature_major(3, N_PROJ + 4 * SLOTS, 12)
            pe.wait_ge(evac_act, 24)
            pe.wait_ge(evac_dve, 24)

            for i, (t0, tn) in enumerate(TILES):
                for h in range(H):
                    last = nc.tensor.transpose(ps[0:tn, 2 + 2 * i + h // 4, P * (h % 4):P * (h % 4 + 1)],
                                               skT[:, h, t0:t0 + tn], ident[:])
                last.then_inc(kout_pe, 1)
            pe.wait_ge(kout_evac, 3)

            for h in range(H + 2):
                if h < H:
                    if h >= 2:
                        pe.wait_ge(z_dve, h - 1)
                    z = ps[:, 2 + h % 2, :]
                    mm(z[:, 0:256], skT[:, h, 0:128], sqT[:, h, 0:256], start=True, stop=True)
                    mm(z[:, 256:384], skT[:, h, 128:256], sqT[:, h, 128:256], start=True, stop=True
                       ).then_inc(z_pe, 1)
                if 1 <= h <= H:
                    k = h - 1
                    pe.wait_ge(sp_ready, k + 1)
                    if k >= 2:
                        pe.wait_ge(d_dve, k - 1)
                    c, s = ps[:, 4 + k % 2, :], spl[k % 2]
                    mm(c[:, 0:256], tri[:], s[:, 0:256], start=True, stop=False)
                    mm(c[:, 128:256], ones[:], s[:, 256:384], start=False, stop=True)
                    mm(c[:, 256:384], tri[:], s[:, 256:384], start=True, stop=True).then_inc(c_pe, 1)
                if h >= 2:
                    k = h - 2
                    pe.wait_ge(a_ready, k + 1)
                    if k >= 2:
                        pe.wait_ge(o_evac, k - 1)
                    o, a = ps[:, 6 + k % 2, :], aa[k % 2]
                    mm(o[:, 0:256], tok[:, 0, P * k:P * (k + 1)], a[:, 0:256], start=True, stop=False)
                    mm(o[:, 128:256], tok[:, 1, P * k:P * (k + 1)], a[:, 256:384], start=False, stop=True
                       ).then_inc(o_pe, 1)
                if h == 4:
                    ada_turn(2)
                if h == 8:
                    ada_turn(3)
                if h < H:
                    for t in range(4 * (h % 4), 4 * (h % 4) + 4):
                        ada_chunk(N_ADA23 + KC * (h // 4) + t, 2 + h // 4, t)

            pe.wait_ge(o_evac, H)
            pe.wait_ge(d_dve, H)

            def turn_keys(b):
                pe.wait_ge(slot_loaded[b], loaded(N_K + b))
                if b >= 1:
                    pe.wait_ge(kT_act, b)
                    pe.wait_ge(kT_dve, b)
                for pg in range(NPG):
                    for h in range(H):
                        last = nc.tensor.transpose(ps[:, 2 + 2 * pg + h // 4, P * (h % 4):P * (h % 4 + 1)],
                                                   ring[:, b, 1024 * pg + P * h:1024 * pg + P * (h + 1)], ident[:])
                    last.then_inc((kT_pe, ring_used)[pg], 1)

            turn_keys(0)
            for b in range(NSEQ):
                pe.wait_ge(kT_act, b + 1)
                pe.wait_ge(kT_dve, b + 1)
                if b >= 1:
                    pe.wait_ge(zr_dve, b)
                for h in range(H):
                    i, j = h // 4, h % 4
                    last = mm(ps[32 * j:32 * j + 32, 6, 256 * i:256 * (i + 1)], sqT[:, h, TP:T], keyT[:, h, :],
                              start=True, stop=True)
                last.then_inc(zr_pe, 1)
                if b + 1 < NSEQ:
                    turn_keys(b + 1)
                pe.wait_ge(zr_dve, b + 1)
                if b >= 1:
                    pe.wait_ge(zt_dve, b)
                for pg in range(NPG):
                    for i in range(2):
                        q = 2 * pg + i
                        last = nc.tensor.transpose(ps[:, 7, P * q:P * (q + 1)],
                                                   zrow[:, 256 * i + P * pg:256 * i + P * (pg + 1)], ident[:])
                last.then_inc(zt_pe, 1)
            for h in range(H):
                last = mm(ps[0:TS, 2, TS * h:TS * (h + 1)], skT[:, h, TP:T], sqT[:, h, TP:T], start=True, stop=True)
            last.then_inc(ss_pe, 1)
            pe.wait_ge(ss_dve, 2)
            c = ps[:, 3, :].rearrange("p (g b h t) -> p g b h t", g=NPG, b=NSEQ, h=H)
            s_new = sN.rearrange("p h (b t) -> p b h t", t=SS)
            s_past = sP.rearrange("p (g b) h t -> p g (b h t)", g=NPG)
            cf = ps[:, 3, :].rearrange("p (g n) -> p g n", g=NPG)
            mm(cf[:, 1], tri[:], s_past[:, 1], start=True, stop=False)
            mm(c[:, 1], ones[0:TS, :], s_new, start=False, stop=True)
            mm(cf[:, 0], tri[:], s_past[:, 0], start=True, stop=False)
            mm(cf[:, 0], ones[:], s_past[:, 1], start=False, stop=False)
            mm(c[:, 0], ones[0:TS, :], s_new, start=False, stop=True)
            mm(ps[0:TS, 4, 0:TS * H], tri[0:TS, 0:TS], sN.rearrange("p h t -> p (h t)"), start=True, stop=True
               ).then_inc(ss_pe, 1)
            pe.wait_ge(ss_act, 2)
            for b in range(NSEQ):
                pe.wait_ge(slot_loaded[b], loaded(N_V + b))
                for pg in range(NPG):
                    for h in range(H):
                        i, j = h // 4, h % 4
                        last = mm(ps[32 * j:32 * j + 32, 5 + i, 0:P], apad[:, pg, b, h, :],
                                  ring[:, b, 1024 * pg + P * h:1024 * pg + P * (h + 1)],
                                  start=(b == 0 and pg == 0), stop=False)
                last.then_inc(ring_used, 1)
            for h in range(H):
                i, j = h // 4, h % 4
                last = mm(ps[32 * j:32 * j + 32, 5 + i, 0:P], aN[:, h, :], tok[0:TS, 2, P * h:P * (h + 1)],
                          start=False, stop=True)
            last.then_inc(ss_pe, 1)
            pe.wait_ge(ss_dve, 4)
            for i in range(2):
                last = nc.tensor.transpose(ps[:, 7, P * i:P * (i + 1)], orow[:, i, :], ident[:])
            last.then_inc(ss_pe, 1)

            ada45 = [(N_ADA45 + KC * s + t, 4 + s, t) for s in range(2) for t in range(KC)]

            def more_ada(k):
                for _ in range(k):
                    if ada45:
                        n, six, t = ada45.pop(0)
                        ada_chunk(n, six, t)
                        if t == KC - 1 and six == 4:
                            ada_turn(4)

            more_ada(10)
            pe.wait_ge(ss_dve, 5)
            pe.wait_ge(hg_dve, 3)
            for tt in range(2):
                for h in range(H):
                    last = mm(ps[:, 2 + 2 * tt + h // 4, P * (h % 4):P * (h % 4 + 1)],
                              khat[:, h, P * tt:P * (tt + 1)], qhat[:, h, P * tt:P * (tt + 1)], start=True, stop=True)
            last.then_inc(hg_pe, 1)
            for h in range(H):
                last = mm(ps[0:TS, 6, TS * h:TS * (h + 1)], khat[:, h, TP:T], qhat[:, h, TP:T], start=True, stop=True)
            last.then_inc(hg_pe, 1)
            more_ada(6)
            for hf_ in range(2):
                heads = range(4 * hf_, 4 * hf_ + 4)
                if hf_ == 0:
                    pe.wait_ge(hg_dve, 6)
                else:
                    pe.wait_ge(hgo_act, 1)
                    pe.wait_ge(us_dve, 12)
                    pe.wait_ge(osm_dve, 1)
                for tt in range(2):
                    for h in range(4):
                        nc.tensor.transpose(ps[:, 4 + tt, P * h:P * (h + 1)],
                                            hf[:, heads[h], P * tt:P * (tt + 1)], ident[:])
                for h in range(4):
                    last = nc.tensor.transpose(ps[0:TS, 6, P * h:P * (h + 1)], hf[:, heads[h], TP:T], ident[:])
                last.then_inc(kd_pe, 1)
                more_ada(4)
                pe.wait_ge(kd_act, hf_ + 1)
                pe.wait_ge(qpad_ready, hf_ + 1)

                def chunk_update(c):
                    if 8 * hf_ + c >= 1:
                        pe.wait_ge(u_dve, 8 * hf_ + c)
                    tt, r0 = c // 4, CH * (c % 4)
                    for h in range(4):
                        k = heads[h]
                        last = mm(ps[:, 2, P * h:P * (h + 1)], kdt[r0:r0 + CH, tt, h, :],
                                  tok[r0:r0 + CH, 3 + tt, P * k:P * (k + 1)], start=True, stop=True,
                                  tile_position=(r0, 0))
                    last.then_inc(u_pe, 1)

                for c in range(8):
                    chunk_update(c)
                    if c % 2 == 0:
                        continue
                    h = c // 2
                    k = heads[h]
                    pe.wait_ge(vblk_ready, k + 1)
                    for half in range(2):
                        if k >= 1:
                            pe.wait_ge(us_dve, 3 * k - 1 + half)
                        mm(ps[:, (4, 7)[half], :], kdts[:, h, :],
                           vblk[:, 4 * half:4 * half + 4, :].rearrange("p b v -> p (b v)"), start=True, stop=True
                           ).then_inc(us_pe, 1)
                    pe.wait_ge(s0_loaded[k % 2], 16 * (k // 2 + 1))
                    for b in range(NSEQ):
                        mm(ps[32 * h:32 * h + 32, 3, 0:P], qpad[:, h, b, :], s0[k % 2][:, b, :],
                           start=(b == 0), stop=False)
                    mm(ps[32 * h:32 * h + 32, 3, 0:P], abufs[:, k, :], tok[0:TS, 5, P * k:P * (k + 1)],
                       start=False, stop=True).then_inc(os_pe, 1)
                    more_ada(2)
                pe.wait_ge(osr_dve, hf_ + 1)
                nc.tensor.transpose(ps[:, 3, P:2 * P], osr, ident[:]).then_inc(osr_pe, 1)
                pe.wait_ge(u_dve, 8 * hf_ + 7)
                for tt in range(2):
                    for h in range(4):
                        k = heads[h]
                        o = ps[:, 5 + h // 2, 256 * (h % 2) + P * tt:256 * (h % 2) + P * (tt + 1)]
                        mm(o, tok[:, 3 + tt, P * k:P * (k + 1)], abuf[:, tt, k, :], start=True, stop=False)
                        for c4 in range(4):
                            c = 4 * tt + c4
                            if c == 0:
                                continue
                            last = mm(o[:, CH * c4:CH * (c4 + 1)], shist[:, c - 1, h, :],
                                      hq[:, k, CH * c:CH * (c + 1)], start=False, stop=(c4 == 3))
                last.then_inc(hgo_pe, 1)
            more_ada(len(ada45))

            pe.wait_ge(u_dve, 16)
            pe.wait_ge(osm_dve, 2)
            for k in range(2 * H):
                pe.wait_ge(nsq_act, k + 1)
                if k >= 2:
                    pe.wait_ge(nrs_act, k - 1)
                mm(ps[:, 2 + k % 2, 0:T], ones[:], sqo[k % 2], start=True, stop=True).then_inc(nm_pe, 1)

            pe.wait_ge(nm_dve, 2 * H)
            pe.wait_ge(nrs_act, 2 * H)

            pe.wait_ge(us_dve, 3 * H)
            pe.wait_ge(hgo_act, 2)

            def sums(m):
                pe.wait_ge(wo_act, m + 1)
                mm(ps[:, 2, 0:T], ones[:], rT[:, m, :], start=(m == 0), stop=(m == KC - 1))
                mm(ps[:, 3, 0:T], ones[:], r2[m % 4], start=(m == 0), stop=(m == KC - 1)).then_inc(st_pe, 1)

            for m in range(KC):
                n = N_WO + m
                pe.wait_ge(slot_loaded[n % SLOTS], loaded(n))
                if m >= 4:
                    pe.wait_ge(wo_dve, m - 3)
                for k in range(KC):
                    last = mm(ps[:, 4 + m % 4, 0:T], ring[:, n % SLOTS, P * k:P * (k + 1)], mixT[:, k, :],
                              start=(k == 0), stop=(k == KC - 1))
                last.then_inc(ring_used, 1)
                if m >= 2:
                    sums(m - 2)
            sums(KC - 2)
            sums(KC - 1)

            pe.sem_inc(moe_used, SLOTS)
            pe.wait_ge(wo_dve, KC)
            for m in range(KC):
                pe.wait_ge(u2_dve, m + 1)
                last = mm(ps[0:NL, 4, 0:T], wr[:, m, :], u2T[:, m, :], start=(m == 0), stop=(m == KC - 1))
            last.then_inc(rt_pe, 1)

            def turn_tokens(n, src):
                i, q = n // 4 % 3, n % 4
                t0, tn = TILES[i]
                if n >= 2:
                    pe.wait_ge(tt_act, n - 1)
                for m in range(4):
                    last = nc.tensor.transpose(ps[0:tn, 6 + n % 2, P * m:P * (m + 1)],
                                               src[:, 4 * q + m, t0:t0 + tn], ident[:])
                last.then_inc(tt_pe, 1)

            pe.wait_ge(rt_act, 1)
            for i, (t0, tn) in enumerate(TILES):
                last = nc.tensor.transpose(ps[0:tn, 5, 64 * i:64 * i + NL], lgT[:, t0:t0 + tn], ident[0:NL, 0:NL])
            last.then_inc(rt_pe, 1)
            for n in range(12):
                turn_tokens(n, u2T)
            pe.wait_ge(rt_dve, 1)
            for i in range(3):
                mm(ps[:, 2, NE * i:NE * (i + 1)], stri[:], both[:, i, :], start=True, stop=(i == 0))
                for k in range(i):
                    mm(ps[:, 2, NE * i:NE * (i + 1)], ones[:], both[:, k, :], start=False, stop=(k == i - 1))
            for i in range(3):
                last = mm(ps[:, 3, 0:NE], ones[:], both[:, i, :], start=(i == 0), stop=(i == 2))
            last.then_inc(rt_pe, 1)
            for n in range(12, 24):
                turn_tokens(n, rT)
            pe.wait_ge(rt_dve, 2)
            for k in range(2):
                for i in range(3):
                    last = mm(ps[0:B, 4, 0:NB1], rsel[k][:, i, :], bsel[k][:, i, :],
                              start=(k == 0 and i == 0), stop=(k == 1 and i == 2))
            last.then_inc(rt_pe, 1)
            pe.wait_ge(tt_act, 24)

            pe.sem_inc(moe_used, MOE_CHUNKS - SLOTS)
            pe.wait_ge(rows_copied, 6)
            pe.wait_ge(ada_ready, 5)
            pe.wait_ge(plan_ready, 2)
            nblocks = pe.value_load(plan[0:1, NB1:NB1 + 1], min_val=0, max_val=NBLK)

            def turn_rows(n):
                pe.wait_ge(gathered, n * 16)
                pe.sem_inc(wait_carrier, 1)
                for m in range(KC):
                    last = nc.tensor.transpose(ps[:, m // 8, B * (m % 8):B * (m % 8 + 1)], xg[:, P * m:P * (m + 1)],
                                               ident[0:B, 0:B])
                last.then_inc(x_turned, 1)

            turn_rows(1)
            for j in range(4):
                if j >= 1:
                    pe.wait_ge(g2_act, j)
                r = slice(32 * j, 32 * j + 32)
                mm(ps[:, 2, :], rowsel[r, 0:P], ada_rows[r, :], start=True, stop=True, tile_position=(32 * j, 0))
                mm(ps[0:TS, 3, :], rowsel[r, P:P + TS], ada_rows[r, :], start=True, stop=True,
                   tile_position=(32 * j, 0)).then_inc(g2_pe, 1)
            pe.wait_ge(g2_act, 4)
            with pe.Fori(0, NBLK) as i:
                with pe.If(i < nblocks):
                    pe.wait_ge(x_copied, i + 1)
                    for c in range(8):
                        pe.wait_ge(moe_loaded[c], i * 16 + 16)
                        for t in range(4):
                            for s in range(2):
                                last = mm(ps[B * s:B * (s + 1), 2 + c // 4, 0:256], xgT[:, 4 * (c % 4) + t, :],
                                          ring[:, c, 512 * t + 256 * s:512 * t + 256 * (s + 1)],
                                          start=(c % 4 == 0 and t == 0), stop=(c % 4 == 3 and t == 3))
                        last.then_inc(moe_used, 1)
                    turn_rows(i + 2)
                    pe.wait_ge(hid_dve, i + 2)
                    for cb in range(2):
                        last = nc.tensor.transpose(ps[:, 4, P * cb:P * (cb + 1)], hid[:, P * cb:P * (cb + 1)], ident[:])
                    last.then_inc(hT_pe, 1)
                    pe.wait_ge(hT_dve, i + 1)
                    pe.wait_ge(y_evac, i * 2 + 2)
                    for q in range(4):
                        pe.wait_ge(moe_loaded[8 + q], i * 16 + 16)
                        for nn in range(2):
                            for s in range(2):
                                last = mm(ps[B * s:B * (s + 1), 5 + nn, :], hT[:, q % 2, B * (q // 2):B * (q // 2 + 1)],
                                          mslot[q][:, 1024 * s + 512 * nn:1024 * s + 512 * (nn + 1)],
                                          start=(q == 0), stop=(q == 3))
                        last.then_inc(moe_used, 1)

        @block.scalar
        def _(act):
            A = nc.scalar.activation
            count = [0]

            def link(ins):
                count[0] += 1
                ins.then_inc(act_step, 1)
                act.wait_ge(act_step, count[0])

            act.sem_inc(evac_act, 2)
            act.sem_inc(y_stored, 32)
            act.wait_ge(c_loaded, 16)
            A(ctmp[:], cin[:], ACT.Exp, scale=-1.0).then_inc(expc_ready, 1)

            def evacuate_heads(trips, n0, dst):
                with act.Fori(0, trips) as g:
                    for c in range(0, SLOTS, 2):
                        act.wait_ge(ring_used, g * SLOTS + used(n0 + c))
                        nc.scalar.copy(dst[:, bass.ds(g * H + c, 1), :].rearrange("p a t -> p (a t)"),
                                       ps[:, 4 + c % 4, 0:T]).then_inc(evac_act, 1)

            evacuate_heads(2, N_PROJ, projT[:, 0:2 * H, :])
            for g in range(2):
                act.wait_ge(ring_used, used(N_PROJ + (2 + g) * SLOTS + 3))
                for i, (t0, tn) in enumerate(TILES):
                    last = nc.scalar.copy(tok[0:tn, 3 * g + i, 0:512], ps[0:tn, 4 + i, :])
                last.then_inc(evac_act, 1)
            evacuate_heads(3, N_PROJ + 4 * SLOTS, projT[:, 2 * H:5 * H, :])

            act.wait_ge(small_loaded, 16 * 11)
            for h in range(H + 1):
                if h < H:
                    act.wait_ge(z_dve, h + 1)
                    if h >= 2:
                        act.wait_ge(sp_ready, h - 1)
                    e = ee[h % 2]
                    link(A(e, zz[h % 2], ACT.Abs))
                    link(A(e, e, ACT.Exp, scale=-1.0))
                    A(e, e, ACT.Ln, bias=1.0).then_inc(soft_act, 1)
                if h >= 1:
                    k = h - 1
                    act.wait_ge(d_dve, k + 1)
                    if k >= 2:
                        act.wait_ge(o_pe, k - 1)
                    A(aa[k % 2], zn[k % 2], ACT.Exp).then_inc(a_ready, 1)

            act.wait_ge(kv_stored, 6 * 16)
            act.wait_ge(o_evac, H)
            for b in range(NSEQ):
                act.wait_ge(kT_pe, b + 1)
                if b >= 1:
                    act.wait_ge(zr_pe, b)
                nc.scalar.copy(keyT[:, :, 0:P], ps[:, 2:4, :].rearrange("p a (h s) -> p (a h) s", s=P)
                               ).then_inc(kT_act, 1)
            act.wait_ge(ss_dve, 1)
            A(eP, zP, ACT.Abs)
            link(A(eN, zN, ACT.Abs))
            A(eP, eP, ACT.Exp, scale=-1.0)
            link(A(eN, eN, ACT.Exp, scale=-1.0))
            A(eP, eP, ACT.Ln, bias=1.0)
            A(eN, eN, ACT.Ln, bias=1.0).then_inc(ss_act, 1)
            act.wait_ge(ss_dve, 3)
            d4 = dP.rearrange("p (g b) h t -> p g b h t", g=NPG)
            for b in range(NSEQ):
                A(apad[:, :, b, :, SS * b:SS * (b + 1)], d4[:, :, b], ACT.Exp)
            A(aN, dN, ACT.Exp).then_inc(ss_act, 1)

            act.wait_ge(ss_dve, 5)
            A(lbt[:, 2, :], lbt[:, 2, :], ACT.Exp).then_inc(lb_act, 1)
            A(qhat, hq, ACT.Exp, scale=-1.0)
            A(t1, hf, ACT.Exp, scale=-1.0).then_inc(hg_act, 1)
            act.wait_ge(hg_dve, 1)
            A(t1, t1, ACT.Ln).then_inc(hg_act, 1)
            act.wait_ge(hg_dve, 2)
            A(qhat, t1, ACT.Exp)
            A(khat, t1, ACT.Exp, scale=-1.0).then_inc(hg_act, 1)
            act.wait_ge(hg_act, 3)
            A(t1, bcum, ACT.Exp)
            bp = bcum[:, :, 0:TP].rearrange("p h (c t) -> p h c t", t=CH)
            bs = bcum[:, :, TP:T].rearrange("p h (c t) -> p h c t", t=SS)
            A(dec[:, :, 0:8], bp[:, :, :, CH - 1], ACT.Exp)
            A(dec[:, :, 8:16], bs[:, :, :, SS - 1], ACT.Exp).then_inc(hg_act, 1)
            act.wait_ge(hg_dve, 4)
            A(t1, t1, ACT.Exp).then_inc(hg_act, 1)
            act.wait_ge(hg_dve, 6)
            A(t1, hg, ACT.Exp, scale=-1.0).then_inc(hg_act, 1)
            act.wait_ge(hg_dve, 7)
            for half in range(2):
                act.wait_ge(kd_pe, half + 1)
                if half == 1:
                    act.wait_ge(us_pe, 8)
                nc.scalar.copy(kdt, ps[:, 4:6, :].rearrange("p a (h s) -> p a h s", s=P))
                nc.scalar.copy(kdts, ps[0:TS, 6, :].rearrange("p (h s) -> p h s", s=P)).then_inc(kd_act, 1)
                act.wait_ge(hgo_pe, half + 1)
                nc.scalar.copy(mixT[:, 4 * half:4 * half + 4, 0:TP],
                               ps[:, 5:7, :].rearrange("p a (h t) -> p (a h) t", h=2)).then_inc(hgo_act, 1)

            act.wait_ge(hgo_act, 2)
            act.wait_ge(osm_dve, 2)
            act.wait_ge(consts_ready, 1)
            for k in range(2 * H + 1):
                if k < 2 * H:
                    if k >= 2:
                        act.wait_ge(nm_pe, k - 1)
                    A(sqo[k % 2], mixT[:, k, :], ACT.Square).then_inc(nsq_act, 1)
                if k >= 1:
                    j = k - 1
                    act.wait_ge(nm_pe, j + 1)
                    if j >= 2:
                        act.wait_ge(nm_dve, j - 1)
                    link(A(rst[j % 2], ps[:, 2 + j % 2, 0:T], ACT.Ln, bias=epsr[:, 0:1], scale=1.0 / P))
                    A(rst[j % 2], rst[j % 2], ACT.Exp, scale=-0.5).then_inc(nrs_act, 1)

            for m in range(KC):
                act.wait_ge(wo_dve, m + 1)
                if m >= 4:
                    act.wait_ge(st_pe, m - 3)
                A(r2[m % 4], rT[:, m, :], ACT.Square).then_inc(wo_act, 1)
            act.wait_ge(ln_dve, 1)
            link(A(lt1, lt1, ACT.Ln, bias=epsr[:, 1:2]))
            A(rstd, lt1, ACT.Exp, scale=-0.5).then_inc(rstd_act, 1)
            for m in range(KC):
                act.wait_ge(ln_dve, 2 + m // 4)
                A(rT[:, m, :], rT[:, m, :], ACT.Identity, bias=ln1t[:, 1, m:m + 1], scale=ln1t[:, 0, m:m + 1]
                  ).then_inc(x1_act, 1)

            act.wait_ge(rt_pe, 1)
            nc.scalar.copy(lgT[:], ps[0:NL, 4, 0:T]).then_inc(rt_act, 1)
            for n in range(12):
                t0, tn = TILES[n // 4]
                act.wait_ge(tt_pe, n + 1)
                nc.scalar.copy(urow[n // 4][0:tn, 512 * (n % 4):512 * (n % 4 + 1)], ps[0:tn, 6 + n % 2, :]
                               ).then_inc(tt_act, 1)
            act.wait_ge(rt_dve, 3)
            A(gexp, gexp, ACT.Exp)
            A(m2, m2, ACT.Exp).then_inc(rt_act, 1)
            for n in range(12, 24):
                i, q = n // 4 - 3, n % 4
                tn = TILES[i][1]
                act.wait_ge(tt_pe, n + 1)
                A(xres[0:tn, i, :].rearrange("t (p m) -> t m p", m=KC)[:, 4 * q:4 * q + 4, :],
                  ps[0:tn, 6 + n % 2, :].rearrange("t (m p) -> t m p", m=4), ACT.Copy, scale=ALPHA
                  ).then_inc(tt_act, 1)

            act.wait_ge(plan_ready, 2)
            nblocks = act.value_load(plan[0:1, NB1:NB1 + 1], min_val=0, max_val=NBLK)

            def copy_rows(n):
                act.wait_ge(x_turned, n)
                nc.scalar.copy(xgT, ps[:, 0:2, :].rearrange("p a (m s) -> p (a m) s", s=B)).then_inc(x_copied, 1)

            act.wait_ge(y_zeroed, 16)
            copy_rows(1)
            for j in range(4):
                act.wait_ge(g2_pe, j + 1)
                nc.scalar.copy(g2p[:, 512 * j:512 * (j + 1)], ps[:, 2, :])
                nc.scalar.copy(g2s[0:TS, 512 * j:512 * (j + 1)], ps[0:TS, 3, :]).then_inc(g2_act, 1)
            with act.Fori(0, NBLK) as i:
                with act.If(i < nblocks):
                    act.wait_ge(moe_used, i * MOE_CHUNKS + (MOE_CHUNKS + 4))
                    act.wait_ge(hid_dve, i + 1)
                    A(hsil, ps[:, 2, 0:256], ACT.Silu).then_inc(sil_act, 1)
                    copy_rows(i + 2)
                    act.wait_ge(moe_used, i * MOE_CHUNKS + 2 * MOE_CHUNKS)
                    act.wait_ge(y_stored, i * 32 + 32)
                    nc.scalar.copy(yout[:, 0:512], ps[:, 5, :]).then_inc(y_evac, 1)
                    act.wait_ge(y_evac, i * 2 + 4)
                    for s in range(2):
                        act.dma_start(y_rows[bass.ds(i * B, B), 1024 * s:1024 * (s + 1)],
                                      yout[B * s:B * (s + 1), :]).then_inc(y_stored, 16)

            for i, (t0, tn) in enumerate(TILES):
                act.wait_ge(fin_gather[i], 32)
                A(ya[i][0:tn, :], ya[i][0:tn, :], ACT.Copy, scale=gate2[0:tn, 0, i:i + 1]).then_inc(fin_act, 1)
                act.wait_ge(fin_dve, 2 * i + 1)
                link(A(rs1[0:tn, :], bnag[0:tn, 1:2], ACT.Ln, bias=epsr[0:tn, 1:2]))
                A(rs1[0:tn, :], rs1[0:tn, :], ACT.Exp, scale=-0.5).then_inc(fin_act, 1)
                act.wait_ge(fin_dve, 2 * i + 2)
                dst = y_p[t0:t0 + tn, :] if i < 2 else y_s[:]
                act.dma_start(dst, yb[i][0:tn, :]).then_inc(out_stored, 16)

        @block.vector
        def _(dve):
            v = nc.vector
            count = [0]

            def link(ins):
                count[0] += 1
                ins.then_inc(dve_step, 1)
                dve.wait_ge(dve_step, count[0])

            dve.sem_inc(evac_dve, 2)
            dve.sem_inc(hid_dve, 1)
            dve.sem_inc(y_evac, 2)
            link(v.memset(silu_c[:], 0.0))
            dve.wait_ge(expc_ready, 1)
            link(v.tensor_scalar(ctmp[:], ctmp[:], 1.0, None, ALU.add))
            link(v.reciprocal(ctmp[:], ctmp[:]))
            v.tensor_tensor(silu_c[:, :, 0:R], cin[:].rearrange("p (m r) -> p m r", r=R),
                            ctmp[:].rearrange("p (m r) -> p m r", r=R), ALU.mult).then_inc(silu_c_ready, 1)
            dve.wait_ge(small_loaded, 16 * 11)
            link(v.tensor_scalar(badaT[:, 1, :], badaT[:, 1, :], 1.0, None, ALU.add))
            link(v.tensor_scalar(badaT[:, 4, :], badaT[:, 4, :], 1.0, None, ALU.add))

            def copy_rows_out(six, n):
                dve.wait_ge(ring_used, used(n))
                if six >= 1:
                    dve.wait_ge(rows_turned, six)
                if six < 5:
                    v.tensor_copy(ada_rows[:], ps[:, 0, :]).then_inc(rows_copied, 1)
                else:
                    v.tensor_tensor(ada_rows[:], ps[:, 0, :], bg2[:], ALU.add).then_inc(rows_copied, 1)

            def add_bias(six):
                dve.wait_ge(rows_turned, six + 1)
                src = ps[:, 1, :].rearrange("p (c j r) -> p c j r", c=4, j=4)[:, :, :, 0:R]
                dst = adaT[:, six].rearrange("p (j c) r -> p c j r", j=4)
                bias = bc(badaT[:, six, :].rearrange("p (j c) -> p c j", j=4), 3, R)
                v.tensor_tensor(dst, src, bias, ALU.add).then_inc(ada_ready, 1)

            for six in range(2):
                copy_rows_out(six, N_ADA01 + KC * six + KC - 1)
                add_bias(six)
            dve.wait_ge(ada_ready, 2)
            dve.wait_ge(x_loaded, 16)

            def seq(ap):
                return bc(ap, len(ap.shape), SS)

            def samp(ap):
                return ap.rearrange("p m (b t) -> p m b t", t=SS)

            for m in range(KC):
                v.tensor_scalar(uT[:, m, 0:TP], uT[:, m, 0:TP], adaT[:, 1, m, 0:1], adaT[:, 0, m, 0:1],
                                ALU.mult, ALU.add)
            us = samp(uT[:, :, TP:T])
            link(v.tensor_tensor(us, us, seq(adaT[:, 1, :, 1:R]), ALU.mult))
            v.tensor_tensor(us, us, seq(adaT[:, 0, :, 1:R]), ALU.add).then_inc(u_ready, 1)

            def evacuate_heads(trips, n0, dst):
                with dve.Fori(0, trips) as g:
                    for c in range(1, SLOTS, 2):
                        dve.wait_ge(ring_used, g * SLOTS + used(n0 + c))
                        v.tensor_copy(dst[:, bass.ds(g * H + c, 1), :].rearrange("p a t -> p (a t)"),
                                      ps[:, 4 + c % 4, 0:T]).then_inc(evac_dve, 1)

            evacuate_heads(2, N_PROJ, projT[:, 0:2 * H, :])
            for g in range(2):
                dve.wait_ge(ring_used, used(N_PROJ + (2 + g) * SLOTS + 7))
                for i, ((t0, tn), bank) in enumerate(zip(TILES, (7, 2, 3))):
                    last = v.tensor_copy(tok[0:tn, 3 * g + i, 512:1024], ps[0:tn, bank, :])
                last.then_inc(evac_dve, 1)
            evacuate_heads(3, N_PROJ + 4 * SLOTS, projT[:, 2 * H:5 * H, :])

            dve.wait_ge(y_zeroed, 16)
            for i, (t0, tn) in enumerate(TILES):
                dve.wait_ge(kout_pe, i + 1)
                v.tensor_copy(kstage[0:tn, i, :].rearrange("p (a n) -> p a n", a=2),
                              ps[0:tn, 2 + 2 * i:4 + 2 * i, :]).then_inc(kout_evac, 1)

            dve.wait_ge(consts_ready, 1)
            for h in range(H + 2):
                if h == 4:
                    copy_rows_out(2, N_ADA23 + KC - 1)
                if h == 5:
                    add_bias(2)
                if h == 8:
                    copy_rows_out(3, N_ADA23 + 2 * KC - 1)
                if h == 9:
                    add_bias(3)
                if h < H:
                    dve.wait_ge(z_pe, h + 1)
                    if h >= 2:
                        dve.wait_ge(a_ready, h - 1)
                        dve.wait_ge(c_pe, h - 1)
                    x, s, n = zz[h % 2], spl[h % 2], zn[h % 2]
                    v.tensor_scalar(x, ps[:, 2 + h % 2, 0:384], SCALE, biasb[:, h:h + 1], ALU.mult, ALU.add
                                    ).then_inc(z_dve, 1)
                    dve.wait_ge(z_dve, h + 1)
                    v.tensor_tensor(n, x, negmask[:], ALU.add)
                    dve.wait_ge(soft_act, h + 1)
                    link(v.scalar_tensor_tensor(s, x, 0.0, ee[h % 2], ALU.max, ALU.add))
                    v.tensor_tensor(s, s, causal[:], ALU.mult).then_inc(sp_ready, 1)
                if 1 <= h <= H:
                    k = h - 1
                    dve.wait_ge(c_pe, k + 1)
                    dve.wait_ge(sp_ready, k + 1)
                    v.tensor_tensor(zn[k % 2], zn[k % 2], ps[:, 4 + k % 2, 0:384], ALU.subtract).then_inc(d_dve, 1)
                if h >= 2:
                    k = h - 2
                    dve.wait_ge(o_pe, k + 1)
                    v.tensor_copy(mixT[:, H + k, 0:TP], ps[:, 6 + k % 2, 0:TP]).then_inc(o_evac, 1)

            dve.wait_ge(kv_stored, 6 * 16)
            dve.wait_ge(o_evac, H)

            def keys_out(b):
                dve.wait_ge(ring_used, used(N_K + b))
                if b >= 1:
                    dve.wait_ge(zr_pe, b)
                v.tensor_copy(keyT[:, :, P:2 * P], ps[:, 4:6, :].rearrange("p a (h s) -> p (a h) s", s=P)
                              ).then_inc(kT_dve, 1)

            keys_out(0)
            zP4 = zP.rearrange("p (g b) h t -> p g b h t", g=NPG)
            for b in range(NSEQ):
                dve.wait_ge(zr_pe, b + 1)
                if b >= 1:
                    dve.wait_ge(zt_pe, b)
                v.tensor_copy(zrow, ps[:, 6, :]).then_inc(zr_dve, 1)
                if b + 1 < NSEQ:
                    keys_out(b + 1)
                dve.wait_ge(zt_pe, b + 1)
                src = ps[:, 7, :].rearrange("p (g h t) -> p g h t", g=NPG, h=H)
                v.tensor_copy(zP4[:, :, b], src[:, :, :, SS * b:SS * (b + 1)]).then_inc(zt_dve, 1)
            dve.wait_ge(zt_dve, NSEQ)
            bias = bc(bc(biasb[:], 1, NPG * NSEQ), 3, SS)
            v.memset(apad, 0.0)
            v.tensor_scalar(zP, zP, SCALE, None, ALU.mult)
            dve.wait_ge(ss_pe, 1)
            link(v.tensor_scalar(zN.rearrange("p h t -> p (h t)"), ps[0:TS, 2, 0:TS * H], SCALE, None, ALU.mult))
            v.tensor_tensor(zP, zP, bias, ALU.add)
            v.tensor_tensor(zN, zN, bc(biasb[0:TS, :], 2, TS), ALU.add).then_inc(ss_dve, 1)
            dve.wait_ge(ss_act, 1)
            v.scalar_tensor_tensor(sP, zP, 0.0, eP, ALU.max, ALU.add)
            link(v.scalar_tensor_tensor(sN, zN, 0.0, eN, ALU.max, ALU.add))
            v.tensor_tensor(zN, zN, bc(neg4[:], 1, H), ALU.add)
            v.tensor_tensor(sN, sN, bc(strict4[:], 1, H), ALU.mult).then_inc(ss_dve, 1)
            dve.wait_ge(ss_pe, 2)
            dve.wait_ge(ss_dve, 2)
            v.tensor_tensor(dP.rearrange("p g h t -> p (g h t)"), zP.rearrange("p g h t -> p (g h t)"),
                            ps[:, 3, :], ALU.subtract)
            v.tensor_tensor(dN.rearrange("p h t -> p (h t)"), zN.rearrange("p h t -> p (h t)"),
                            ps[0:TS, 4, 0:TS * H], ALU.subtract).then_inc(ss_dve, 1)
            dve.wait_ge(ss_pe, 3)
            v.tensor_copy(orow, ps[:, 5:7, 0:P]).then_inc(ss_dve, 1)
            link(v.tensor_tensor(lbt[:, 2, :], lbt[:, 1, :], lbt[:, 0, :], ALU.subtract))
            dve.wait_ge(ss_pe, 4)
            v.tensor_copy(mixT[:, H:2 * H, TP:T], ps[:, 7, 0:256].rearrange("p (h t) -> p h t", t=TS)
                          ).then_inc(ss_dve, 1)

            flat = lambda ap: ap.rearrange("p h t -> p (h t)")
            link(v.memset(reset, 1.0))
            r3 = reset.rearrange("p (h t) -> p h t", t=T)
            v.memset(r3[:, :, 0:TP].rearrange("p h (c t) -> p h c t", t=CH)[:, :, :, 0:1], 0.0)
            v.memset(r3[:, :, TP:T].rearrange("p h (c t) -> p h c t", t=SS)[:, :, :, 0:1], 0.0)
            v.memset(abuf, 0.0)
            v.memset(abufs, 0.0)
            dve.wait_ge(lb_act, 1)
            link(v.tensor_scalar(lbt[:, 2, :], lbt[:, 2, :], 1.0, None, ALU.add))
            link(v.reciprocal(lbt[:, 2, :], lbt[:, 2, :]))
            dve.wait_ge(hg_act, 1)
            v.tensor_scalar(qhat, qhat, 1.0, None, ALU.add)
            v.tensor_scalar(t1, t1, 1.0, None, ALU.add)
            link(v.tensor_scalar(lbt[:, 3, :], lbt[:, 2, :], -1.0, 1.0, ALU.mult, ALU.add))
            v.reciprocal(qhat, qhat)
            link(v.reciprocal(t1, t1))
            v.tensor_tensor(hq, hq, qhat, ALU.mult)
            for h in range(H):
                last = v.tensor_scalar(t1[:, h, :], t1[:, h, :], lbt[:, 3, h:h + 1], lbt[:, 2, h:h + 1],
                                       ALU.mult, ALU.add)
            link(last)
            v.tensor_scalar(hf, t1, -1.0, 1.0, ALU.mult, ALU.add).then_inc(hg_dve, 1)
            dve.wait_ge(hg_act, 2)
            for half in range(2):
                last = v.tensor_tensor_scan(flat(bcum[:, 4 * half:4 * half + 4, :]), reset,
                                            flat(t1[:, 4 * half:4 * half + 4, :]), 0.0, ALU.mult, ALU.add)
            link(last)
            bp = bcum[:, :, 0:TP].rearrange("p h (c t) -> p h c t", t=CH)
            bs = bcum[:, :, TP:T].rearrange("p h (c t) -> p h c t", t=SS)
            tp = t1[:, :, 0:TP].rearrange("p h (c t) -> p h c t", t=CH)
            ts = t1[:, :, TP:T].rearrange("p h (c t) -> p h c t", t=SS)
            for h in range(H):
                v.tensor_tensor(tp[:, h], bp[:, h], bc(bp[:, h, :, CH // 2 - 1], 2, CH), ALU.subtract)
                last = v.tensor_tensor(ts[:, h], bs[:, h], bc(bs[:, h, :, SS // 2 - 1], 2, SS), ALU.subtract)
            link(last)
            v.tensor_scalar(t1, t1, 80.0, -80.0, ALU.min, ALU.max).then_inc(hg_dve, 1)
            dve.wait_ge(hg_act, 3)
            dve.wait_ge(hg_dve, 2)
            v.tensor_tensor(qhat, qhat, hq, ALU.mult)
            v.tensor_tensor(khat, khat, hf, ALU.mult).then_inc(hg_dve, 1)
            dve.wait_ge(hg_act, 4)
            dve.wait_ge(hg_dve, 3)
            link(v.tensor_tensor(hq, hq, t1, ALU.mult))
            for h in range(H):
                v.tensor_tensor(tp[:, h], bc(bp[:, h, :, CH - 1], 2, CH), bp[:, h], ALU.subtract)
                last = v.tensor_tensor(ts[:, h], bc(bs[:, h, :, SS - 1], 2, SS), bs[:, h], ALU.subtract)
            last.then_inc(hg_dve, 1)
            dve.wait_ge(hg_pe, 2)
            for tt in range(2):
                for i in range(2):
                    v.copy_predicated(abuf[:, tt, 4 * i:4 * i + 4, :], bc(chunkmask[:].bitcast(U32), 1, 4),
                                      ps[:, 2 + 2 * tt + i, :].rearrange("p (h t) -> p h t", t=P))
            v.copy_predicated(abufs, bc(incl4[:].bitcast(U32), 1, H),
                              ps[0:TS, 6, 0:256].rearrange("p (h t) -> p h t", t=TS)).then_inc(hg_dve, 1)
            copy_rows_out(4, N_ADA45 + KC - 1)
            dve.wait_ge(hg_act, 5)
            v.tensor_tensor(hf, hf, t1, ALU.mult).then_inc(hg_dve, 1)
            dve.wait_ge(hg_act, 6)
            link(v.tensor_scalar(t1, t1, 1.0, None, ALU.add))
            link(v.reciprocal(t1, t1))
            v.tensor_tensor(hg, hg, t1, ALU.mult).then_inc(hg_dve, 1)
            link(v.memset(qpad, 0.0))
            for half in range(2):
                heads = slice(4 * half, 4 * half + 4)
                if half == 1:
                    dve.wait_ge(os_pe, 4)
                for b in range(NSEQ):
                    last = v.tensor_copy(qpad[:, :, b, SS * b:SS * (b + 1)],
                                         hq[:, heads, TP + SS * b:TP + SS * (b + 1)])
                last.then_inc(qpad_ready, 1)

                def state_after(c):
                    dve.wait_ge(u_pe, 8 * half + c + 1)
                    upd = ps[:, 2, :].rearrange("p (h v) -> p h v", v=P)
                    if c == 0:
                        if half == 1:
                            dve.wait_ge(hgo_pe, 1)
                            dve.wait_ge(sprompt_stored, 16)
                        v.tensor_copy(shist[:, 0], upd).then_inc(u_dve, 1)
                    else:
                        dve.wait_ge(u_dve, 8 * half + c)
                        link(v.tensor_tensor(shist[:, c], shist[:, c - 1], bc(dec[:, heads, c], 2, P), ALU.mult))
                        v.tensor_tensor(shist[:, c], shist[:, c], upd, ALU.add).then_inc(u_dve, 1)

                for c in range(8):
                    state_after(c)
                    if c % 2 == 0:
                        continue
                    k = 4 * half + c // 2
                    dve.wait_ge(s0_loaded[k % 2], 16 * (k // 2 + 1))
                    if k >= 1:
                        dve.wait_ge(ssample_stored, 16 * k)
                    v.tensor_tensor(snew, s0[k % 2], bc(dec[:, k, 8:16], 2, P), ALU.mult).then_inc(us_dve, 1)
                    for i, bank in enumerate((4, 7)):
                        dve.wait_ge(us_pe, 2 * k + i + 1)
                        dve.wait_ge(us_dve, 3 * k + 1)
                        part = snew[:, 4 * i:4 * i + 4, :]
                        v.tensor_tensor(part, part, ps[:, bank, :].rearrange("p (b v) -> p b v", v=P), ALU.add
                                        ).then_inc(us_dve, 1)
                dve.wait_ge(os_pe, 4 * (half + 1))
                if half == 1:
                    dve.wait_ge(osr_pe, 1)
                v.tensor_copy(osr, ps[:, 3, 0:P]).then_inc(osr_dve, 1)
                dve.wait_ge(osr_pe, half + 1)
                v.tensor_copy(mixT[:, heads, TP:T], ps[:, 3, P:2 * P].rearrange("p (h t) -> p h t", t=TS)
                              ).then_inc(osm_dve, 1)
                if half == 0:
                    add_bias(4)
            copy_rows_out(5, N_ADA45 + 2 * KC - 1)

            for k in range(2 * H):
                dve.wait_ge(nrs_act, k + 1)
                w = normw[:, k // H:k // H + 1]
                ins = v.scalar_tensor_tensor(mixT[:, k, :], mixT[:, k, :], w, rst[k % 2], ALU.mult, ALU.mult)
                if k < H:
                    link(ins)
                    ins = v.tensor_tensor(mixT[:, k, :], mixT[:, k, :], hg[:, k, :], ALU.mult)
                ins.then_inc(nm_dve, 1)

            dve.wait_ge(xa_ready, 1)
            for m in range(KC):
                dve.wait_ge(ring_used, used(N_WO + m))
                o = ps[:, 4 + m % 4, :]
                rs = rT[:, m, TP:T].rearrange("p (b t) -> p b t", t=SS)
                link(v.tensor_tensor(rs, o[:, TP:T].rearrange("p (b t) -> p b t", t=SS), seq(adaT[:, 2, m, 1:R]),
                                     ALU.mult))
                v.scalar_tensor_tensor(rT[:, m, 0:TP], o[:, 0:TP], adaT[:, 2, m, 0:1], xa[:, m, 0:TP],
                                       ALU.mult, ALU.add)
                v.tensor_tensor(rT[:, m, TP:T], rT[:, m, TP:T], xa[:, m, TP:T], ALU.add).then_inc(wo_dve, 1)
            dve.wait_ge(st_pe, KC)
            dve.wait_ge(wo_act, KC)
            v.tensor_scalar(lt1, ps[:, 3, 0:T], 1.0 / D, None, ALU.mult)
            link(v.tensor_scalar(mu, ps[:, 2, 0:T], 1.0 / D, None, ALU.mult))
            link(v.tensor_tensor(rstd, mu, mu, ALU.mult))
            link(v.tensor_tensor(lt1, lt1, rstd, ALU.subtract))
            v.tensor_scalar(lt1, lt1, 0.0, None, ALU.max).then_inc(ln_dve, 1)
            link(v.tensor_tensor(rT, rT, bc(mu, 1, KC), ALU.subtract))
            dve.wait_ge(rstd_act, 1)
            for q in range(4):
                part = rT[:, 4 * q:4 * q + 4, :]
                v.tensor_tensor(part, part, bc(rstd, 1, 4), ALU.mult).then_inc(ln_dve, 1)
            for m in range(KC):
                dve.wait_ge(x1_act, m + 1)
                us = u2T[:, m, TP:T].rearrange("p (b t) -> p b t", t=SS)
                xs = rT[:, m, TP:T].rearrange("p (b t) -> p b t", t=SS)
                link(v.tensor_tensor(us, xs, seq(adaT[:, 4, m, 1:R]), ALU.mult))
                v.tensor_scalar(u2T[:, m, 0:TP], rT[:, m, 0:TP], adaT[:, 4, m, 0:1], adaT[:, 3, m, 0:1],
                                ALU.mult, ALU.add)
                v.tensor_tensor(us, us, seq(adaT[:, 3, m, 1:R]), ALU.add).then_inc(u2_dve, 1)

            v.memset(lg, 0.0)
            v.memset(vm, 0.0)
            link(v.memset(onesNE, 1.0))
            v.memset(vm[:, 0:2], 1.0)
            link(v.memset(vm[0:32, 2:3], 1.0))
            dve.wait_ge(rt_pe, 2)
            v.tensor_tensor(lg[:, 0:2, :], ps[:, 5, 0:128].rearrange("p (i n) -> p i n", n=64)[:, :, 0:NL],
                            bc(br[:], 1, 2), ALU.add)
            link(v.tensor_tensor(lg[0:32, 2, :], ps[0:32, 5, 128:128 + NL], br[0:32, :], ALU.add))
            gl = lg[:, :, 0:NG]
            el = lg[:, :, NG:NL].rearrange("p i (g e) -> p i g e", e=NEG)

            def first_max(out, x, m, n):
                link(v.tensor_tensor(out, x, bc(m, 2, n), ALU.is_equal))
                link(v.tensor_tensor(out, out, bc(rev4[:, 0:n], 1, 3), ALU.mult))
                link(v.tensor_reduce(tmp3, out, AX, ALU.max))
                link(v.tensor_tensor(out, out, bc(tmp3, 2, n), ALU.is_equal))

            link(v.tensor_reduce(gmax, gl, AX, ALU.max))
            first_max(gone, gl, gmax, NG)
            v.tensor_tensor(gexp, gl, bc(gmax, 2, NG), ALU.subtract)
            link(v.tensor_tensor(pick, el, bc(gone, 3, NEG), ALU.mult))
            link(v.tensor_reduce(esel, pick.rearrange("p i g e -> p i e g"), AX, ALU.add))
            link(v.tensor_reduce(m1, esel, AX, ALU.max))
            first_max(e1, esel, m1, NEG)
            link(v.tensor_scalar(cand, e1, -3.0e38, None, ALU.mult))
            link(v.tensor_tensor(cand, cand, esel, ALU.add))
            link(v.tensor_reduce(m2, cand, AX, ALU.max))
            first_max(e2, cand, m2, NEG)
            link(v.tensor_tensor(m2, m2, m1, ALU.subtract))
            link(v.tensor_tensor(gone, gone, bc(vm, 2, NG), ALU.mult))
            for k, e in enumerate((e1, e2)):
                for i in range(3):
                    last = v.tensor_tensor(oneh[k][:, i], bc(gone[:, i], 2, NEG), bc(e[:, i], 1, NG), ALU.mult)
            link(last)
            oh = [oneh[k].rearrange("p i g e -> p i (g e)") for k in range(2)]
            v.tensor_tensor(both, oh[0], oh[1], ALU.add).then_inc(rt_dve, 1)

            dve.wait_ge(rt_pe, 3)
            link(v.tensor_copy(cnt, ps[:, 3, 0:NE]))
            link(v.tensor_scalar(nb, cnt, 0.0, None, ALU.is_gt))
            for j in range(1, (T + B - 1) // B):
                link(v.scalar_tensor_tensor(nb, cnt, float(B * j), nb, ALU.is_gt, ALU.add))
            link(v.tensor_tensor_scan(cum, onesNE, nb, 0.0, ALU.mult, ALU.add))
            v.tensor_tensor(base, cum, nb, ALU.subtract)
            link(v.tensor_tensor(ecmp, bc(cum[0:1, :], 1, NB1), bc(iotab[0:1, 0:NB1], 2, NE), ALU.is_le))
            link(v.tensor_reduce(eid, ecmp, AX, ALU.add))
            link(v.tensor_scalar(eid, eid, NE - 1.0, None, ALU.min))
            v.tensor_copy(plan[0:1, 0:NB1], eid)
            v.tensor_copy(plan[0:1, NB1:NB1 + 1], cum[0:1, NE - 1:NE]).then_inc(plan_ready, 1)
            link(v.tensor_copy(rank, ps[:, 2, 0:3 * NE].rearrange("p (i e) -> p i e", e=NE)))
            v.memset(gslot[:], 0.0)
            for k in range(2):
                link(v.tensor_tensor(tmp32, oh[k], rank, ALU.mult))
                link(v.tensor_reduce(rk, tmp32, AX, ALU.add))
                link(v.tensor_scalar(blkr, rk, float(B), None, ALU.is_ge))
                for j in range(2, (T + B - 1) // B):
                    link(v.scalar_tensor_tensor(blkr, rk, float(B * j), blkr, ALU.is_ge, ALU.add))
                link(v.scalar_tensor_tensor(sl, blkr, -float(B), rk, ALU.mult, ALU.add))
                link(v.tensor_tensor(tmp32, oh[k], bc(base, 1, 3), ALU.mult))
                link(v.tensor_reduce(blk, tmp32, AX, ALU.add))
                link(v.tensor_tensor(blk, blk, blkr, ALU.add))
                link(v.scalar_tensor_tensor(gslot[:, k, :], blk, float(B), sl, ALU.mult, ALU.add))
                if k == 0:
                    link(v.tensor_tensor(tokid[:], tokid[:], vm, ALU.mult))
                for i in range(3):
                    v.tensor_scalar(rsel[k][:, i, :], iotab[:], sl[:, i:i + 1], None, ALU.is_equal)
                    last = v.tensor_scalar(bsel[k][:, i, :], iotab[:, 0:NB1], blk[:, i:i + 1], tokid[:, i:i + 1],
                                           ALU.is_equal, ALU.mult)
                if k == 0:
                    link(last)
            last.then_inc(rt_dve, 1)
            v.tensor_copy(rowidx[:], gslot[:]).then_inc(rt_dve, 1)
            dve.wait_ge(rt_pe, 4)
            v.tensor_copy(idxs[:], ps[0:B, 4, 0:NB1]).then_inc(plan_ready, 1)
            dve.wait_ge(rt_act, 2)
            link(v.tensor_reduce(gw, gexp, AX, ALU.add))
            link(v.tensor_scalar(tmp3, m2, 1.0, None, ALU.add))
            link(v.tensor_tensor(gw, gw, tmp3, ALU.mult))
            link(v.reciprocal(gate2[:, 0, :], gw))
            link(v.tensor_tensor(gate2[:, 1, :], gate2[:, 0, :], m2, ALU.mult))

            dve.wait_ge(plan_ready, 2)
            nblocks = dve.value_load(plan[0:1, NB1:NB1 + 1], min_val=0, max_val=NBLK)
            with dve.Fori(0, NBLK) as i:
                with dve.If(i < nblocks):
                    dve.wait_ge(sil_act, i + 1)
                    dve.wait_ge(moe_used, i * MOE_CHUNKS + (MOE_CHUNKS + 8))
                    dve.wait_ge(hT_pe, i + 1)
                    v.tensor_tensor(hid, hsil, ps[:, 3, 0:256], ALU.mult).then_inc(hid_dve, 1)
                    dve.wait_ge(hT_pe, i + 2)
                    v.tensor_copy(hT, ps[:, 4, 0:256].rearrange("p (c s) -> p c s", s=P)).then_inc(hT_dve, 1)
                    dve.wait_ge(moe_used, i * MOE_CHUNKS + 2 * MOE_CHUNKS)
                    dve.wait_ge(y_stored, i * 32 + 32)
                    v.tensor_copy(yout[:, 512:1024], ps[:, 6, :]).then_inc(y_evac, 1)

            dve.wait_ge(late_loaded, 16)
            dve.wait_ge(g2_act, 4)
            for i, (t0, tn) in enumerate(TILES):
                w = yb[i][0:tn, :]
                dve.wait_ge(fin_act, 2 * i + 1)
                link(v.scalar_tensor_tensor(w, w, gate2[0:tn, 1, i:i + 1], ya[i][0:tn, :], ALU.mult, ALU.add))
                link(v.tensor_tensor(w, w, (g2p if i < 2 else g2s)[0:tn, :], ALU.mult))
                link(v.tensor_tensor(w, w, xres[0:tn, i, :], ALU.add))
                for q in range(4):
                    last = v.bn_stats(bnst[0:tn, q, :], w[:, 512 * q:512 * (q + 1)])
                link(last)
                v.bn_aggr(bnag[0:tn, :], bnst[0:tn, :, :].rearrange("p q s -> p (q s)")).then_inc(fin_dve, 1)
                dve.wait_ge(fin_act, 2 * i + 2)
                link(v.tensor_scalar(w, w, bnag[0:tn, 0:1], rs1[0:tn, :], ALU.subtract, ALU.mult))
                link(v.tensor_tensor(w, w, ln2b[0:tn, 0, :], ALU.mult))
                v.tensor_tensor(w, w, ln2b[0:tn, 1, :], ALU.add).then_inc(fin_dve, 1)


def kernel(**inputs):
    import numpy as np
    import concourse.bacc as bacc
    from concourse.bass_utils import run_bass_kernel_spmd

    a = {k: np.asarray(x) for k, x in inputs.items()}

    def feature_major(x):
        return np.ascontiguousarray(x.reshape(-1, P, KC).transpose(1, 2, 0))

    w_ada = a["w_ada"][0].reshape(P, KC, 6, D)
    perm = w_ada.reshape(P, KC, 6, P, KC).transpose(2, 1, 0, 4, 3).reshape(6, KC, P, D)
    ada = np.concatenate([perm[:5], w_ada[:, :, 5].transpose(1, 0, 2)[None]])
    b_ada = a["b_ada"][0].reshape(6, D)
    w_in = a["w_in"][0].reshape(P, KC, 7, 1024)
    groups = []
    for n, g in enumerate((4, 5, 6, 2, 0, 1, 3)):
        w = w_in[:, :, g]
        if n in (2, 3):
            w = w.reshape(P, 4, 4, 2, 512).transpose(3, 1, 0, 2, 4)
        else:
            w = w.reshape(P, KC, H, P).transpose(2, 0, 1, 3)
        groups.append(w.reshape(SLOTS, P, D))
    w_o = a["w_o"][0].reshape(KC, P, P, KC).transpose(3, 1, 0, 2).reshape(2, SLOTS, P, D)
    arrays = {
        "xT": feature_major(np.concatenate([a["x_prompt"].reshape(-1, D), a["x_sample"].reshape(-1, D)])),
        "cT": feature_major(np.concatenate([a["c_prompt"], a["c_sample"]])),
        "w_ada": ada,
        "b_adaT": b_ada[:5].reshape(5, P, KC).transpose(1, 0, 2),
        "b_g2": b_ada[5].reshape(4, 512),
        "w_in": np.stack(groups),
        "w_o": w_o,
        "w_r": np.concatenate([a["w_gr"][0], a["w_er"][0].reshape(D, NE)], axis=1).reshape(P, KC, NL),
        "b_r": np.concatenate([a["b_gr"][0], a["b_er"][0].reshape(NE)]),
        "lb_logits": a["hg_lb_logits"].reshape(2, H, P).transpose(2, 0, 1),
        "norms": np.stack([a["hg_norm"][0], a["sb_norm"][0]], axis=1),
        "sb_bias": a["sb_bias"][0],
        "ln1": np.stack([a["ln1_g"][0], a["ln1_b"][0]]).reshape(2, P, KC).transpose(1, 0, 2),
        "ln2": np.stack([a["ln2_g"][0], a["ln2_b"][0]]),
        "cache_k": a["cache_k"][0].reshape(NPHYS, PAGE, 1024),
        "cache_v": a["cache_v"][0].reshape(NPHYS, PAGE, 1024),
        "page_table": a["page_table"].reshape(1, NSEQ * NPG),
        "state": a["state_hgrn"][0],
        "w_gate": a["w_gate"][0], "w_up": a["w_up"][0], "w_down": a["w_down"][0],
    }
    arrays = {k: np.ascontiguousarray(x) for k, x in arrays.items()}
    outs = {"y_p": (TP, D), "y_s": (TS, D), "k_p": (TP, 1024), "v_p": (TP, 1024), "s_p": (H, P, P),
            "k_s": (TS, 1024), "v_s": (TS, 1024), "s_s": (NSEQ, H, P, P)}
    nc = bacc.Bacc("TRN2", target_bir_lowering=False, num_devices=1)
    aps = {k: nc.dram_tensor(k, x.shape, mybir.dt.from_np(x.dtype), kind="ExternalInput").ap()
           for k, x in arrays.items()}
    aps |= {k: nc.dram_tensor(k, s, F32, kind="ExternalOutput").ap() for k, s in outs.items()}
    aps["u2_rows"] = nc.dram_tensor("u2_rows", (T, D), F32, kind="Internal").ap()
    aps["y_rows"] = nc.dram_tensor("y_rows", (NBLK * B, D), F32, kind="Internal").ap()
    layer(nc, **aps)
    r = run_bass_kernel_spmd(nc, [arrays], core_ids=[0]).results[0]
    return (r["y_p"].reshape(1, TP, D), r["y_s"].reshape(NSEQ, SS, D),
            r["k_p"].reshape(1, 1, TP, H, P), r["v_p"].reshape(1, 1, TP, H, P), r["s_p"].reshape(1, 1, H, P, P),
            r["k_s"].reshape(1, NSEQ, SS, H, P), r["v_s"].reshape(1, NSEQ, SS, H, P),
            r["s_s"].reshape(1, NSEQ, H, P, P))
```

```python
from contextlib import ExitStack

import concourse.bass as bass
from concourse import mybir

F32 = mybir.dt.float32
I32 = mybir.dt.int32
U32 = mybir.dt.uint32
ACT = mybir.ActivationFunctionType
ALU = mybir.AluOpType
AX = mybir.AxisListType.X

P = 128
D = 2048
KC = D // P
TP, NSEQ, SS = 256, 8, 4
TS = NSEQ * SS
T = TP + TS
H = 8
R = 1 + NSEQ
PAST, PAGE = 256, 128
NPG = PAST // PAGE
NPHYS = 20
SCALE = 128 ** -0.5
ALPHA = 2.0 ** 0.25
LN_EPS, RMS_EPS = 1e-5, 1e-6
NG, NEG, NE, FF = 4, 8, 32, 512
NL = NG + NE
B = 64
NBLK = NE + (2 * T) // B - 1
CH = 32
SLOTS = 8
MOE_CHUNKS = 12
TILES = [(0, 128), (128, 128), (256, 32)]
NEG_BIG = -1.0e30


def layer(nc, xT, cT, w_ada, b_adaT, b_g2, w_in, w_o, w_r, b_r, lb_logits, norms, sb_bias,
          ln1, ln2, cache_k, cache_v, page_table, state, w_gate, w_up, w_down,
          y_p, y_s, k_p, v_p, s_p, k_s, v_s, s_s, u2_rows, y_rows):
    with ExitStack() as ctx:
        def sb(name, shape, dt=F32):
            return ctx.enter_context(nc.sbuf_tensor(name, shape, dt))

        def sem(name):
            return ctx.enter_context(nc.semaphore(name))

        ps = ctx.enter_context(nc.psum_tensor("ps", [P, 8, 512], F32))
        ring = sb("ring", [P, SLOTS, D])

        ident = sb("ident", [P, P])
        tri = sb("tri", [P, P])
        ones = sb("ones", [P, P])
        causal = sb("causal", [P, 384])
        negmask = sb("negmask", [P, 384])
        chunkmask = sb("chunkmask", [P, P])
        strict4 = sb("strict4", [TS, TS])
        neg4 = sb("neg4", [TS, TS])
        incl4 = sb("incl4", [TS, TS])
        seqmask = sb("seqmask", [TS, NSEQ])
        rowsel = sb("rowsel", [P, P + TS])
        silu_c = sb("silu_c", [P, KC, 32])
        ctmp = sb("ctmp", [P, KC * R])
        cin = sb("cin", [P, KC * R])
        adaT = sb("adaT", [P, 5, KC, R])
        badaT = sb("badaT", [P, 5, KC])
        ada_rows = sb("ada_rows", [P, 512])
        bg2 = sb("bg2", [P, 512])
        lbt = sb("lbt", [P, 4, H])
        normw = sb("normw", [P, 2])
        biasb = sb("biasb", [P, H])
        ln1t = sb("ln1t", [P, 2, KC])
        epsr = sb("epsr", [P, 2])
        wr = sb("wr", [P, KC, NL])
        br = sb("br", [P, NL])
        pages = sb("pages", [1, NSEQ * NPG], I32)

        ARENA = 31488
        arena = sb("arena", [P, ARENA])

        def area(at, *shape, parts=P):
            n = 1
            for s in shape:
                n *= s
            assert at + n <= ARENA, (at, shape)
            v = arena[0:parts, at:at + n]
            if len(shape) == 1:
                return v
            names = "abcde"[:len(shape)]
            return v.rearrange(f"p ({' '.join(names)}) -> p {' '.join(names)}",
                               **{k: s for k, s in zip(names, shape)})

        uT = area(0, KC, T)
        mixT = uT
        SQ = 4608
        projT = area(SQ, 5 * H, T)
        sqT, skT = projT[:, 0:H, :], projT[:, H:2 * H, :]
        hf, hq, hg = (projT[:, (2 + i) * H:(3 + i) * H, :] for i in range(3))
        hf_hq = projT[:, 2 * H:4 * H, :]
        hout = hf
        TOK = SQ + 5 * H * T
        tok = area(TOK, 6, 1024)
        TMP = TOK + 6 * 1024
        kstage = area(TMP + 5120, 3, 1024)
        soft = [[area(at + 384 * i, 384) for i in range(5)] for at in (SQ + 3 * H * T, 0)]
        zz, ee, spl, zn, aa = ([s[i] for s in soft] for i in range(5))
        keyT = area(TMP, H, PAST)
        zrow = area(TMP + 2048, 512)
        apad = area(TMP, NPG, NSEQ, H, TS)
        zP = area(TMP + 4096, NPG * NSEQ, H, SS)
        eP = area(TMP + 4608, NPG * NSEQ, H, SS)
        sP = area(TMP + 5120, NPG * NSEQ, H, SS)
        dP = area(TMP + 5632, NPG * NSEQ, H, SS)
        zN = area(TMP + 6144, H, TS, parts=TS)
        eN = area(TMP + 6400, H, TS, parts=TS)
        sN = area(TMP + 6656, H, TS, parts=TS)
        dN = area(TMP + 6912, H, TS, parts=TS)
        aN = area(TMP + 7168, H, TS, parts=TS)
        orow = area(TMP + 7424, 2, P)
        qhat = area(SQ, H, T)
        khat = area(SQ + H * T, H, T)
        bcum = area(TMP, H, T)
        t1 = area(TMP + 2304, H, T)
        shist = area(TMP, 8, 4, P)
        kdts = area(TMP + 4096, 4, P, parts=TS)
        abuf = area(TMP + 4608, 2, H, P)
        abufs = area(TMP + 6656, H, TS, parts=TS)
        dec = area(TMP + 6912, H, 16)
        reset = area(TMP + 7040, 4 * T)
        kdt = area(TMP + 7040, 2, 4, P)
        osr = area(TMP + 8064, P)
        vblk = area(TMP + 8192, NSEQ, P, parts=TS)
        s0 = [area(TOK + 1024 * i, NSEQ, P) for i in range(2)]
        qpad = area(TOK + 2048, 4, NSEQ, TS)
        sqo = [area(TMP + 4608 + T * i, T) for i in range(2)]
        rst = [area(TMP + 4608 + T * (2 + i), T) for i in range(2)]
        xa = area(4608, KC, T)
        rT = area(9216, KC, T)
        r2 = [area(13824 + T * i, T) for i in range(4)]
        mu = area(14976, T)
        rstd = area(15264, T)
        lt1 = area(15552, T)
        u2T = area(4608, KC, T)
        urow = [area(16384 + 2048 * i, D) for i in range(3)]
        RT = 28700
        zeros = area(24576, D)
        lgT = area(15840, T, parts=NL)
        mslot = [area(0 + D * i, D) for i in range(4)]
        xres = area(22528, 3, D)
        xg = area(8192, D, parts=B)
        xgT = area(10240, KC, B)
        hid = area(11264, 256)
        hsil = area(11520, 256)
        hT = area(11776, 2, P)
        yout = area(12032, 1024)
        g2p = area(13056, D)
        g2s = area(15104, D)
        ln2b = area(17152, 2, D)
        ya = [area(0, D), area(2048, D), area(4096, D)]
        yb = [area(6144, D), area(8192, D), area(10240, D)]

        slot_loaded = [sem(f"slot_loaded{i}") for i in range(SLOTS)]
        moe_loaded = [sem(f"moe_loaded{i}") for i in range(MOE_CHUNKS)]
        ring_used = sem("ring_used")
        moe_used = sem("moe_used")
        (x_loaded, c_loaded, small_loaded, late_loaded, pages_loaded, xa_loaded, k_stored, v_stored, sprompt_stored,
         ssample_stored, u2_stored, gathered, y_stored, out_stored) = (sem(n) for n in (
             "x_loaded", "c_loaded", "small_loaded", "late_loaded", "pages_loaded", "xa_loaded", "k_stored", "v_stored",
             "sprompt_stored", "ssample_stored", "u2_stored", "gathered", "y_stored", "out_stored"))
        s0_loaded = [sem(f"s0_loaded{i}") for i in range(2)]
        fin_gather = [sem(f"fin_gather{i}") for i in range(3)]
        pool_step, dve_step, act_step = sem("pool_step"), sem("dve_step"), sem("act_step")
        consts_ready, expc_ready, silu_c_ready = sem("consts_ready"), sem("expc_ready"), sem("silu_c_ready")
        rows_copied, rows_turned, ada_ready = sem("rows_copied"), sem("rows_turned"), sem("ada_ready")
        u_ready, evac_act, evac_dve = sem("u_ready"), sem("evac_act"), sem("evac_dve")
        kout_pe, kout_evac = sem("kout_pe"), sem("kout_evac")
        (z_pe, z_dve, soft_act, sp_ready, c_pe, d_dve, a_ready, o_pe, o_evac) = (sem(n) for n in (
            "z_pe", "z_dve", "soft_act", "sp_ready", "c_pe", "d_dve", "a_ready", "o_pe", "o_evac"))
        kT_pe, kT_act, kT_dve, zr_pe, zr_dve, zt_pe, zt_dve = (
            sem(n) for n in ("kT_pe", "kT_act", "kT_dve", "zr_pe", "zr_dve", "zt_pe", "zt_dve"))
        ss_pe, ss_dve, ss_act = sem("ss_pe"), sem("ss_dve"), sem("ss_act")
        hg_pe, hg_dve, hg_act, vblk_ready, lb_dve, lb_act = (
            sem(n) for n in ("hg_pe", "hg_dve", "hg_act", "vblk_ready", "lb_dve", "lb_act"))
        kd_pe, kd_act, u_pe, u_dve = sem("kd_pe"), sem("kd_act"), sem("u_pe"), sem("u_dve")
        us_pe, us_dve, os_pe = sem("us_pe"), sem("us_dve"), sem("os_pe")
        qpad_ready, osr_dve, osr_pe, osm_dve = (sem(n) for n in ("qpad_ready", "osr_dve", "osr_pe", "osm_dve"))
        hgo_pe, hgo_act = sem("hgo_pe"), sem("hgo_act")
        nsq_act, nm_pe, nrs_act, nm_dve = sem("nsq_act"), sem("nm_pe"), sem("nrs_act"), sem("nm_dve")
        xa_ready, wo_dve, wo_act, st_pe = sem("xa_ready"), sem("wo_dve"), sem("wo_act"), sem("st_pe")
        ln_dve, rstd_act, x1_act, u2_dve = sem("ln_dve"), sem("rstd_act"), sem("x1_act"), sem("u2_dve")
        rt_pe, rt_dve, rt_act, tt_pe, tt_act = (sem(n) for n in ("rt_pe", "rt_dve", "rt_act", "tt_pe", "tt_act"))
        plan_ready, idx_ready = sem("plan_ready"), sem("idx_ready")
        x_turned, x_copied = sem("x_turned"), sem("x_copied")
        sil_act, hid_dve, hT_pe, hT_dve, y_evac = (sem(n) for n in ("sil_act", "hid_dve", "hT_pe", "hT_dve", "y_evac"))
        g2_pe, g2_act = sem("g2_pe"), sem("g2_act")
        zeros_ready, y_zeroed = sem("zeros_ready"), sem("y_zeroed")
        wait_carrier = sem("wait_carrier")
        fin_dve, fin_act = sem("fin_dve"), sem("fin_act")

        def rta(at, *shape, parts=P):
            return area(RT + at, *shape, parts=parts)
        lg = rta(0, 3, NL)
        vm = rta(108, 3)
        gmax = rta(111, 3)
        gone = rta(114, 3, NG)
        gexp = rta(126, 3, NG)
        gw = rta(138, 3)
        pick = rta(141, 3, NG, NEG)
        esel = rta(237, 3, NEG)
        e1 = rta(261, 3, NEG)
        e2 = rta(285, 3, NEG)
        m1 = rta(309, 3)
        m2 = rta(312, 3)
        cand = rta(315, 3, NEG)
        oneh = [rta(339 + 96 * k, 3, NG, NEG) for k in range(2)]
        both = rta(531, 3, NE)
        rank = rta(627, 3, NE)
        cnt = rta(723, NE)
        nb = rta(755, NE)
        cum = rta(787, NE)
        base = rta(819, NE)
        tmp32 = rta(851, 3, NE)
        rk = rta(947, 3)
        blkr = rta(950, 3)
        sl = rta(953, 3)
        blk = rta(956, 3)
        tmp3 = rta(959, 3)
        onesNE = rta(962, NE)
        rsel = [rta(994 + 192 * k, 3, B) for k in range(2)]
        NB1 = NBLK + 1
        bsel = [rta(1378 + 123 * k, 3, NB1) for k in range(2)]
        eid = rta(1624, NB1, parts=1)
        ecmp = area(13824, NB1, NE, parts=1)
        gate2 = sb("gate2", [P, 2, 3])
        tokid = sb("tokid", [P, 3])
        iotab = sb("iotab", [P, B])
        rev4 = sb("rev4", [P, NEG])
        rowidx = sb("rowidx", [P, 2, 3], I32)
        gslot = sb("gslot", [P, 2, 3])
        bnst = sb("bnst", [P, 4, 6])
        bnag = sb("bnag", [P, 2])
        rs1 = sb("rs1", [P, 1])
        plan = sb("plan", [1, NB1 + 1], I32)
        idxs = sb("idxs", [B, NB1], I32)
        idx1 = sb("idx1", [B, 1], I32)

        block = ctx.enter_context(nc.Block())

        def bc(ap, at, n):
            v = ap.unsqueeze(at)
            return v.to_broadcast([*v.shape[:at], n, *v.shape[at + 1:]])

        N_MIX, N_SQ, N_SV, N_V, N_WO = 2 * KC, 2 * KC + 96, 2 * KC + 112, 2 * KC + 128, 2 * KC + 136
        MIX = 3 * SLOTS

        def used(n):
            return SLOTS + n + 1

        def loaded(n):
            def pages_of(m):
                return N_V <= m < N_WO or (N_SV <= m < N_V and (m - N_SV) % 2 == 1)
            return 16 * sum(2 if pages_of(m) else 1 for m in range(n % SLOTS, n + 1, SLOTS))

        @block.sync
        def _(sp):
            def put(n_wait, slot, src):
                sp.wait_ge(ring_used, n_wait)
                sp.dma_start(ring[:, slot, :], src).then_inc(slot_loaded[slot], 16)

            sp.dma_start(cin[:], cT.rearrange("p m r -> p (m r)")).then_inc(c_loaded, 16)
            sp.dma_start(pages[:], page_table[:]).then_inc(pages_loaded, 16)
            with sp.Fori(0, 2) as g:
                for t in range(KC):
                    put(g * KC + (t + 1), t % SLOTS, w_ada[bass.ds(g, 1), t].rearrange("g p n -> p (g n)"))
            with sp.Fori(0, 4) as g:
                for c in range(SLOTS):
                    for t in (2 * c, 2 * c + 1):
                        k = 3 * c + t % 2
                        put(g * MIX + (N_MIX + k + 1), k % SLOTS,
                            w_ada[bass.ds(g + 2, 1), t].rearrange("g p n -> p (g n)"))
                    k = 3 * c + 2
                    put(g * MIX + (N_MIX + k + 1), k % SLOTS, w_in[bass.ds(g, 1), c].rearrange("g p n -> p (g n)"))
            with sp.Fori(0, 2) as g:
                for c in range(SLOTS):
                    put(g * SLOTS + (N_SQ + c + 1), c, w_in[bass.ds(g + 4, 1), c].rearrange("g p n -> p (g n)"))
            sp.wait_ge(pages_loaded, 16)

            def put_pages(n, b, cache):
                sp.wait_ge(ring_used, n + 1)
                for pg in range(NPG):
                    i = b * NPG + pg
                    page = sp.value_load(pages[0:1, i:i + 1], min_val=0, max_val=NPHYS - 1)
                    sp.dma_start(ring[:, n % SLOTS, pg * 1024:(pg + 1) * 1024],
                                 cache[bass.ds(page, 1)].rearrange("g p n -> p (g n)")
                                 ).then_inc(slot_loaded[n % SLOTS], 16)

            for c in range(SLOTS):
                put(N_SV + 2 * c + 1, 2 * c % SLOTS, w_in[6, c])
                put_pages(N_SV + 2 * c + 1, c, cache_k)
            for b in range(NSEQ):
                put_pages(N_V + b, b, cache_v)
            with sp.Fori(0, 2) as g:
                for c in range(SLOTS):
                    put(g * SLOTS + (N_WO + c + 1), c, w_o[bass.ds(g, 1), c].rearrange("g p n -> p (g n)"))
            sp.wait_ge(plan_ready, 1)
            nblocks = sp.value_load(plan[0:1, NB1:NB1 + 1], min_val=0, max_val=NBLK)
            with sp.Fori(0, NBLK) as i:
                with sp.If(i < nblocks):
                    e = sp.value_load(plan[0:1, bass.ds(i, 1)], min_val=0, max_val=NE - 1)
                    for c in range(MOE_CHUNKS):
                        dst = ring[:, c, :] if c < SLOTS else mslot[c - SLOTS]
                        if c < 8:
                            w, q = (w_gate, w_up)[c // 4], c % 4
                            src = w[bass.ds(e, 1)].rearrange("e (p t) n -> p (e t) n", p=P)[:, 4 * q:4 * q + 4, :]
                            dst = dst.rearrange("p (t n) -> p t n", t=4)
                        else:
                            q = c - 8
                            src = w_down[bass.ds(e, 1)].rearrange("e f n -> (e f) n")[P * q:P * (q + 1), :]
                        sp.wait_ge(moe_used, i * MOE_CHUNKS + (c + 1))
                        sp.dma_start(dst, src).then_inc(moe_loaded[c], 16)
            sp.wait_ge(y_stored, nblocks * 32 + 32)
            sp.sem_inc(wait_carrier, 1)
            sp.wait_ge(k_stored, 3 * 16)
            sp.wait_ge(v_stored, 3 * 16)
            sp.wait_ge(sprompt_stored, 2 * 16)
            sp.wait_ge(ssample_stored, H * 16)
            sp.wait_ge(u2_stored, 3 * 16)
            sp.wait_ge(out_stored, 3 * 16)

        @block.gpsimd
        def _(pool):
            count = [0]

            def link(ins):
                count[0] += 1
                ins.then_inc(pool_step, 1)
                pool.wait_ge(pool_step, count[0])

            def keep(view, pattern, base_, cm, fill, op=ALU.is_ge):
                link(nc.gpsimd.affine_select(out=view, in_=view, pattern=pattern, compare_op=op, fill=fill,
                                             base=base_, channel_multiplier=cm))

            pool.dma_start(uT, xT[:]).then_inc(x_loaded, 16)
            pool.dma_start(badaT[:], b_adaT[:]).then_inc(small_loaded, 16)
            pool.dma_start(lbt[:, 0:2, :], lb_logits[:]).then_inc(small_loaded, 16)
            pool.dma_start(normw[:], norms[:]).then_inc(small_loaded, 16)
            pool.dma_start(biasb[:], sb_bias.partition_broadcast(P)).then_inc(small_loaded, 16)
            pool.dma_start(ln1t[:], ln1[:]).then_inc(small_loaded, 16)
            pool.dma_start(wr[:], w_r[:]).then_inc(small_loaded, 16)
            pool.dma_start(br[:], b_r.partition_broadcast(P)).then_inc(small_loaded, 16)
            for j in range(4):
                pool.dma_start(bg2[32 * j:32 * j + 32, :], b_g2[j].partition_broadcast(32)).then_inc(small_loaded, 16)

            g = nc.gpsimd
            g.memset(ones[:], 1.0)
            g.memset(ident[:], 0.0)
            g.memset(tri[:], 1.0)
            g.memset(causal[:], 1.0)
            g.memset(negmask[:], 0.0)
            g.memset(chunkmask[:], 1.0)
            g.memset(strict4[:], 1.0)
            g.memset(incl4[:], 1.0)
            g.memset(neg4[:], 0.0)
            g.memset(seqmask[:], 1.0)
            g.memset(rowsel[:], 0.0)
            g.iota(tokid[:], [[P, 3]], base=0, channel_multiplier=1, allow_small_or_imprecise_dtypes=True)
            g.iota(iotab[:], [[1, B]], base=0, channel_multiplier=0, allow_small_or_imprecise_dtypes=True)
            g.iota(rev4[:], [[-1, NEG]], base=NEG, channel_multiplier=0, allow_small_or_imprecise_dtypes=True)
            g.memset(epsr[:, 0:1], RMS_EPS)
            link(g.memset(epsr[:, 1:2], LN_EPS))
            keep(ident[:], [[-1, P]], 0, 1, 1.0, ALU.not_equal)
            keep(tri[:], [[-1, P]], 0, 1, 0.0)
            for v, fill in ((causal, 0.0), (negmask, NEG_BIG)):
                keep(v[:, 0:128], [[1, P]], -1, -1, fill)
                keep(v[:, 256:384], [[1, P]], -1, -1, fill)
            keep(chunkmask[:], [[1, P]], 0, -1, 0.0)
            v = chunkmask[:].rearrange("p (a b) -> p a b", b=CH)
            keep(v, [[-CH, P // CH], [0, CH]], 0, 1, 0.0)
            for m, lo, fill in ((strict4, -1, 0.0), (neg4, -1, NEG_BIG), (incl4, 0, 0.0)):
                keep(m[:], [[1, TS]], lo, -1, fill)
                v = m[:].rearrange("p (a b) -> p a b", b=SS)
                keep(v, [[-SS, NSEQ], [0, SS]], 0, 1, fill)
            keep(seqmask[:], [[-SS, NSEQ]], 0, 1, 0.0)
            keep(seqmask[:], [[SS, NSEQ]], SS - 1, -1, 0.0)
            link(g.memset(rowsel[0:1, 0:P], 1.0))
            link(g.memset(rowsel[0:TS, P:P + TS], 1.0))
            v = rowsel[0:TS, P:P + TS].rearrange("p (a b) -> p a b", b=SS)
            keep(v, [[-1, NSEQ], [0, SS]], -1, 1, 0.0, ALU.is_equal)
            for j in range(1, 4):
                link(g.tensor_copy(rowsel[32 * j:32 * j + 32, :], rowsel[0:32, :]))
            pool.sem_inc(consts_ready, 1)

            for h in range(2):
                pool.dma_start(s0[h], state[:, h].rearrange("b p v -> p b v")).then_inc(s0_loaded[h], 16)
            pool.wait_ge(evac_act, 15)
            pool.wait_ge(evac_dve, 15)
            for h in range(H):
                if h >= 1:
                    pool.wait_ge(us_pe, 2 * h)
                nc.gpsimd.tensor_tensor(vblk, bc(tok[0:TS, 5, h * P:(h + 1) * P], 1, NSEQ),
                                        bc(seqmask[:], 2, P), ALU.mult).then_inc(vblk_ready, 1)
                pool.wait_ge(us_dve, 3 * (h + 1))
                pool.dma_start(s_s[:, h].rearrange("b p v -> p b v"), s0[h % 2]).then_inc(ssample_stored, 16)
                if h + 2 < H:
                    pool.wait_ge(ssample_stored, 16 * (h + 1))
                    pool.dma_start(s0[h % 2], state[:, h + 2].rearrange("b p v -> p b v")
                                   ).then_inc(s0_loaded[h % 2], 16)
                if h % 4 == 3:
                    pool.wait_ge(u_dve, 8 * (h // 4 + 1))
                    pool.dma_start(s_p[h - 3:h + 1].rearrange("h p v -> p h v"), shist[:, 7, :, :]
                                   ).then_inc(sprompt_stored, 16)

            for i, (t0, tn) in enumerate(TILES):
                pool.wait_ge(kout_evac, i + 1)
                dst = k_p[t0:t0 + tn, :] if i < 2 else k_s[:]
                pool.dma_start(dst, kstage[0:tn, i, :]).then_inc(k_stored, 16)
            pool.wait_ge(evac_act, 24)
            pool.wait_ge(evac_dve, 24)
            for i, (t0, tn) in enumerate(TILES):
                dst = v_p[t0:t0 + tn, :] if i < 2 else v_s[:]
                pool.dma_start(dst, tok[0:tn, i, :]).then_inc(v_stored, 16)

            pool.wait_ge(o_pe, H)
            pool.wait_ge(ss_pe, 4)
            pool.dma_start(xa, xT[:]).then_inc(xa_loaded, 16)
            g.memset(zeros, 0.0).then_inc(zeros_ready, 1)
            pool.wait_ge(xa_loaded, 16)
            nc.gpsimd.tensor_scalar(xa, xa, ALPHA, 0.0, ALU.mult, ALU.add).then_inc(xa_ready, 1)
            pool.wait_ge(zeros_ready, 1)
            pool.dma_start(y_rows.rearrange("(n p) d -> p n d", p=P), bc(zeros, 1, NBLK * B // P)
                           ).then_inc(y_zeroed, 16)

            for i, (t0, tn) in enumerate(TILES):
                pool.wait_ge(tt_act, 4 * (i + 1))
                pool.dma_start(u2_rows[t0:t0 + tn, :], urow[i][0:tn, :]).then_inc(u2_stored, 16)
            pool.wait_ge(plan_ready, 2)
            nblocks = pool.value_load(plan[0:1, NB1:NB1 + 1], min_val=0, max_val=NBLK)
            pool.wait_ge(u2_stored, 3 * 16)

            def gather(n):
                pool.wait_ge(idx_ready, n)
                pool.sem_inc(wait_carrier, 1)
                nc.gpsimd.indirect_dma_start(out=xg, out_offset=None, in_=u2_rows[:],
                                             in_offset=bass.IndirectOffsetOnAxis(idx1[:, 0:1], 0)
                                             ).then_inc(gathered, 16)

            nc.gpsimd.tensor_copy(idx1[:], idxs[:, 0:1]).then_inc(idx_ready, 1)
            pool.wait_ge(tt_act, 24)
            gather(1)
            pool.dma_start(ln2b, ln2.partition_broadcast(P)).then_inc(late_loaded, 16)
            with pool.Fori(0, NBLK) as i:
                with pool.If(i < nblocks):
                    pool.wait_ge(gathered, i * 16 + 16)
                    nc.gpsimd.tensor_copy(idx1[:], idxs[:, bass.ds(i + 1, 1)]).then_inc(idx_ready, 1)
                    pool.wait_ge(x_turned, i + 1)
                    gather(i + 2)
            pool.wait_ge(y_stored, nblocks * 32 + 32)
            pool.wait_ge(gathered, nblocks * 16 + 16)
            pool.wait_ge(x_copied, nblocks + 1)
            pool.sem_inc(wait_carrier, 1)
            for i, (t0, tn) in enumerate(TILES):
                for k, dst in enumerate((ya, yb)):
                    nc.gpsimd.indirect_dma_start(out=dst[i][0:tn, :], out_offset=None, in_=y_rows[:],
                                                 in_offset=bass.IndirectOffsetOnAxis(rowidx[0:tn, k, i:i + 1], 0)
                                                 ).then_inc(fin_gather[i], 16)

        @block.tensor
        def _(pe):
            mm = nc.tensor.matmul

            def ada_chunk(slot, is_loaded, t, freed):
                pe.wait_ge(slot_loaded[slot], is_loaded)
                if t == 0 and freed is not None:
                    pe.wait_ge(rows_copied, freed)
                for j in range(4):
                    last = mm(ps[32 * j:32 * j + 32, 0, :], silu_c[:, t, :], ring[:, slot, 512 * j:512 * (j + 1)],
                              start=(t == 0), stop=(t == KC - 1))
                last.then_inc(ring_used, 1)

            def ada_turn(copied, freed):
                pe.wait_ge(rows_copied, copied)
                if freed is not None:
                    pe.wait_ge(ada_ready, freed)
                for c in range(4):
                    last = nc.tensor.transpose(ps[:, 1, P * c:P * (c + 1)], ada_rows[:, P * c:P * (c + 1)], ident[:])
                last.then_inc(rows_turned, 1)

            def head_chunk(slot, bank):
                for t in range(KC):
                    last = mm(ps[:, bank, 0:T], ring[:, slot, P * t:P * (t + 1)], uT[:, t, :],
                              start=(t == 0), stop=(t == KC - 1))
                last.then_inc(ring_used, 1)

            def row_chunk(slot, c):
                for t in range(4):
                    for i, (t0, tn) in enumerate(TILES):
                        last = mm(ps[0:tn, 4 + i, :], uT[:, 4 * (c % 4) + t, t0:t0 + tn],
                                  ring[:, slot, 512 * t:512 * (t + 1)],
                                  start=(c % 4 == 0 and t == 0), stop=(c % 4 == 3 and t == 3))
                last.then_inc(ring_used, 1)

            pe.sem_inc(ring_used, SLOTS)
            pe.sem_inc(hT_pe, 1)
            pe.wait_ge(silu_c_ready, 1)
            pe.wait_ge(consts_ready, 1)
            for six in range(2):
                for t in range(KC):
                    n = six * KC + t
                    ada_chunk(n % SLOTS, loaded(n), t, six if six else None)
                ada_turn(six + 1, six if six else None)

            pe.wait_ge(u_ready, 1)
            with pe.Fori(0, 3) as g:
                for c in range(SLOTS):
                    for t in (2 * c, 2 * c + 1):
                        n = N_MIX + 3 * c + t % 2
                        ada_chunk(n % SLOTS, g * 48 + loaded(n), t, g + 2)
                    n = N_MIX + 3 * c + 2
                    pe.wait_ge(slot_loaded[n % SLOTS], g * 48 + loaded(n))
                    pe.wait_ge((evac_act, evac_dve)[c % 2], g * 4 + (2 + c // 2 - 1))
                    head_chunk(n % SLOTS, 4 + c % 4)
                ada_turn(g + 3, g + 2)

            def chunk_scores(tt):
                for h in range(H):
                    last = mm(ps[:, 2 + h // 4, P * (h % 4):P * (h % 4 + 1)],
                              khat[:, h, P * tt:P * (tt + 1)], qhat[:, h, P * tt:P * (tt + 1)], start=True, stop=True)
                return last

            for c in range(SLOTS):
                for t in (2 * c, 2 * c + 1):
                    n = N_MIX + 3 * MIX + 3 * c + t % 2
                    ada_chunk(n % SLOTS, loaded(n), t, 5)
                n = N_MIX + 3 * MIX + 3 * c + 2
                pe.wait_ge(slot_loaded[n % SLOTS], loaded(n))
                if c == 0:
                    pe.wait_ge(evac_act, 14)
                    pe.wait_ge(evac_dve, 14)
                if c == 4:
                    pe.wait_ge(evac_act, 15)
                row_chunk(n % SLOTS, c)
                if c == 2:
                    pe.wait_ge(hg_dve, 3)
                    for h in range(H):
                        mm(ps[0:TS, 7, TS * h:TS * (h + 1)], khat[:, h, TP:T], qhat[:, h, TP:T], start=True, stop=True)
                    chunk_scores(0).then_inc(hg_pe, 1)
                if c == 5:
                    pe.wait_ge(hg_dve, 7)
                    chunk_scores(1).then_inc(hg_pe, 1)

            pe.wait_ge(evac_dve, 15)
            for half in range(2):
                heads = range(4 * half, 4 * half + 4)
                if half == 0:
                    pe.wait_ge(rows_copied, 6)
                    pe.wait_ge(ada_ready, 5)
                    pe.wait_ge(hg_dve, 8)
                else:
                    pe.wait_ge(us_dve, 12)
                    pe.wait_ge(osm_dve, 1)
                    pe.wait_ge(hgo_act, 2)
                for tt in range(2):
                    for h in range(4):
                        nc.tensor.transpose(ps[:, tt, P * h:P * (h + 1)],
                                            hf[:, heads[h], P * tt:P * (tt + 1)], ident[:])
                for h in range(4):
                    last = nc.tensor.transpose(ps[0:TS, 7, P * h:P * (h + 1)], hf[:, heads[h], TP:T], ident[:])
                last.then_inc(kd_pe, 1)
                for c in range(8):
                    n = N_SQ + 8 * half + c
                    pe.wait_ge(slot_loaded[c], loaded(n))
                    pe.wait_ge((evac_act, evac_dve)[c % 2], 15 + 4 * half + c // 2)
                    head_chunk(c, 4 + c % 2)
                    if c == 0:
                        pe.wait_ge(kd_act, half + 1)
                        pe.wait_ge(qpad_ready, half + 1)
                    if 8 * half + c >= 1:
                        pe.wait_ge(u_dve, 8 * half + c)
                    tt, r0 = c // 4, CH * (c % 4)
                    for h in range(4):
                        k = heads[h]
                        last = mm(ps[:, 2, P * h:P * (h + 1)], kdt[r0:r0 + CH, tt, h, :],
                                  tok[r0:r0 + CH, 3 + tt, P * k:P * (k + 1)], start=True, stop=True,
                                  tile_position=(r0, 0))
                    last.then_inc(u_pe, 1)
                    if c % 2 == 0:
                        continue
                    h = c // 2
                    k = heads[h]
                    pe.wait_ge(s0_loaded[k % 2], 16 * (k // 2 + 1))
                    for b in range(NSEQ):
                        mm(ps[32 * h:32 * h + 32, 3, 0:P], qpad[:, h, b, :], s0[k % 2][:, b, :],
                           start=(b == 0), stop=False)
                    mm(ps[32 * h:32 * h + 32, 3, 0:P], abufs[:, k, :], tok[0:TS, 5, P * k:P * (k + 1)],
                       start=False, stop=True).then_inc(os_pe, 1)
                    pe.wait_ge(vblk_ready, k + 1)
                    for part in range(2):
                        if k >= 1:
                            pe.wait_ge(us_dve, 3 * k - 1 + part)
                        mm(ps[:, part, :], kdts[:, h, :],
                           vblk[:, 4 * part:4 * part + 4, :].rearrange("p b v -> p (b v)"), start=True, stop=True
                           ).then_inc(us_pe, 1)
                pe.wait_ge(u_dve, 8 * half + 7)
                for pair in range(2):
                    if pair == 1:
                        pe.wait_ge(osr_dve, half + 1)
                        nc.tensor.transpose(ps[:, 3, P:2 * P], osr, ident[:]).then_inc(osr_pe, 1)
                        pe.wait_ge(hgo_act, 2 * half + 1)
                    for tt in range(2):
                        for h in (2 * pair, 2 * pair + 1):
                            k = heads[h]
                            o = ps[:, 7, 256 * (h % 2) + P * tt:256 * (h % 2) + P * (tt + 1)]
                            mm(o, tok[:, 3 + tt, P * k:P * (k + 1)], abuf[:, tt, k, :], start=True, stop=False)
                            for c4 in range(4):
                                c = 4 * tt + c4
                                if c == 0:
                                    continue
                                last = mm(o[:, CH * c4:CH * (c4 + 1)], shist[:, c - 1, h, :],
                                          hq[:, k, CH * c:CH * (c + 1)], start=False, stop=(c4 == 3))
                    last.then_inc(hgo_pe, 1)

            pe.wait_ge(evac_act, 23)
            pe.wait_ge(evac_dve, 23)
            pe.wait_ge(us_dve, 3 * H)
            pe.wait_ge(u_dve, 16)
            pe.wait_ge(osm_dve, 2)
            for i, (t0, tn) in enumerate(TILES):
                if i == 2:
                    pe.wait_ge(kout_evac, 1)
                for h in range(H):
                    last = nc.tensor.transpose(ps[0:tn, 2 * (i % 2) + h // 4, P * (h % 4):P * (h % 4 + 1)],
                                               skT[:, h, t0:t0 + tn], ident[:])
                last.then_inc(kout_pe, 1)

            for c in range(SLOTS + 1):
                if c < SLOTS:
                    n = N_SV + 2 * c
                    pe.wait_ge(slot_loaded[n % SLOTS], loaded(n))
                    if c == 4:
                        pe.wait_ge(evac_act, 24)
                    row_chunk(n % SLOTS, c)
                if c >= 1:
                    pe.wait_ge(kT_act, c)
                    pe.wait_ge(kT_dve, c)
                    pe.wait_ge(hgo_act, 4)
                    if c >= 2:
                        pe.wait_ge(zt_dve, c - 1)
                    for h in range(H):
                        i, j = h // 4, h % 4
                        last = mm(ps[32 * j:32 * j + 32, 7, 256 * i:256 * (i + 1)], sqT[:, h, TP:T], keyT[:, h, :],
                                  start=True, stop=True)
                    last.then_inc(zr_pe, 1)
                if c < SLOTS:
                    n = N_SV + 2 * c + 1
                    pe.wait_ge(slot_loaded[n % SLOTS], loaded(n))
                    if c == 0:
                        pe.wait_ge(kout_evac, 3)
                    for pg in range(NPG):
                        for h in range(H):
                            last = nc.tensor.transpose(ps[:, 2 * pg + h // 4, P * (h % 4):P * (h % 4 + 1)],
                                                       ring[:, n % SLOTS, 1024 * pg + P * h:1024 * pg + P * (h + 1)],
                                                       ident[:])
                        last.then_inc((kT_pe, ring_used)[pg], 1)
                if c >= 1:
                    pe.wait_ge(zr_dve, c)
                    for pg in range(NPG):
                        for i in range(2):
                            q = 2 * pg + i
                            last = nc.tensor.transpose(ps[:, 7, P * q:P * (q + 1)],
                                                       zrow[:, 256 * i + P * pg:256 * i + P * (pg + 1)], ident[:])
                    last.then_inc(zt_pe, 1)
            pe.wait_ge(evac_act, 24)
            pe.wait_ge(evac_dve, 24)
            pe.wait_ge(zt_dve, NSEQ)

            for h in range(H + 2):
                if h < H:
                    if h >= 2:
                        pe.wait_ge(z_dve, h - 1)
                    z = ps[:, 2 + h % 2, :]
                    mm(z[:, 0:256], skT[:, h, 0:128], sqT[:, h, 0:256], start=True, stop=True)
                    mm(z[:, 256:384], skT[:, h, 128:256], sqT[:, h, 128:256], start=True, stop=True
                       ).then_inc(z_pe, 1)
                if 1 <= h <= H:
                    k = h - 1
                    pe.wait_ge(sp_ready, k + 1)
                    if k >= 2:
                        pe.wait_ge(d_dve, k - 1)
                    c, s = ps[:, 4 + k % 2, :], spl[k % 2]
                    mm(c[:, 0:256], tri[:], s[:, 0:256], start=True, stop=False)
                    mm(c[:, 128:256], ones[:], s[:, 256:384], start=False, stop=True)
                    mm(c[:, 256:384], tri[:], s[:, 256:384], start=True, stop=True).then_inc(c_pe, 1)
                if h >= 2:
                    k = h - 2
                    pe.wait_ge(a_ready, k + 1)
                    if k >= 2:
                        pe.wait_ge(o_evac, k - 1)
                    o, a = ps[:, 6 + k % 2, :], aa[k % 2]
                    mm(o[:, 0:256], tok[:, 0, P * k:P * (k + 1)], a[:, 0:256], start=True, stop=False)
                    mm(o[:, 128:256], tok[:, 1, P * k:P * (k + 1)], a[:, 256:384], start=False, stop=True
                       ).then_inc(o_pe, 1)
                if h == 0:
                    pe.wait_ge(kT_act, NSEQ)
                    pe.wait_ge(kT_dve, NSEQ)
                    for k in range(H):
                        last = mm(ps[0:TS, 0, TS * k:TS * (k + 1)], skT[:, k, TP:T], sqT[:, k, TP:T],
                                  start=True, stop=True)
                    last.then_inc(ss_pe, 1)
                if h == 3:
                    pe.wait_ge(ss_dve, 2)
                    c = ps[:, 1, :].rearrange("p (g b h t) -> p g b h t", g=NPG, b=NSEQ, h=H)
                    s_new = sN.rearrange("p h (b t) -> p b h t", t=SS)
                    s_past = sP.rearrange("p (g b) h t -> p g (b h t)", g=NPG)
                    cf = ps[:, 1, :].rearrange("p (g n) -> p g n", g=NPG)
                    mm(cf[:, 1], tri[:], s_past[:, 1], start=True, stop=False)
                    mm(c[:, 1], ones[0:TS, :], s_new, start=False, stop=True)
                    mm(cf[:, 0], tri[:], s_past[:, 0], start=True, stop=False)
                    mm(cf[:, 0], ones[:], s_past[:, 1], start=False, stop=False)
                    mm(c[:, 0], ones[0:TS, :], s_new, start=False, stop=True)
                    mm(ps[0:TS, 0, 0:TS * H], tri[0:TS, 0:TS], sN.rearrange("p h t -> p (h t)"), start=True, stop=True
                       ).then_inc(ss_pe, 1)
                if h == 5:
                    pe.wait_ge(ss_act, 2)
                    for b in range(NSEQ):
                        pe.wait_ge(slot_loaded[b], loaded(N_V + b))
                        for pg in range(NPG):
                            for k in range(H):
                                i, j = k // 4, k % 4
                                last = mm(ps[32 * j:32 * j + 32, i, 0:P], apad[:, pg, b, k, :],
                                          ring[:, b, 1024 * pg + P * k:1024 * pg + P * (k + 1)],
                                          start=(b == 0 and pg == 0), stop=False)
                        last.then_inc(ring_used, 1)
                    for k in range(H):
                        i, j = k // 4, k % 4
                        last = mm(ps[32 * j:32 * j + 32, i, 0:P], aN[:, k, :], tok[0:TS, 2, P * k:P * (k + 1)],
                                  start=False, stop=True)
                    last.then_inc(ss_pe, 1)
                if h == 8:
                    pe.wait_ge(ss_dve, 4)
                    for i in range(2):
                        last = nc.tensor.transpose(ps[:, 0, P * i:P * (i + 1)], orow[:, i, :], ident[:])
                    last.then_inc(ss_pe, 1)

            for k in range(2 * H):
                pe.wait_ge(nsq_act, k + 1)
                if k >= 2:
                    pe.wait_ge(nrs_act, k - 1)
                mm(ps[:, 2 + k % 2, 0:T], ones[:], sqo[k % 2], start=True, stop=True).then_inc(nm_pe, 1)

            pe.wait_ge(nm_dve, 2 * H)
            pe.wait_ge(nrs_act, 2 * H)

            pe.wait_ge(d_dve, H)
            pe.wait_ge(o_evac, H)

            def sums(m):
                pe.wait_ge(wo_act, m + 1)
                mm(ps[:, 2, 0:T], ones[:], rT[:, m, :], start=(m == 0), stop=(m == KC - 1))
                mm(ps[:, 3, 0:T], ones[:], r2[m % 4], start=(m == 0), stop=(m == KC - 1)).then_inc(st_pe, 1)

            for m in range(KC):
                n = N_WO + m
                pe.wait_ge(slot_loaded[n % SLOTS], loaded(n))
                if m >= 4:
                    pe.wait_ge(wo_dve, m - 3)
                for k in range(KC):
                    last = mm(ps[:, 4 + m % 4, 0:T], ring[:, n % SLOTS, P * k:P * (k + 1)], mixT[:, k, :],
                              start=(k == 0), stop=(k == KC - 1))
                last.then_inc(ring_used, 1)
                if m >= 2:
                    sums(m - 2)
            sums(KC - 2)
            sums(KC - 1)

            pe.sem_inc(moe_used, SLOTS)
            pe.wait_ge(wo_dve, KC)
            for m in range(KC):
                pe.wait_ge(u2_dve, m + 1)
                last = mm(ps[0:NL, 4, 0:T], wr[:, m, :], u2T[:, m, :], start=(m == 0), stop=(m == KC - 1))
            last.then_inc(rt_pe, 1)

            def turn_tokens(n, src):
                i, q = n // 4 % 3, n % 4
                t0, tn = TILES[i]
                if n >= 2:
                    pe.wait_ge(tt_act, n - 1)
                for m in range(4):
                    last = nc.tensor.transpose(ps[0:tn, 6 + n % 2, P * m:P * (m + 1)],
                                               src[:, 4 * q + m, t0:t0 + tn], ident[:])
                last.then_inc(tt_pe, 1)

            pe.wait_ge(rt_act, 1)
            for i, (t0, tn) in enumerate(TILES):
                last = nc.tensor.transpose(ps[0:tn, 5, 64 * i:64 * i + NL], lgT[:, t0:t0 + tn], ident[0:NL, 0:NL])
            last.then_inc(rt_pe, 1)
            for n in range(12):
                turn_tokens(n, u2T)
            pe.wait_ge(rt_dve, 1)
            for i in range(3):
                mm(ps[:, 2, NE * i:NE * (i + 1)], causal[:, 0:P], both[:, i, :], start=True, stop=(i == 0))
                for k in range(i):
                    mm(ps[:, 2, NE * i:NE * (i + 1)], ones[:], both[:, k, :], start=False, stop=(k == i - 1))
            for i in range(3):
                last = mm(ps[:, 3, 0:NE], ones[:], both[:, i, :], start=(i == 0), stop=(i == 2))
            last.then_inc(rt_pe, 1)
            for n in range(12, 24):
                turn_tokens(n, rT)
            pe.wait_ge(rt_dve, 2)
            for k in range(2):
                for i in range(3):
                    last = mm(ps[0:B, 4, 0:NB1], rsel[k][:, i, :], bsel[k][:, i, :],
                              start=(k == 0 and i == 0), stop=(k == 1 and i == 2))
            last.then_inc(rt_pe, 1)
            pe.wait_ge(tt_act, 24)

            pe.sem_inc(moe_used, MOE_CHUNKS - SLOTS)
            pe.wait_ge(ss_dve, 5)
            pe.wait_ge(plan_ready, 2)
            nblocks = pe.value_load(plan[0:1, NB1:NB1 + 1], min_val=0, max_val=NBLK)

            def turn_rows(n):
                pe.wait_ge(gathered, n * 16)
                pe.sem_inc(wait_carrier, 1)
                for m in range(KC):
                    last = nc.tensor.transpose(ps[:, m // 8, B * (m % 8):B * (m % 8 + 1)], xg[:, P * m:P * (m + 1)],
                                               ident[0:B, 0:B])
                last.then_inc(x_turned, 1)

            turn_rows(1)
            for j in range(4):
                if j >= 1:
                    pe.wait_ge(g2_act, j)
                r = slice(32 * j, 32 * j + 32)
                mm(ps[:, 2, :], rowsel[r, 0:P], ada_rows[r, :], start=True, stop=True, tile_position=(32 * j, 0))
                mm(ps[0:TS, 3, :], rowsel[r, P:P + TS], ada_rows[r, :], start=True, stop=True,
                   tile_position=(32 * j, 0)).then_inc(g2_pe, 1)
            pe.wait_ge(g2_act, 4)
            with pe.Fori(0, NBLK) as i:
                with pe.If(i < nblocks):
                    pe.wait_ge(x_copied, i + 1)
                    for c in range(8):
                        pe.wait_ge(moe_loaded[c], i * 16 + 16)
                        for t in range(4):
                            for s in range(2):
                                last = mm(ps[B * s:B * (s + 1), 2 + c // 4, 0:256], xgT[:, 4 * (c % 4) + t, :],
                                          ring[:, c, 512 * t + 256 * s:512 * t + 256 * (s + 1)],
                                          start=(c % 4 == 0 and t == 0), stop=(c % 4 == 3 and t == 3))
                        last.then_inc(moe_used, 1)
                    turn_rows(i + 2)
                    pe.wait_ge(hid_dve, i + 2)
                    for cb in range(2):
                        last = nc.tensor.transpose(ps[:, 4, P * cb:P * (cb + 1)], hid[:, P * cb:P * (cb + 1)], ident[:])
                    last.then_inc(hT_pe, 1)
                    pe.wait_ge(hT_dve, i + 1)
                    pe.wait_ge(y_evac, i * 2 + 2)
                    for q in range(4):
                        pe.wait_ge(moe_loaded[8 + q], i * 16 + 16)
                        for nn in range(2):
                            for s in range(2):
                                last = mm(ps[B * s:B * (s + 1), 5 + nn, :], hT[:, q % 2, B * (q // 2):B * (q // 2 + 1)],
                                          mslot[q][:, 1024 * s + 512 * nn:1024 * s + 512 * (nn + 1)],
                                          start=(q == 0), stop=(q == 3))
                        last.then_inc(moe_used, 1)

        @block.scalar
        def _(act):
            A = nc.scalar.activation
            count = [0]

            def link(ins):
                count[0] += 1
                ins.then_inc(act_step, 1)
                act.wait_ge(act_step, count[0])

            act.sem_inc(evac_act, 2)
            act.sem_inc(y_stored, 32)
            act.wait_ge(c_loaded, 16)
            A(ctmp[:], cin[:], ACT.Exp, scale=-1.0).then_inc(expc_ready, 1)

            with act.Fori(0, 2) as g:
                for c in range(0, SLOTS, 2):
                    act.wait_ge(ring_used, g * MIX + used(N_MIX + 3 * c + 2))
                    nc.scalar.copy(hf_hq[:, bass.ds(g * H + c, 1), :].rearrange("p a t -> p (a t)"),
                                   ps[:, 4 + c % 4, 0:T]).then_inc(evac_act, 1)

            def evacuate_head(dst, n, bank):
                act.wait_ge(ring_used, used(n))
                nc.scalar.copy(dst, ps[:, bank, 0:T]).then_inc(evac_act, 1)

            def evacuate_rows(n, slot):
                act.wait_ge(ring_used, used(n))
                for i, (t0, tn) in enumerate(TILES):
                    last = nc.scalar.copy(tok[0:tn, slot + i, 0:512], ps[0:tn, 4 + i, :])
                last.then_inc(evac_act, 1)

            act.wait_ge(lb_dve, 1)
            A(lbt[:, 2, :], lbt[:, 2, :], ACT.Exp).then_inc(lb_act, 1)
            act.wait_ge(evac_act, 2 + 8)
            act.wait_ge(evac_dve, 2 + 8)
            A(qhat, hq, ACT.Exp, scale=-1.0)
            A(t1, hf, ACT.Exp, scale=-1.0).then_inc(hg_act, 1)
            N_G = N_MIX + 2 * MIX + 2
            evacuate_head(hg[:, 0, :], N_G, 4)
            act.wait_ge(hg_dve, 1)
            A(t1, t1, ACT.Ln).then_inc(hg_act, 1)
            evacuate_head(hg[:, 2, :], N_G + 3 * 2, 6)
            act.wait_ge(hg_dve, 2)
            A(qhat, t1, ACT.Exp)
            A(khat, t1, ACT.Exp, scale=-1.0).then_inc(hg_act, 1)
            act.wait_ge(hg_act, 3)
            A(t1, bcum, ACT.Exp)
            bp = bcum[:, :, 0:TP].rearrange("p h (c t) -> p h c t", t=CH)
            bs = bcum[:, :, TP:T].rearrange("p h (c t) -> p h c t", t=SS)
            A(dec[:, :, 0:8], bp[:, :, :, CH - 1], ACT.Exp)
            A(dec[:, :, 8:16], bs[:, :, :, SS - 1], ACT.Exp).then_inc(hg_act, 1)
            evacuate_head(hg[:, 4, :], N_G + 3 * 4, 4)
            act.wait_ge(hg_dve, 4)
            A(t1, t1, ACT.Exp).then_inc(hg_act, 1)
            evacuate_head(hg[:, 6, :], N_G + 3 * 6, 6)
            act.wait_ge(hg_dve, 5)
            act.wait_ge(evac_act, 2 + 12)
            act.wait_ge(evac_dve, 2 + 12)
            A(t1, hg, ACT.Exp, scale=-1.0).then_inc(hg_act, 1)
            evacuate_rows(N_MIX + 3 * MIX + 3 * 3 + 2, 3)

            for half in range(2):
                act.wait_ge(kd_pe, half + 1)
                if half == 0:
                    act.wait_ge(hg_dve, 6)
                    act.wait_ge(hg_pe, 2)
                else:
                    act.wait_ge(us_pe, 8)
                nc.scalar.copy(kdt, ps[:, 0:2, :].rearrange("p a (h s) -> p a h s", s=P))
                nc.scalar.copy(kdts, ps[0:TS, 7, :].rearrange("p (h s) -> p h s", s=P)).then_inc(kd_act, 1)
                for c in range(0, SLOTS, 2):
                    evacuate_head(projT[:, 8 * half + c, :], N_SQ + 8 * half + c, 4)
                for pair in range(2):
                    act.wait_ge(hgo_pe, 2 * half + pair + 1)
                    k = 4 * half + 2 * pair
                    nc.scalar.copy(hout[:, k:k + 2, 0:TP], ps[:, 7, :].rearrange("p (h t) -> p h t", h=2)
                                   ).then_inc(hgo_act, 1)

            act.wait_ge(sprompt_stored, 2 * 16)
            for c in range(SLOTS):
                if c == 3:
                    act.wait_ge(ssample_stored, H * 16)
                    act.wait_ge(os_pe, H)
                    evacuate_rows(N_SV + 2 * 3, 0)
                act.wait_ge(kT_pe, c + 1)
                if c >= 1:
                    act.wait_ge(zr_pe, c)
                nc.scalar.copy(keyT[:, :, 0:P], ps[:, 0:2, :].rearrange("p a (h s) -> p (a h) s", s=P)
                               ).then_inc(kT_act, 1)

            act.wait_ge(small_loaded, 16 * 11)
            for h in range(H + 1):
                if h < H:
                    act.wait_ge(z_dve, h + 1)
                    if h >= 2:
                        act.wait_ge(sp_ready, h - 1)
                    e = ee[h % 2]
                    link(A(e, zz[h % 2], ACT.Abs))
                    link(A(e, e, ACT.Exp, scale=-1.0))
                    A(e, e, ACT.Ln, bias=1.0).then_inc(soft_act, 1)
                if h >= 1:
                    k = h - 1
                    act.wait_ge(d_dve, k + 1)
                    if k >= 2:
                        act.wait_ge(o_pe, k - 1)
                    A(aa[k % 2], zn[k % 2], ACT.Exp).then_inc(a_ready, 1)
                if h == 1:
                    act.wait_ge(ss_dve, 1)
                    A(eP, zP, ACT.Abs)
                    link(A(eN, zN, ACT.Abs))
                    A(eP, eP, ACT.Exp, scale=-1.0)
                    link(A(eN, eN, ACT.Exp, scale=-1.0))
                    A(eP, eP, ACT.Ln, bias=1.0)
                    A(eN, eN, ACT.Ln, bias=1.0).then_inc(ss_act, 1)
                if h == 4:
                    act.wait_ge(ss_dve, 3)
                    d4 = dP.rearrange("p (g b) h t -> p g b h t", g=NPG)
                    for b in range(NSEQ):
                        A(apad[:, :, b, :, SS * b:SS * (b + 1)], d4[:, :, b], ACT.Exp)
                    A(aN, dN, ACT.Exp).then_inc(ss_act, 1)

            act.wait_ge(hgo_act, 4)
            act.wait_ge(osm_dve, 2)
            act.wait_ge(ss_dve, 5)
            act.wait_ge(o_evac, H)
            act.wait_ge(consts_ready, 1)
            for k in range(2 * H + 1):
                if k < 2 * H:
                    if k >= 2:
                        act.wait_ge(nm_pe, k - 1)
                    A(sqo[k % 2], (hout if k < H else mixT)[:, k, :], ACT.Square).then_inc(nsq_act, 1)
                if k >= 1:
                    j = k - 1
                    act.wait_ge(nm_pe, j + 1)
                    if j >= 2:
                        act.wait_ge(nm_dve, j - 1)
                    link(A(rst[j % 2], ps[:, 2 + j % 2, 0:T], ACT.Ln, bias=epsr[:, 0:1], scale=1.0 / P))
                    A(rst[j % 2], rst[j % 2], ACT.Exp, scale=-0.5).then_inc(nrs_act, 1)

            for m in range(KC):
                act.wait_ge(wo_dve, m + 1)
                if m >= 4:
                    act.wait_ge(st_pe, m - 3)
                A(r2[m % 4], rT[:, m, :], ACT.Square).then_inc(wo_act, 1)
            act.wait_ge(ln_dve, 1)
            link(A(lt1, lt1, ACT.Ln, bias=epsr[:, 1:2]))
            A(rstd, lt1, ACT.Exp, scale=-0.5).then_inc(rstd_act, 1)
            for m in range(KC):
                act.wait_ge(ln_dve, 2 + m // 4)
                A(rT[:, m, :], rT[:, m, :], ACT.Identity, bias=ln1t[:, 1, m:m + 1], scale=ln1t[:, 0, m:m + 1]
                  ).then_inc(x1_act, 1)

            act.wait_ge(v_stored, 3 * 16)
            act.wait_ge(rt_pe, 1)
            nc.scalar.copy(lgT[:], ps[0:NL, 4, 0:T]).then_inc(rt_act, 1)
            for n in range(12):
                t0, tn = TILES[n // 4]
                act.wait_ge(tt_pe, n + 1)
                nc.scalar.copy(urow[n // 4][0:tn, 512 * (n % 4):512 * (n % 4 + 1)], ps[0:tn, 6 + n % 2, :]
                               ).then_inc(tt_act, 1)
            act.wait_ge(rt_dve, 3)
            A(gexp, gexp, ACT.Exp)
            A(m2, m2, ACT.Exp).then_inc(rt_act, 1)
            for n in range(12, 24):
                i, q = n // 4 - 3, n % 4
                if n == 12:
                    act.wait_ge(y_zeroed, 16)
                tn = TILES[i][1]
                act.wait_ge(tt_pe, n + 1)
                A(xres[0:tn, i, :].rearrange("t (p m) -> t m p", m=KC)[:, 4 * q:4 * q + 4, :],
                  ps[0:tn, 6 + n % 2, :].rearrange("t (m p) -> t m p", m=4), ACT.Copy, scale=ALPHA
                  ).then_inc(tt_act, 1)

            act.wait_ge(plan_ready, 2)
            nblocks = act.value_load(plan[0:1, NB1:NB1 + 1], min_val=0, max_val=NBLK)

            def copy_rows(n):
                act.wait_ge(x_turned, n)
                nc.scalar.copy(xgT, ps[:, 0:2, :].rearrange("p a (m s) -> p (a m) s", s=B)).then_inc(x_copied, 1)

            act.wait_ge(y_zeroed, 16)
            copy_rows(1)
            for j in range(4):
                act.wait_ge(g2_pe, j + 1)
                nc.scalar.copy(g2p[:, 512 * j:512 * (j + 1)], ps[:, 2, :])
                nc.scalar.copy(g2s[0:TS, 512 * j:512 * (j + 1)], ps[0:TS, 3, :]).then_inc(g2_act, 1)
            with act.Fori(0, NBLK) as i:
                with act.If(i < nblocks):
                    act.wait_ge(moe_used, i * MOE_CHUNKS + (MOE_CHUNKS + 4))
                    act.wait_ge(hid_dve, i + 1)
                    A(hsil, ps[:, 2, 0:256], ACT.Silu).then_inc(sil_act, 1)
                    copy_rows(i + 2)
                    act.wait_ge(moe_used, i * MOE_CHUNKS + 2 * MOE_CHUNKS)
                    act.wait_ge(y_stored, i * 32 + 32)
                    nc.scalar.copy(yout[:, 0:512], ps[:, 5, :]).then_inc(y_evac, 1)
                    act.wait_ge(y_evac, i * 2 + 4)
                    for s in range(2):
                        act.dma_start(y_rows[bass.ds(i * B, B), 1024 * s:1024 * (s + 1)],
                                      yout[B * s:B * (s + 1), :]).then_inc(y_stored, 16)

            for i, (t0, tn) in enumerate(TILES):
                act.wait_ge(fin_gather[i], 32)
                A(ya[i][0:tn, :], ya[i][0:tn, :], ACT.Copy, scale=gate2[0:tn, 0, i:i + 1]).then_inc(fin_act, 1)
                act.wait_ge(fin_dve, 2 * i + 1)
                link(A(rs1[0:tn, :], bnag[0:tn, 1:2], ACT.Ln, bias=epsr[0:tn, 1:2]))
                A(rs1[0:tn, :], rs1[0:tn, :], ACT.Exp, scale=-0.5).then_inc(fin_act, 1)
                act.wait_ge(fin_dve, 2 * i + 2)
                dst = y_p[t0:t0 + tn, :] if i < 2 else y_s[:]
                act.dma_start(dst, yb[i][0:tn, :]).then_inc(out_stored, 16)

        @block.vector
        def _(dve):
            v = nc.vector
            count = [0]

            def link(ins):
                count[0] += 1
                ins.then_inc(dve_step, 1)
                dve.wait_ge(dve_step, count[0])

            dve.sem_inc(evac_dve, 2)
            dve.sem_inc(hid_dve, 1)
            dve.sem_inc(y_evac, 2)
            link(v.memset(silu_c[:], 0.0))
            dve.wait_ge(expc_ready, 1)
            link(v.tensor_scalar(ctmp[:], ctmp[:], 1.0, None, ALU.add))
            link(v.reciprocal(ctmp[:], ctmp[:]))
            v.tensor_tensor(silu_c[:, :, 0:R], cin[:].rearrange("p (m r) -> p m r", r=R),
                            ctmp[:].rearrange("p (m r) -> p m r", r=R), ALU.mult).then_inc(silu_c_ready, 1)
            dve.wait_ge(small_loaded, 16 * 11)
            link(v.tensor_scalar(badaT[:, 1, :], badaT[:, 1, :], 1.0, None, ALU.add))
            link(v.tensor_scalar(badaT[:, 4, :], badaT[:, 4, :], 1.0, None, ALU.add))

            v.tensor_tensor(lbt[:, 2, :], lbt[:, 1, :], lbt[:, 0, :], ALU.subtract).then_inc(lb_dve, 1)

            def copy_rows_out(n_used, turned, bias=None):
                dve.wait_ge(ring_used, n_used)
                if turned is not None:
                    dve.wait_ge(rows_turned, turned)
                if bias is None:
                    v.tensor_copy(ada_rows[:], ps[:, 0, :]).then_inc(rows_copied, 1)
                else:
                    v.tensor_tensor(ada_rows[:], ps[:, 0, :], bias, ALU.add).then_inc(rows_copied, 1)

            def add_bias(six):
                dve.wait_ge(rows_turned, six + 1)
                for c in range(4):
                    src = ps[:, 1, P * c:P * (c + 1)].rearrange("p (j r) -> p j r", j=4)[:, :, 0:R]
                    dst = adaT[:, bass.ds(six, 1)].rearrange("p a (j c) r -> p c (a j) r", j=4)[:, c]
                    bias = badaT[:, bass.ds(six, 1), :].rearrange("p a (j c) -> p c (a j)", j=4)[:, c]
                    last = v.tensor_tensor(dst, src, bc(bias, 2, R), ALU.add)
                last.then_inc(ada_ready, 1)

            for six in range(2):
                copy_rows_out(used(KC * six + KC - 1), six if six else None)
                add_bias(six)
            dve.wait_ge(ada_ready, 2)
            dve.wait_ge(x_loaded, 16)

            def seq(ap):
                return bc(ap, len(ap.shape), SS)

            def samp(ap):
                return ap.rearrange("p m (b t) -> p m b t", t=SS)

            for m in range(KC):
                v.tensor_scalar(uT[:, m, 0:TP], uT[:, m, 0:TP], adaT[:, 1, m, 0:1], adaT[:, 0, m, 0:1],
                                ALU.mult, ALU.add)
            us = samp(uT[:, :, TP:T])
            link(v.tensor_tensor(us, us, seq(adaT[:, 1, :, 1:R]), ALU.mult))
            v.tensor_tensor(us, us, seq(adaT[:, 0, :, 1:R]), ALU.add).then_inc(u_ready, 1)

            with dve.Fori(0, 2) as g:
                for c in range(1, SLOTS, 2):
                    if c == 7:
                        copy_rows_out(g * MIX + used(N_MIX + 22), g + 2)
                    dve.wait_ge(ring_used, g * MIX + used(N_MIX + 3 * c + 2))
                    v.tensor_copy(hf_hq[:, bass.ds(g * H + c, 1), :].rearrange("p a t -> p (a t)"),
                                  ps[:, 4 + c % 4, 0:T]).then_inc(evac_dve, 1)
                add_bias(g + 2)

            def evacuate_head(dst, n, bank):
                dve.wait_ge(ring_used, used(n))
                v.tensor_copy(dst, ps[:, bank, 0:T]).then_inc(evac_dve, 1)

            def evacuate_rows(n, slot):
                dve.wait_ge(ring_used, used(n))
                for i, (t0, tn) in enumerate(TILES):
                    last = v.tensor_copy(tok[0:tn, slot + i, 512:1024], ps[0:tn, 4 + i, :])
                last.then_inc(evac_dve, 1)

            N_G = N_MIX + 2 * MIX + 2
            flat = lambda ap: ap.rearrange("p h t -> p (h t)")
            link(v.memset(reset, 1.0))
            r3 = reset.rearrange("p (h t) -> p h t", t=T)
            v.memset(r3[:, :, 0:TP].rearrange("p h (c t) -> p h c t", t=CH)[:, :, :, 0:1], 0.0)
            v.memset(r3[:, :, TP:T].rearrange("p h (c t) -> p h c t", t=SS)[:, :, :, 0:1], 0.0)
            v.memset(abuf, 0.0)
            v.memset(abufs, 0.0)
            dve.wait_ge(lb_act, 1)
            link(v.tensor_scalar(lbt[:, 2, :], lbt[:, 2, :], 1.0, None, ALU.add))
            link(v.reciprocal(lbt[:, 2, :], lbt[:, 2, :]))
            dve.wait_ge(hg_act, 1)
            v.tensor_scalar(qhat, qhat, 1.0, None, ALU.add)
            v.tensor_scalar(t1, t1, 1.0, None, ALU.add)
            link(v.tensor_scalar(lbt[:, 3, :], lbt[:, 2, :], -1.0, 1.0, ALU.mult, ALU.add))
            v.reciprocal(qhat, qhat)
            link(v.reciprocal(t1, t1))
            v.tensor_tensor(hq, hq, qhat, ALU.mult)
            for h in range(H):
                last = v.tensor_scalar(t1[:, h, :], t1[:, h, :], lbt[:, 3, h:h + 1], lbt[:, 2, h:h + 1],
                                       ALU.mult, ALU.add)
            link(last)
            v.tensor_scalar(hf, t1, -1.0, 1.0, ALU.mult, ALU.add).then_inc(hg_dve, 1)
            evacuate_head(hg[:, 1, :], N_G + 3 * 1, 5)
            dve.wait_ge(hg_act, 2)
            for half in range(2):
                last = v.tensor_tensor_scan(flat(bcum[:, 4 * half:4 * half + 4, :]), reset,
                                            flat(t1[:, 4 * half:4 * half + 4, :]), 0.0, ALU.mult, ALU.add)
            link(last)
            bp = bcum[:, :, 0:TP].rearrange("p h (c t) -> p h c t", t=CH)
            bs = bcum[:, :, TP:T].rearrange("p h (c t) -> p h c t", t=SS)
            tp = t1[:, :, 0:TP].rearrange("p h (c t) -> p h c t", t=CH)
            ts = t1[:, :, TP:T].rearrange("p h (c t) -> p h c t", t=SS)
            for h in range(H):
                v.tensor_tensor(tp[:, h], bp[:, h], bc(bp[:, h, :, CH // 2 - 1], 2, CH), ALU.subtract)
                last = v.tensor_tensor(ts[:, h], bs[:, h], bc(bs[:, h, :, SS // 2 - 1], 2, SS), ALU.subtract)
            link(last)
            v.tensor_scalar(t1, t1, 80.0, -80.0, ALU.min, ALU.max).then_inc(hg_dve, 1)
            evacuate_head(hg[:, 3, :], N_G + 3 * 3, 7)
            dve.wait_ge(hg_act, 3)
            dve.wait_ge(hg_dve, 2)
            v.tensor_tensor(qhat, qhat, hq, ALU.mult)
            v.tensor_tensor(khat, khat, hf, ALU.mult).then_inc(hg_dve, 1)
            dve.wait_ge(hg_act, 4)
            dve.wait_ge(hg_dve, 3)
            link(v.tensor_tensor(hq, hq, t1, ALU.mult))
            for h in range(H):
                v.tensor_tensor(tp[:, h], bc(bp[:, h, :, CH - 1], 2, CH), bp[:, h], ALU.subtract)
                last = v.tensor_tensor(ts[:, h], bc(bs[:, h, :, SS - 1], 2, SS), bs[:, h], ALU.subtract)
            last.then_inc(hg_dve, 1)
            evacuate_head(hg[:, 5, :], N_G + 3 * 5, 5)
            copy_rows_out(used(N_MIX + 2 * MIX + 22), 4)
            evacuate_head(hg[:, 7, :], N_G + 3 * 7, 7)
            add_bias(4)
            dve.wait_ge(hg_act, 5)
            v.tensor_tensor(hf, hf, t1, ALU.mult).then_inc(hg_dve, 1)
            dve.wait_ge(hg_act, 6)
            link(v.tensor_scalar(t1, t1, 1.0, None, ALU.add))
            link(v.reciprocal(t1, t1))
            v.tensor_tensor(hg, hg, t1, ALU.mult).then_inc(hg_dve, 1)

            def keep_scores(tt):
                dve.wait_ge(hg_pe, tt + 1)
                for i in range(2):
                    last = v.copy_predicated(abuf[:, tt, 4 * i:4 * i + 4, :], bc(chunkmask[:].bitcast(U32), 1, 4),
                                             ps[:, 2 + i, :].rearrange("p (h t) -> p h t", t=P))
                return last

            last = keep_scores(0)
            last = v.copy_predicated(abufs, bc(incl4[:].bitcast(U32), 1, H),
                                     ps[0:TS, 7, 0:256].rearrange("p (h t) -> p h t", t=TS))
            last.then_inc(hg_dve, 1)
            keep_scores(1).then_inc(hg_dve, 1)
            copy_rows_out(used(N_MIX + 3 * MIX + 22), 5, bg2[:])
            evacuate_rows(N_MIX + 3 * MIX + 23, 3)

            link(v.memset(qpad, 0.0))
            for half in range(2):
                heads = slice(4 * half, 4 * half + 4)
                if half == 1:
                    dve.wait_ge(os_pe, 4)
                for b in range(NSEQ):
                    last = v.tensor_copy(qpad[:, :, b, SS * b:SS * (b + 1)],
                                         hq[:, heads, TP + SS * b:TP + SS * (b + 1)])
                last.then_inc(qpad_ready, 1)

                def state_after(c):
                    dve.wait_ge(u_pe, 8 * half + c + 1)
                    upd = ps[:, 2, :].rearrange("p (h v) -> p h v", v=P)
                    if c == 0:
                        if half == 1:
                            dve.wait_ge(hgo_pe, 2)
                            dve.wait_ge(sprompt_stored, 16)
                        v.tensor_copy(shist[:, 0], upd).then_inc(u_dve, 1)
                    else:
                        dve.wait_ge(u_dve, 8 * half + c)
                        link(v.tensor_tensor(shist[:, c], shist[:, c - 1], bc(dec[:, heads, c], 2, P), ALU.mult))
                        v.tensor_tensor(shist[:, c], shist[:, c], upd, ALU.add).then_inc(u_dve, 1)

                for c in range(8):
                    if c % 2 == 1:
                        evacuate_head(projT[:, 8 * half + c, :], N_SQ + 8 * half + c, 5)
                    state_after(c)
                    if c % 2 == 0:
                        continue
                    k = 4 * half + c // 2
                    dve.wait_ge(os_pe, k + 1)
                    s_new = s0[k % 2]
                    v.tensor_tensor(s_new, s_new, bc(dec[:, k, 8:16], 2, P), ALU.mult).then_inc(us_dve, 1)
                    for i in range(2):
                        dve.wait_ge(us_pe, 2 * k + i + 1)
                        dve.wait_ge(us_dve, 3 * k + 1)
                        part = s_new[:, 4 * i:4 * i + 4, :]
                        v.tensor_tensor(part, part, ps[:, i, :].rearrange("p (b v) -> p b v", v=P), ALU.add
                                        ).then_inc(us_dve, 1)
                dve.wait_ge(os_pe, 4 * (half + 1))
                if half == 1:
                    dve.wait_ge(osr_pe, 1)
                v.tensor_copy(osr, ps[:, 3, 0:P]).then_inc(osr_dve, 1)
                dve.wait_ge(osr_pe, half + 1)
                v.tensor_copy(hout[:, heads, TP:T], ps[:, 3, P:2 * P].rearrange("p (h t) -> p h t", t=TS)
                              ).then_inc(osm_dve, 1)

            dve.wait_ge(hgo_pe, 4)
            for i, (t0, tn) in enumerate(TILES):
                dve.wait_ge(kout_pe, i + 1)
                v.tensor_copy(kstage[0:tn, i, :].rearrange("p (a n) -> p a n", a=2),
                              ps[0:tn, 2 * (i % 2):2 * (i % 2) + 2, :]).then_inc(kout_evac, 1)

            dve.wait_ge(sprompt_stored, 2 * 16)
            zP4 = zP.rearrange("p (g b) h t -> p g b h t", g=NPG)
            for c in range(SLOTS + 1):
                if c == 7:
                    dve.wait_ge(ssample_stored, H * 16)
                    evacuate_rows(N_SV + 2 * 7, 0)
                if c >= 1:
                    dve.wait_ge(zr_pe, c)
                    if c >= 2:
                        dve.wait_ge(zt_pe, c - 1)
                    v.tensor_copy(zrow, ps[:, 7, :]).then_inc(zr_dve, 1)
                if c < SLOTS:
                    dve.wait_ge(ring_used, used(N_SV + 2 * c + 1))
                    v.tensor_copy(keyT[:, :, P:2 * P], ps[:, 2:4, :].rearrange("p a (h s) -> p (a h) s", s=P)
                                  ).then_inc(kT_dve, 1)
                if c >= 1:
                    dve.wait_ge(zt_pe, c)
                    src = ps[:, 7, :].rearrange("p (g h t) -> p g h t", g=NPG, h=H)
                    v.tensor_copy(zP4[:, :, c - 1], src[:, :, :, SS * (c - 1):SS * c]).then_inc(zt_dve, 1)

            dve.wait_ge(hgo_pe, 4)
            for h in range(H + 2):
                if h < H:
                    dve.wait_ge(z_pe, h + 1)
                    if h >= 2:
                        dve.wait_ge(a_ready, h - 1)
                        dve.wait_ge(c_pe, h - 1)
                    x, s, n = zz[h % 2], spl[h % 2], zn[h % 2]
                    v.tensor_scalar(x, ps[:, 2 + h % 2, 0:384], SCALE, biasb[:, h:h + 1], ALU.mult, ALU.add
                                    ).then_inc(z_dve, 1)
                    dve.wait_ge(z_dve, h + 1)
                    v.tensor_tensor(n, x, negmask[:], ALU.add)
                    dve.wait_ge(soft_act, h + 1)
                    link(v.scalar_tensor_tensor(s, x, 0.0, ee[h % 2], ALU.max, ALU.add))
                    v.tensor_tensor(s, s, causal[:], ALU.mult).then_inc(sp_ready, 1)
                if 1 <= h <= H:
                    k = h - 1
                    dve.wait_ge(c_pe, k + 1)
                    dve.wait_ge(sp_ready, k + 1)
                    v.tensor_tensor(zn[k % 2], zn[k % 2], ps[:, 4 + k % 2, 0:384], ALU.subtract).then_inc(d_dve, 1)
                if h >= 2:
                    k = h - 2
                    dve.wait_ge(o_pe, k + 1)
                    v.tensor_copy(mixT[:, H + k, 0:TP], ps[:, 6 + k % 2, 0:TP]).then_inc(o_evac, 1)
                if h == 1:
                    dve.wait_ge(zt_dve, NSEQ)
                    dve.wait_ge(k_stored, 3 * 16)
                    bias = bc(bc(biasb[:], 1, NPG * NSEQ), 3, SS)
                    v.memset(apad, 0.0)
                    v.tensor_scalar(zP, zP, SCALE, None, ALU.mult)
                    dve.wait_ge(ss_pe, 1)
                    link(v.tensor_scalar(zN.rearrange("p h t -> p (h t)"), ps[0:TS, 0, 0:TS * H], SCALE, None,
                                         ALU.mult))
                    v.tensor_tensor(zP, zP, bias, ALU.add)
                    v.tensor_tensor(zN, zN, bc(biasb[0:TS, :], 2, TS), ALU.add).then_inc(ss_dve, 1)
                if h == 2:
                    dve.wait_ge(ss_act, 1)
                    v.scalar_tensor_tensor(sP, zP, 0.0, eP, ALU.max, ALU.add)
                    link(v.scalar_tensor_tensor(sN, zN, 0.0, eN, ALU.max, ALU.add))
                    v.tensor_tensor(zN, zN, bc(neg4[:], 1, H), ALU.add)
                    v.tensor_tensor(sN, sN, bc(strict4[:], 1, H), ALU.mult).then_inc(ss_dve, 1)
                if h == 4:
                    dve.wait_ge(ss_pe, 2)
                    dve.wait_ge(ss_dve, 2)
                    v.tensor_tensor(dP.rearrange("p g h t -> p (g h t)"), zP.rearrange("p g h t -> p (g h t)"),
                                    ps[:, 1, :], ALU.subtract)
                    v.tensor_tensor(dN.rearrange("p h t -> p (h t)"), zN.rearrange("p h t -> p (h t)"),
                                    ps[0:TS, 0, 0:TS * H], ALU.subtract).then_inc(ss_dve, 1)
                if h == 7:
                    dve.wait_ge(ss_pe, 3)
                    v.tensor_copy(orow, ps[:, 0:2, 0:P]).then_inc(ss_dve, 1)
                if h == 9:
                    dve.wait_ge(ss_pe, 4)
                    v.tensor_copy(mixT[:, H:2 * H, TP:T], ps[:, 0, 0:256].rearrange("p (h t) -> p h t", t=TS)
                                  ).then_inc(ss_dve, 1)

            for k in range(2 * H):
                dve.wait_ge(nrs_act, k + 1)
                w = normw[:, k // H:k // H + 1]
                src = (hout if k < H else mixT)[:, k, :]
                ins = v.scalar_tensor_tensor(mixT[:, k, :], src, w, rst[k % 2], ALU.mult, ALU.mult)
                if k < H:
                    link(ins)
                    ins = v.tensor_tensor(mixT[:, k, :], mixT[:, k, :], hg[:, k, :], ALU.mult)
                ins.then_inc(nm_dve, 1)

            dve.wait_ge(xa_ready, 1)
            for m in range(KC):
                dve.wait_ge(ring_used, used(N_WO + m))
                o = ps[:, 4 + m % 4, :]
                rs = rT[:, m, TP:T].rearrange("p (b t) -> p b t", t=SS)
                link(v.tensor_tensor(rs, o[:, TP:T].rearrange("p (b t) -> p b t", t=SS), seq(adaT[:, 2, m, 1:R]),
                                     ALU.mult))
                v.scalar_tensor_tensor(rT[:, m, 0:TP], o[:, 0:TP], adaT[:, 2, m, 0:1], xa[:, m, 0:TP],
                                       ALU.mult, ALU.add)
                v.tensor_tensor(rT[:, m, TP:T], rT[:, m, TP:T], xa[:, m, TP:T], ALU.add).then_inc(wo_dve, 1)
            dve.wait_ge(st_pe, KC)
            dve.wait_ge(wo_act, KC)
            v.tensor_scalar(lt1, ps[:, 3, 0:T], 1.0 / D, None, ALU.mult)
            link(v.tensor_scalar(mu, ps[:, 2, 0:T], 1.0 / D, None, ALU.mult))
            link(v.tensor_tensor(rstd, mu, mu, ALU.mult))
            link(v.tensor_tensor(lt1, lt1, rstd, ALU.subtract))
            v.tensor_scalar(lt1, lt1, 0.0, None, ALU.max).then_inc(ln_dve, 1)
            link(v.tensor_tensor(rT, rT, bc(mu, 1, KC), ALU.subtract))
            dve.wait_ge(rstd_act, 1)
            for q in range(4):
                part = rT[:, 4 * q:4 * q + 4, :]
                v.tensor_tensor(part, part, bc(rstd, 1, 4), ALU.mult).then_inc(ln_dve, 1)
            for m in range(KC):
                dve.wait_ge(x1_act, m + 1)
                us = u2T[:, m, TP:T].rearrange("p (b t) -> p b t", t=SS)
                xs = rT[:, m, TP:T].rearrange("p (b t) -> p b t", t=SS)
                link(v.tensor_tensor(us, xs, seq(adaT[:, 4, m, 1:R]), ALU.mult))
                v.tensor_scalar(u2T[:, m, 0:TP], rT[:, m, 0:TP], adaT[:, 4, m, 0:1], adaT[:, 3, m, 0:1],
                                ALU.mult, ALU.add)
                v.tensor_tensor(us, us, seq(adaT[:, 3, m, 1:R]), ALU.add).then_inc(u2_dve, 1)

            v.memset(lg, 0.0)
            v.memset(vm, 0.0)
            link(v.memset(onesNE, 1.0))
            v.memset(vm[:, 0:2], 1.0)
            link(v.memset(vm[0:32, 2:3], 1.0))
            dve.wait_ge(rt_pe, 2)
            v.tensor_tensor(lg[:, 0:2, :], ps[:, 5, 0:128].rearrange("p (i n) -> p i n", n=64)[:, :, 0:NL],
                            bc(br[:], 1, 2), ALU.add)
            link(v.tensor_tensor(lg[0:32, 2, :], ps[0:32, 5, 128:128 + NL], br[0:32, :], ALU.add))
            gl = lg[:, :, 0:NG]
            el = lg[:, :, NG:NL].rearrange("p i (g e) -> p i g e", e=NEG)

            def first_max(out, x, m, n):
                link(v.tensor_tensor(out, x, bc(m, 2, n), ALU.is_equal))
                link(v.tensor_tensor(out, out, bc(rev4[:, 0:n], 1, 3), ALU.mult))
                link(v.tensor_reduce(tmp3, out, AX, ALU.max))
                link(v.tensor_tensor(out, out, bc(tmp3, 2, n), ALU.is_equal))

            link(v.tensor_reduce(gmax, gl, AX, ALU.max))
            first_max(gone, gl, gmax, NG)
            v.tensor_tensor(gexp, gl, bc(gmax, 2, NG), ALU.subtract)
            link(v.tensor_tensor(pick, el, bc(gone, 3, NEG), ALU.mult))
            link(v.tensor_reduce(esel, pick.rearrange("p i g e -> p i e g"), AX, ALU.add))
            link(v.tensor_reduce(m1, esel, AX, ALU.max))
            first_max(e1, esel, m1, NEG)
            link(v.tensor_scalar(cand, e1, -3.0e38, None, ALU.mult))
            link(v.tensor_tensor(cand, cand, esel, ALU.add))
            link(v.tensor_reduce(m2, cand, AX, ALU.max))
            first_max(e2, cand, m2, NEG)
            link(v.tensor_tensor(m2, m2, m1, ALU.subtract))
            link(v.tensor_tensor(gone, gone, bc(vm, 2, NG), ALU.mult))
            for k, e in enumerate((e1, e2)):
                for i in range(3):
                    last = v.tensor_tensor(oneh[k][:, i], bc(gone[:, i], 2, NEG), bc(e[:, i], 1, NG), ALU.mult)
            link(last)
            oh = [oneh[k].rearrange("p i g e -> p i (g e)") for k in range(2)]
            v.tensor_tensor(both, oh[0], oh[1], ALU.add).then_inc(rt_dve, 1)

            dve.wait_ge(rt_pe, 3)
            link(v.tensor_copy(cnt, ps[:, 3, 0:NE]))
            link(v.tensor_scalar(nb, cnt, 0.0, None, ALU.is_gt))
            for j in range(1, (T + B - 1) // B):
                link(v.scalar_tensor_tensor(nb, cnt, float(B * j), nb, ALU.is_gt, ALU.add))
            link(v.tensor_tensor_scan(cum, onesNE, nb, 0.0, ALU.mult, ALU.add))
            v.tensor_tensor(base, cum, nb, ALU.subtract)
            link(v.tensor_tensor(ecmp, bc(cum[0:1, :], 1, NB1), bc(iotab[0:1, 0:NB1], 2, NE), ALU.is_le))
            link(v.tensor_reduce(eid, ecmp, AX, ALU.add))
            link(v.tensor_scalar(eid, eid, NE - 1.0, None, ALU.min))
            v.tensor_copy(plan[0:1, 0:NB1], eid)
            v.tensor_copy(plan[0:1, NB1:NB1 + 1], cum[0:1, NE - 1:NE]).then_inc(plan_ready, 1)
            link(v.tensor_copy(rank, ps[:, 2, 0:3 * NE].rearrange("p (i e) -> p i e", e=NE)))
            v.memset(gslot[:], 0.0)
            for k in range(2):
                link(v.tensor_tensor(tmp32, oh[k], rank, ALU.mult))
                link(v.tensor_reduce(rk, tmp32, AX, ALU.add))
                link(v.tensor_scalar(blkr, rk, float(B), None, ALU.is_ge))
                for j in range(2, (T + B - 1) // B):
                    link(v.scalar_tensor_tensor(blkr, rk, float(B * j), blkr, ALU.is_ge, ALU.add))
                link(v.scalar_tensor_tensor(sl, blkr, -float(B), rk, ALU.mult, ALU.add))
                link(v.tensor_tensor(tmp32, oh[k], bc(base, 1, 3), ALU.mult))
                link(v.tensor_reduce(blk, tmp32, AX, ALU.add))
                link(v.tensor_tensor(blk, blk, blkr, ALU.add))
                link(v.scalar_tensor_tensor(gslot[:, k, :], blk, float(B), sl, ALU.mult, ALU.add))
                if k == 0:
                    link(v.tensor_tensor(tokid[:], tokid[:], vm, ALU.mult))
                for i in range(3):
                    v.tensor_scalar(rsel[k][:, i, :], iotab[:], sl[:, i:i + 1], None, ALU.is_equal)
                    last = v.tensor_scalar(bsel[k][:, i, :], iotab[:, 0:NB1], blk[:, i:i + 1], tokid[:, i:i + 1],
                                           ALU.is_equal, ALU.mult)
                if k == 0:
                    link(last)
            last.then_inc(rt_dve, 1)
            v.tensor_copy(rowidx[:], gslot[:]).then_inc(rt_dve, 1)
            dve.wait_ge(rt_pe, 4)
            v.tensor_copy(idxs[:], ps[0:B, 4, 0:NB1]).then_inc(plan_ready, 1)
            dve.wait_ge(rt_act, 2)
            link(v.tensor_reduce(gw, gexp, AX, ALU.add))
            link(v.tensor_scalar(tmp3, m2, 1.0, None, ALU.add))
            link(v.tensor_tensor(gw, gw, tmp3, ALU.mult))
            link(v.reciprocal(gate2[:, 0, :], gw))
            link(v.tensor_tensor(gate2[:, 1, :], gate2[:, 0, :], m2, ALU.mult))

            dve.wait_ge(plan_ready, 2)
            nblocks = dve.value_load(plan[0:1, NB1:NB1 + 1], min_val=0, max_val=NBLK)
            with dve.Fori(0, NBLK) as i:
                with dve.If(i < nblocks):
                    dve.wait_ge(sil_act, i + 1)
                    dve.wait_ge(moe_used, i * MOE_CHUNKS + (MOE_CHUNKS + 8))
                    dve.wait_ge(hT_pe, i + 1)
                    v.tensor_tensor(hid, hsil, ps[:, 3, 0:256], ALU.mult).then_inc(hid_dve, 1)
                    dve.wait_ge(hT_pe, i + 2)
                    v.tensor_copy(hT, ps[:, 4, 0:256].rearrange("p (c s) -> p c s", s=P)).then_inc(hT_dve, 1)
                    dve.wait_ge(moe_used, i * MOE_CHUNKS + 2 * MOE_CHUNKS)
                    dve.wait_ge(y_stored, i * 32 + 32)
                    v.tensor_copy(yout[:, 512:1024], ps[:, 6, :]).then_inc(y_evac, 1)

            dve.wait_ge(late_loaded, 16)
            dve.wait_ge(g2_act, 4)
            for i, (t0, tn) in enumerate(TILES):
                w = yb[i][0:tn, :]
                dve.wait_ge(fin_act, 2 * i + 1)
                link(v.scalar_tensor_tensor(w, w, gate2[0:tn, 1, i:i + 1], ya[i][0:tn, :], ALU.mult, ALU.add))
                link(v.tensor_tensor(w, w, (g2p if i < 2 else g2s)[0:tn, :], ALU.mult))
                link(v.tensor_tensor(w, w, xres[0:tn, i, :], ALU.add))
                for q in range(4):
                    last = v.bn_stats(bnst[0:tn, q, :], w[:, 512 * q:512 * (q + 1)])
                link(last)
                v.bn_aggr(bnag[0:tn, :], bnst[0:tn, :, :].rearrange("p q s -> p (q s)")).then_inc(fin_dve, 1)
                dve.wait_ge(fin_act, 2 * i + 2)
                link(v.tensor_scalar(w, w, bnag[0:tn, 0:1], rs1[0:tn, :], ALU.subtract, ALU.mult))
                link(v.tensor_tensor(w, w, ln2b[0:tn, 0, :], ALU.mult))
                v.tensor_tensor(w, w, ln2b[0:tn, 1, :], ALU.add).then_inc(fin_dve, 1)


def kernel(**inputs):
    import numpy as np
    import concourse.bacc as bacc
    from concourse.bass_utils import run_bass_kernel_spmd

    a = {k: np.asarray(x) for k, x in inputs.items()}

    def feature_major(x):
        return np.ascontiguousarray(x.reshape(-1, P, KC).transpose(1, 2, 0))

    w_ada = a["w_ada"][0].reshape(P, KC, 6, D)
    perm = w_ada.reshape(P, KC, 6, P, KC).transpose(2, 1, 0, 4, 3).reshape(6, KC, P, D)
    ada = np.concatenate([perm[:5], w_ada[:, :, 5].transpose(1, 0, 2)[None]])
    b_ada = a["b_ada"][0].reshape(6, D)
    w_in = a["w_in"][0].reshape(P, KC, 7, 1024)
    groups = []
    for n, g in enumerate((1, 0, 3, 2, 4, 5, 6)):
        w = w_in[:, :, g]
        if n in (3, 6):
            w = w.reshape(P, 4, 4, 2, 512).transpose(3, 1, 0, 2, 4)
        else:
            w = w.reshape(P, KC, H, P).transpose(2, 0, 1, 3)
        groups.append(w.reshape(SLOTS, P, D))
    w_o = a["w_o"][0].reshape(KC, P, P, KC).transpose(3, 1, 0, 2).reshape(2, SLOTS, P, D)
    arrays = {
        "xT": feature_major(np.concatenate([a["x_prompt"].reshape(-1, D), a["x_sample"].reshape(-1, D)])),
        "cT": feature_major(np.concatenate([a["c_prompt"], a["c_sample"]])),
        "w_ada": ada,
        "b_adaT": b_ada[:5].reshape(5, P, KC).transpose(1, 0, 2),
        "b_g2": b_ada[5].reshape(4, 512),
        "w_in": np.stack(groups),
        "w_o": w_o,
        "w_r": np.concatenate([a["w_gr"][0], a["w_er"][0].reshape(D, NE)], axis=1).reshape(P, KC, NL),
        "b_r": np.concatenate([a["b_gr"][0], a["b_er"][0].reshape(NE)]),
        "lb_logits": a["hg_lb_logits"].reshape(2, H, P).transpose(2, 0, 1),
        "norms": np.stack([a["hg_norm"][0], a["sb_norm"][0]], axis=1),
        "sb_bias": a["sb_bias"][0],
        "ln1": np.stack([a["ln1_g"][0], a["ln1_b"][0]]).reshape(2, P, KC).transpose(1, 0, 2),
        "ln2": np.stack([a["ln2_g"][0], a["ln2_b"][0]]),
        "cache_k": a["cache_k"][0].reshape(NPHYS, PAGE, 1024),
        "cache_v": a["cache_v"][0].reshape(NPHYS, PAGE, 1024),
        "page_table": a["page_table"].reshape(1, NSEQ * NPG),
        "state": a["state_hgrn"][0],
        "w_gate": a["w_gate"][0], "w_up": a["w_up"][0], "w_down": a["w_down"][0],
    }
    arrays = {k: np.ascontiguousarray(x) for k, x in arrays.items()}
    outs = {"y_p": (TP, D), "y_s": (TS, D), "k_p": (TP, 1024), "v_p": (TP, 1024), "s_p": (H, P, P),
            "k_s": (TS, 1024), "v_s": (TS, 1024), "s_s": (NSEQ, H, P, P)}
    nc = bacc.Bacc("TRN2", target_bir_lowering=False, num_devices=1)
    aps = {k: nc.dram_tensor(k, x.shape, mybir.dt.from_np(x.dtype), kind="ExternalInput").ap()
           for k, x in arrays.items()}
    aps |= {k: nc.dram_tensor(k, s, F32, kind="ExternalOutput").ap() for k, s in outs.items()}
    aps["u2_rows"] = nc.dram_tensor("u2_rows", (T, D), F32, kind="Internal").ap()
    aps["y_rows"] = nc.dram_tensor("y_rows", (NBLK * B, D), F32, kind="Internal").ap()
    layer(nc, **aps)
    r = run_bass_kernel_spmd(nc, [arrays], core_ids=[0]).results[0]
    return (r["y_p"].reshape(1, TP, D), r["y_s"].reshape(NSEQ, SS, D),
            r["k_p"].reshape(1, 1, TP, H, P), r["v_p"].reshape(1, 1, TP, H, P), r["s_p"].reshape(1, 1, H, P, P),
            r["k_s"].reshape(1, NSEQ, SS, H, P), r["v_s"].reshape(1, NSEQ, SS, H, P),
            r["s_s"].reshape(1, NSEQ, H, P, P))
```

```python
from contextlib import ExitStack

import concourse.bass as bass
from concourse import mybir

F32 = mybir.dt.float32
I32 = mybir.dt.int32
U32 = mybir.dt.uint32
ACT = mybir.ActivationFunctionType
ALU = mybir.AluOpType
AX = mybir.AxisListType.X

P = 128
D = 2048
KC = D // P
TP, NSEQ, SS = 256, 8, 4
TS = NSEQ * SS
T = TP + TS
H = 8
R = 1 + NSEQ
PAST, PAGE = 256, 128
NPG = PAST // PAGE
NPHYS = 20
SCALE = 128 ** -0.5
ALPHA = 2.0 ** 0.25
LN_EPS, RMS_EPS = 1e-5, 1e-6
NG, NEG, NE, FF = 4, 8, 32, 512
NL = NG + NE
B = 64
NBLK = NE + (2 * T) // B - 1
CH = 32
SLOTS = 8
MOE_CHUNKS = 12
TILES = [(0, 128), (128, 128), (256, 32)]
NEG_BIG = -1.0e30


def layer(nc, xT, cT, w_ada, b_adaT, b_g2, w_in, w_o, w_r, b_r, lb_logits, norms, sb_bias,
          ln1, ln2, cache_k, cache_v, page_table, state, w_gate, w_up, w_down,
          y_p, y_s, k_p, v_p, s_p, k_s, v_s, s_s, u2_rows):
    with ExitStack() as ctx:
        def sb(name, shape, dt=F32):
            return ctx.enter_context(nc.sbuf_tensor(name, shape, dt))

        def sem(name):
            return ctx.enter_context(nc.semaphore(name))

        ps = ctx.enter_context(nc.psum_tensor("ps", [P, 8, 512], F32))
        ring = sb("ring", [P, SLOTS, D])

        ident = sb("ident", [P, P])
        tri = sb("tri", [P, P])
        ones = sb("ones", [P, P])
        causal = sb("causal", [P, 384])
        negmask = sb("negmask", [P, 384])
        chunkmask = sb("chunkmask", [P, P])
        strict4 = sb("strict4", [TS, TS])
        neg4 = sb("neg4", [TS, TS])
        incl4 = sb("incl4", [TS, TS])
        seqmask = sb("seqmask", [TS, NSEQ])
        rowsel = sb("rowsel", [P, P + TS])
        silu_c = sb("silu_c", [P, KC, 32])
        ctmp = sb("ctmp", [P, KC * R])
        cin = sb("cin", [P, KC * R])
        adaT = sb("adaT", [P, 5, KC, R])
        badaT = sb("badaT", [P, 5, KC])
        ada_rows = sb("ada_rows", [P, 512])
        bg2 = sb("bg2", [P, 512])
        lbt = sb("lbt", [P, 4, H])
        normw = sb("normw", [P, 2])
        biasb = sb("biasb", [P, H])
        ln1t = sb("ln1t", [P, 2, KC])
        epsr = sb("epsr", [P, 2])
        wr = sb("wr", [P, KC, NL])
        br = sb("br", [P, NL])
        pages = sb("pages", [1, NSEQ * NPG], I32)

        ARENA = 31488
        arena = sb("arena", [P, ARENA])

        def area(at, *shape, parts=P):
            n = 1
            for s in shape:
                n *= s
            assert at + n <= ARENA, (at, shape)
            v = arena[0:parts, at:at + n]
            if len(shape) == 1:
                return v
            names = "abcde"[:len(shape)]
            return v.rearrange(f"p ({' '.join(names)}) -> p {' '.join(names)}",
                               **{k: s for k, s in zip(names, shape)})

        uT = area(0, KC, T)
        mixT = uT
        SQ = 4608
        projT = area(SQ, 5 * H, T)
        sqT, skT = projT[:, 0:H, :], projT[:, H:2 * H, :]
        hf, hq, hg = (projT[:, (2 + i) * H:(3 + i) * H, :] for i in range(3))
        hf_hq = projT[:, 2 * H:4 * H, :]
        hout = hf
        TOK = SQ + 5 * H * T
        tok = area(TOK, 6, 1024)
        TMP = TOK + 6 * 1024
        kstage = area(TMP + 5120, 3, 1024)
        soft = [[area(at + 384 * i, 384) for i in range(5)] for at in (SQ + 3 * H * T, 0)]
        zz, ee, spl, zn, aa = ([s[i] for s in soft] for i in range(5))
        keyT = area(TMP, H, PAST)
        zrow = area(TMP + 2048, 512)
        apad = area(TMP, NPG, NSEQ, H, TS)
        zP = area(TMP + 4096, NPG * NSEQ, H, SS)
        eP = area(TMP + 4608, NPG * NSEQ, H, SS)
        sP = area(TMP + 5120, NPG * NSEQ, H, SS)
        dP = area(TMP + 5632, NPG * NSEQ, H, SS)
        zN = area(TMP + 6144, H, TS, parts=TS)
        eN = area(TMP + 6400, H, TS, parts=TS)
        sN = area(TMP + 6656, H, TS, parts=TS)
        dN = area(TMP + 6912, H, TS, parts=TS)
        aN = area(TMP + 7168, H, TS, parts=TS)
        orow = area(TMP + 7424, 2, P)
        qhat = area(SQ, H, T)
        khat = area(SQ + H * T, H, T)
        bcum = area(TMP, H, T)
        t1 = area(TMP + 2304, H, T)
        shist = area(TMP, 8, 4, P)
        kdts = area(TMP + 4096, 4, P, parts=TS)
        abuf = area(TMP + 4608, 2, H, P)
        abufs = area(TMP + 6656, H, TS, parts=TS)
        dec = area(TMP + 6912, H, 16)
        reset = area(TMP + 7040, 4 * T)
        kdt = area(TMP + 7040, 2, 4, P)
        osr = area(TMP + 8064, P)
        vblk = area(TMP + 8192, NSEQ, P, parts=TS)
        s0 = [area(TOK + 1024 * i, NSEQ, P) for i in range(2)]
        qpad = area(TOK + 2048, 4, NSEQ, TS)
        sqo = [area(TMP + 2304 * i, H, T) for i in range(2)]
        rst = [area(TMP + 2304 * (2 + i), H, T) for i in range(2)]
        xa = area(4608, KC, T)
        rT = area(9216, KC, T)
        r2 = [area(13824 + T * i, T) for i in range(4)]
        mu = area(14976, T)
        rstd = area(15264, T)
        lt1 = area(15552, T)
        u2T = area(4608, KC, T)
        urow = [area(16384 + 2048 * i, D) for i in range(3)]
        RT = 28700
        lgT = area(15840, T, parts=NL)
        mslot = [area(0 + D * i, D) for i in range(4)]
        xres = area(22528, 3, D)
        xg = area(8192, D, parts=B)
        xgT = area(10240, KC, B)
        hid = area(11264, 256)
        hsil = area(11520, 256)
        hT = area(11776, 2, P)
        yout = area(12032, 1024)
        g2p = area(13056, D)
        g2s = area(15104, D)
        moe_out = [area(17152, D), area(19200, D), area(8192, D)]
        sum_s = area(28700, 512)
        where = area(21248, 4, T)
        spread = area(30748, T)
        spread1 = area(31036, T)
        diag = area(11264, 4, 3, P)
        ln2b = ring[:, 0:2, :]

        slot_loaded = [sem(f"slot_loaded{i}") for i in range(SLOTS)]
        moe_loaded = [sem(f"moe_loaded{i}") for i in range(MOE_CHUNKS)]
        ring_used = sem("ring_used")
        moe_used = sem("moe_used")
        (x_loaded, c_loaded, small_loaded, late_loaded, pages_loaded, xa_loaded, k_stored, v_stored, sprompt_stored,
         ssample_stored, u2_stored, gathered, spec_loaded, out_stored) = (sem(n) for n in (
             "x_loaded", "c_loaded", "small_loaded", "late_loaded", "pages_loaded", "xa_loaded", "k_stored", "v_stored",
             "sprompt_stored", "ssample_stored", "u2_stored", "gathered", "spec_loaded", "out_stored"))
        s0_loaded = [sem(f"s0_loaded{i}") for i in range(2)]
        pool_step, dve_step, act_step = sem("pool_step"), sem("dve_step"), sem("act_step")
        consts_ready, expc_ready, silu_c_ready = sem("consts_ready"), sem("expc_ready"), sem("silu_c_ready")
        rows_copied, rows_turned, ada_ready = sem("rows_copied"), sem("rows_turned"), sem("ada_ready")
        u_ready, evac_act, evac_dve = sem("u_ready"), sem("evac_act"), sem("evac_dve")
        kout_pe, kout_evac = sem("kout_pe"), sem("kout_evac")
        (z_pe, z_dve, soft_act, sp_ready, c_pe, d_dve, a_ready, o_pe, o_evac) = (sem(n) for n in (
            "z_pe", "z_dve", "soft_act", "sp_ready", "c_pe", "d_dve", "a_ready", "o_pe", "o_evac"))
        kT_pe, kT_act, kT_dve, zr_pe, zr_dve, zt_pe, zt_dve = (
            sem(n) for n in ("kT_pe", "kT_act", "kT_dve", "zr_pe", "zr_dve", "zt_pe", "zt_dve"))
        ss_pe, ss_dve, ss_act = sem("ss_pe"), sem("ss_dve"), sem("ss_act")
        hg_pe, hg_dve, hg_act, vblk_ready, lb_dve, lb_act = (
            sem(n) for n in ("hg_pe", "hg_dve", "hg_act", "vblk_ready", "lb_dve", "lb_act"))
        kd_pe, kd_act, u_pe, u_dve = sem("kd_pe"), sem("kd_act"), sem("u_pe"), sem("u_dve")
        us_pe, us_dve, os_pe = sem("us_pe"), sem("us_dve"), sem("os_pe")
        qpad_ready, osr_dve, osr_pe, osm_dve = (sem(n) for n in ("qpad_ready", "osr_dve", "osr_pe", "osm_dve"))
        hgo_pe, hgo_act = sem("hgo_pe"), sem("hgo_act")
        nsq_pool, nsq_act, nm_pe, nln_act, nrs_act, nm_dve = (
            sem(n) for n in ("nsq_pool", "nsq_act", "nm_pe", "nln_act", "nrs_act", "nm_dve"))
        xa_ready, wo_dve, wo_act, st_pe = sem("xa_ready"), sem("wo_dve"), sem("wo_act"), sem("st_pe")
        ln_dve, rstd_act, x1_act, u2_dve = sem("ln_dve"), sem("rstd_act"), sem("x1_act"), sem("u2_dve")
        rt_pe, rt_dve, rt_act, tt_pe, tt_act = (sem(n) for n in ("rt_pe", "rt_dve", "rt_act", "tt_pe", "tt_act"))
        plan_ready, idx_ready = sem("plan_ready"), sem("idx_ready")
        x_turned, x_copied = sem("x_turned"), sem("x_copied")
        sil_act, hid_dve, hT_pe, hT_dve, y_evac = (sem(n) for n in ("sil_act", "hid_dve", "hT_pe", "hT_dve", "y_evac"))
        g2_pe, g2_act = sem("g2_pe"), sem("g2_act")
        diag_ready, where_pe, spread_step, spread_ready, comb_pe, sum_dve = (
            sem(n) for n in ("diag_ready", "where_pe", "spread_step", "spread_ready", "comb_pe", "sum_dve"))
        sum_s_act, out_s_pool, ln_pool = sem("sum_s_act"), sem("out_s_pool"), sem("ln_pool")
        wait_carrier = sem("wait_carrier")
        var_dve, fin_dve, fin_act, norm_act, fin_pool = (
            sem(n) for n in ("var_dve", "fin_dve", "fin_act", "norm_act", "fin_pool"))

        def rta(at, *shape, parts=P):
            return area(RT + at, *shape, parts=parts)
        lg = rta(0, 3, NL)
        vm = rta(108, 3)
        gmax = rta(111, 3)
        gone = rta(114, 3, NG)
        gexp = rta(126, 3, NG)
        gw = rta(138, 3)
        pick = rta(141, 3, NG, NEG)
        esel = rta(237, 3, NEG)
        e1 = rta(261, 3, NEG)
        e2 = rta(285, 3, NEG)
        m1 = rta(309, 3)
        m2 = rta(312, 3)
        cand = rta(315, 3, NEG)
        oneh = [rta(339 + 96 * k, 3, NG, NEG) for k in range(2)]
        both = rta(531, 3, NE)
        rank = rta(627, 3, NE)
        cnt = rta(723, NE)
        nb = rta(755, NE)
        cum = rta(787, NE)
        base = rta(819, NE)
        tmp32 = rta(851, 3, NE)
        rk = rta(947, 3)
        blkr = rta(950, 3)
        sl = rta(953, 3)
        blk = rta(956, 3)
        tmp3 = rta(959, 3)
        onesNE = rta(962, NE)
        rsel = [rta(994 + 192 * k, 3, B) for k in range(2)]
        NB1 = NBLK + 1
        bsel = [rta(1378 + 123 * k, 3, NB1) for k in range(2)]
        eid = rta(1624, NB1, parts=1)
        ecmp = area(13824, NB1, NE, parts=1)
        gate2 = sb("gate2", [P, 2, 3])
        tokid = sb("tokid", [P, 3])
        iotab = sb("iotab", [P, B])
        rev4 = sb("rev4", [P, NEG])
        slotid = sb("slotid", [P, 2])
        shift = sb("shift", [P, 3])
        gslot = sb("gslot", [P, 2, 3])
        bnst = sb("bnst", [P, 4, 6])
        bnag = sb("bnag", [P, 3, 2])
        rs1 = sb("rs1", [P, 3])
        plan = sb("plan", [1, NB1 + 1], I32)
        idxs = sb("idxs", [B, NB1], I32)
        idx1 = sb("idx1", [B, 1], I32)

        block = ctx.enter_context(nc.Block())

        def bc(ap, at, n):
            v = ap.unsqueeze(at)
            return v.to_broadcast([*v.shape[:at], n, *v.shape[at + 1:]])

        N_MIX, N_SQ, N_SV, N_V, N_WO = 2 * KC, 2 * KC + 96, 2 * KC + 112, 2 * KC + 128, 2 * KC + 136
        MIX = 3 * SLOTS

        def used(n):
            return SLOTS + n + 1

        def loaded(n):
            def pages_of(m):
                return N_V <= m < N_WO or (N_SV <= m < N_V and (m - N_SV) % 2 == 1)
            return 16 * sum(2 if pages_of(m) else 1 for m in range(n % SLOTS, n + 1, SLOTS))

        @block.sync
        def _(sp):
            def put(n_wait, slot, src):
                sp.wait_ge(ring_used, n_wait)
                sp.dma_start(ring[:, slot, :], src).then_inc(slot_loaded[slot], 16)

            sp.dma_start(cin[:], cT.rearrange("p m r -> p (m r)")).then_inc(c_loaded, 16)
            sp.dma_start(pages[:], page_table[:]).then_inc(pages_loaded, 16)
            with sp.Fori(0, 2) as g:
                for t in range(KC):
                    put(g * KC + (t + 1), t % SLOTS, w_ada[bass.ds(g, 1), t].rearrange("g p n -> p (g n)"))
            with sp.Fori(0, 4) as g:
                for c in range(SLOTS):
                    for t in (2 * c, 2 * c + 1):
                        k = 3 * c + t % 2
                        put(g * MIX + (N_MIX + k + 1), k % SLOTS,
                            w_ada[bass.ds(g + 2, 1), t].rearrange("g p n -> p (g n)"))
                    k = 3 * c + 2
                    put(g * MIX + (N_MIX + k + 1), k % SLOTS, w_in[bass.ds(g, 1), c].rearrange("g p n -> p (g n)"))
            with sp.Fori(0, 2) as g:
                for c in range(SLOTS):
                    put(g * SLOTS + (N_SQ + c + 1), c, w_in[bass.ds(g + 4, 1), c].rearrange("g p n -> p (g n)"))
            sp.wait_ge(pages_loaded, 16)

            def put_pages(n, b, cache):
                sp.wait_ge(ring_used, n + 1)
                for pg in range(NPG):
                    i = b * NPG + pg
                    page = sp.value_load(pages[0:1, i:i + 1], min_val=0, max_val=NPHYS - 1)
                    sp.dma_start(ring[:, n % SLOTS, pg * 1024:(pg + 1) * 1024],
                                 cache[bass.ds(page, 1)].rearrange("g p n -> p (g n)")
                                 ).then_inc(slot_loaded[n % SLOTS], 16)

            for c in range(SLOTS):
                put(N_SV + 2 * c + 1, 2 * c % SLOTS, w_in[6, c])
                put_pages(N_SV + 2 * c + 1, c, cache_k)
            for b in range(NSEQ):
                put_pages(N_V + b, b, cache_v)
            with sp.Fori(0, 2) as g:
                for c in range(SLOTS):
                    put(g * SLOTS + (N_WO + c + 1), c, w_o[bass.ds(g, 1), c].rearrange("g p n -> p (g n)"))
            def put_expert(e, c, signal):
                dst = ring[:, c, :] if c < SLOTS else mslot[c - SLOTS]
                if c < 8:
                    w, q = (w_gate, w_up)[c // 4], c % 4
                    src = w[bass.ds(e, 1)].rearrange("e (p t) n -> p (e t) n", p=P)[:, 4 * q:4 * q + 4, :]
                    dst = dst.rearrange("p (t n) -> p t n", t=4)
                else:
                    q = c - 8
                    src = w_down[bass.ds(e, 1)].rearrange("e f n -> (e f) n")[P * q:P * (q + 1), :]
                sp.dma_start(dst, src).then_inc(signal, 16)

            for c in range(MOE_CHUNKS):
                if c < SLOTS:
                    sp.wait_ge(ring_used, used(N_WO + 8 + c))
                if c == SLOTS + 2:
                    sp.wait_ge(tt_act, 12)
                put_expert(0, c, spec_loaded)
            sp.wait_ge(plan_ready, 1)
            nblocks = sp.value_load(plan[0:1, NB1:NB1 + 1], min_val=0, max_val=NBLK)
            first = sp.value_load(plan[0:1, 0:1], min_val=0, max_val=NE - 1)
            sp.wait_ge(spec_loaded, MOE_CHUNKS * 16)
            with sp.If(first < 1):
                for c in range(MOE_CHUNKS):
                    sp.sem_inc(moe_loaded[c], 16)
            with sp.If(first > 0):
                for c in range(MOE_CHUNKS):
                    put_expert(first, c, moe_loaded[c])
            with sp.Fori(1, NBLK) as i:
                with sp.If(i < nblocks):
                    e = sp.value_load(plan[0:1, bass.ds(i, 1)], min_val=0, max_val=NE - 1)
                    for c in range(MOE_CHUNKS):
                        sp.wait_ge(moe_used, i * MOE_CHUNKS + (c + 1))
                        put_expert(e, c, moe_loaded[c])
            sp.wait_ge(k_stored, 3 * 16)
            sp.wait_ge(v_stored, 3 * 16)
            sp.wait_ge(sprompt_stored, 2 * 16)
            sp.wait_ge(ssample_stored, H * 16)
            sp.wait_ge(u2_stored, 3 * 16)
            sp.wait_ge(out_stored, 3 * 16)

        @block.gpsimd
        def _(pool):
            count = [0]

            def link(ins):
                count[0] += 1
                ins.then_inc(pool_step, 1)
                pool.wait_ge(pool_step, count[0])

            def keep(view, pattern, base_, cm, fill, op=ALU.is_ge):
                link(nc.gpsimd.affine_select(out=view, in_=view, pattern=pattern, compare_op=op, fill=fill,
                                             base=base_, channel_multiplier=cm))

            pool.dma_start(uT, xT[:]).then_inc(x_loaded, 16)
            pool.dma_start(badaT[:], b_adaT[:]).then_inc(small_loaded, 16)
            pool.dma_start(lbt[:, 0:2, :], lb_logits[:]).then_inc(small_loaded, 16)
            pool.dma_start(normw[:], norms[:]).then_inc(small_loaded, 16)
            pool.dma_start(biasb[:], sb_bias.partition_broadcast(P)).then_inc(small_loaded, 16)
            pool.dma_start(ln1t[:], ln1[:]).then_inc(small_loaded, 16)
            pool.dma_start(wr[:], w_r[:]).then_inc(small_loaded, 16)
            pool.dma_start(br[:], b_r.partition_broadcast(P)).then_inc(small_loaded, 16)
            for j in range(4):
                pool.dma_start(bg2[32 * j:32 * j + 32, :], b_g2[j].partition_broadcast(32)).then_inc(small_loaded, 16)

            g = nc.gpsimd
            g.memset(ones[:], 1.0)
            g.memset(ident[:], 0.0)
            g.memset(tri[:], 1.0)
            g.memset(causal[:], 1.0)
            g.memset(negmask[:], 0.0)
            g.memset(chunkmask[:], 1.0)
            g.memset(strict4[:], 1.0)
            g.memset(incl4[:], 1.0)
            g.memset(neg4[:], 0.0)
            g.memset(seqmask[:], 1.0)
            g.memset(rowsel[:], 0.0)
            g.iota(tokid[:], [[P, 3]], base=0, channel_multiplier=1, allow_small_or_imprecise_dtypes=True)
            g.iota(iotab[:], [[1, B]], base=0, channel_multiplier=0, allow_small_or_imprecise_dtypes=True)
            g.iota(rev4[:], [[-1, NEG]], base=NEG, channel_multiplier=0, allow_small_or_imprecise_dtypes=True)
            g.memset(epsr[:, 0:1], RMS_EPS)
            link(g.memset(epsr[:, 1:2], LN_EPS))
            keep(ident[:], [[-1, P]], 0, 1, 1.0, ALU.not_equal)
            keep(tri[:], [[-1, P]], 0, 1, 0.0)
            for v, fill in ((causal, 0.0), (negmask, NEG_BIG)):
                keep(v[:, 0:128], [[1, P]], -1, -1, fill)
                keep(v[:, 256:384], [[1, P]], -1, -1, fill)
            keep(chunkmask[:], [[1, P]], 0, -1, 0.0)
            v = chunkmask[:].rearrange("p (a b) -> p a b", b=CH)
            keep(v, [[-CH, P // CH], [0, CH]], 0, 1, 0.0)
            for m, lo, fill in ((strict4, -1, 0.0), (neg4, -1, NEG_BIG), (incl4, 0, 0.0)):
                keep(m[:], [[1, TS]], lo, -1, fill)
                v = m[:].rearrange("p (a b) -> p a b", b=SS)
                keep(v, [[-SS, NSEQ], [0, SS]], 0, 1, fill)
            keep(seqmask[:], [[-SS, NSEQ]], 0, 1, 0.0)
            keep(seqmask[:], [[SS, NSEQ]], SS - 1, -1, 0.0)
            link(g.memset(rowsel[0:1, 0:P], 1.0))
            link(g.memset(rowsel[0:TS, P:P + TS], 1.0))
            v = rowsel[0:TS, P:P + TS].rearrange("p (a b) -> p a b", b=SS)
            keep(v, [[-1, NSEQ], [0, SS]], -1, 1, 0.0, ALU.is_equal)
            for j in range(1, 4):
                link(g.tensor_copy(rowsel[32 * j:32 * j + 32, :], rowsel[0:32, :]))
            pool.sem_inc(consts_ready, 1)

            for h in range(2):
                pool.dma_start(s0[h], state[:, h].rearrange("b p v -> p b v")).then_inc(s0_loaded[h], 16)
            pool.wait_ge(evac_act, 15)
            pool.wait_ge(evac_dve, 15)
            for h in range(H):
                if h >= 1:
                    pool.wait_ge(us_pe, 2 * h)
                nc.gpsimd.tensor_tensor(vblk, bc(tok[0:TS, 5, h * P:(h + 1) * P], 1, NSEQ),
                                        bc(seqmask[:], 2, P), ALU.mult).then_inc(vblk_ready, 1)
                pool.wait_ge(us_dve, 3 * (h + 1))
                pool.dma_start(s_s[:, h].rearrange("b p v -> p b v"), s0[h % 2]).then_inc(ssample_stored, 16)
                if h + 2 < H:
                    pool.wait_ge(ssample_stored, 16 * (h + 1))
                    pool.dma_start(s0[h % 2], state[:, h + 2].rearrange("b p v -> p b v")
                                   ).then_inc(s0_loaded[h % 2], 16)
                if h % 4 == 3:
                    pool.wait_ge(u_dve, 8 * (h // 4 + 1))
                    pool.dma_start(s_p[h - 3:h + 1].rearrange("h p v -> p h v"), shist[:, 7, :, :]
                                   ).then_inc(sprompt_stored, 16)

            for i, (t0, tn) in enumerate(TILES):
                pool.wait_ge(kout_evac, i + 1)
                dst = k_p[t0:t0 + tn, :] if i < 2 else k_s[:]
                pool.dma_start(dst, kstage[0:tn, i, :]).then_inc(k_stored, 16)
            pool.wait_ge(evac_act, 24)
            pool.wait_ge(evac_dve, 24)
            for i, (t0, tn) in enumerate(TILES):
                dst = v_p[t0:t0 + tn, :] if i < 2 else v_s[:]
                pool.dma_start(dst, tok[0:tn, i, :]).then_inc(v_stored, 16)

            pool.wait_ge(hgo_act, 4)
            pool.wait_ge(osm_dve, 2)
            pool.wait_ge(ss_pe, 3)
            nc.gpsimd.tensor_tensor(sqo[0], hout, hout, ALU.mult).then_inc(nsq_pool, 1)

            pool.wait_ge(o_pe, H)
            pool.wait_ge(ss_pe, 4)
            pool.dma_start(xa, xT[:]).then_inc(xa_loaded, 16)
            pool.wait_ge(xa_loaded, 16)
            nc.gpsimd.tensor_scalar(xa, xa, ALPHA, 0.0, ALU.mult, ALU.add).then_inc(xa_ready, 1)

            pool.wait_ge(ln_dve, 1)
            part = rT[:, 12:16, :]
            link(nc.gpsimd.tensor_tensor(part, part, bc(mu, 1, 4), ALU.subtract))
            pool.wait_ge(rstd_act, 1)
            nc.gpsimd.tensor_tensor(part, part, bc(rstd, 1, 4), ALU.mult).then_inc(ln_pool, 1)

            for i, (t0, tn) in enumerate(TILES):
                pool.wait_ge(tt_act, 4 * (i + 1))
                pool.dma_start(u2_rows[t0:t0 + tn, :], urow[i][0:tn, :]).then_inc(u2_stored, 16)
            pool.wait_ge(plan_ready, 2)
            nblocks = pool.value_load(plan[0:1, NB1:NB1 + 1], min_val=0, max_val=NBLK)
            pool.wait_ge(u2_stored, 3 * 16)

            def gather(n):
                pool.wait_ge(idx_ready, n)
                pool.sem_inc(wait_carrier, 1)
                nc.gpsimd.indirect_dma_start(out=xg, out_offset=None, in_=u2_rows[:],
                                             in_offset=bass.IndirectOffsetOnAxis(idx1[:, 0:1], 0)
                                             ).then_inc(gathered, 16)

            nc.gpsimd.tensor_copy(idx1[:], idxs[:, 0:1]).then_inc(idx_ready, 1)
            pool.wait_ge(tt_act, 24)
            gather(1)
            with pool.Fori(0, NBLK) as i:
                with pool.If(i < nblocks):
                    pool.wait_ge(gathered, i * 16 + 16)
                    nc.gpsimd.tensor_copy(idx1[:], idxs[:, bass.ds(i + 1, 1)]).then_inc(idx_ready, 1)
                    pool.wait_ge(x_turned, i + 1)
                    gather(i + 2)
            pool.wait_ge(moe_used, nblocks * MOE_CHUNKS + SLOTS)
            pool.wait_ge(gathered, nblocks * 16 + 16)
            pool.sem_inc(wait_carrier, 1)
            pool.dma_start(ln2b, ln2.partition_broadcast(P)).then_inc(late_loaded, 16)
            pool.wait_ge(sum_s_act, 1)
            pool.wait_ge(g2_act, 4)
            w = moe_out[2][0:TS, :]
            link(nc.gpsimd.tensor_tensor(w, w, g2s[0:TS, :], ALU.mult))
            nc.gpsimd.tensor_tensor(w, w, xres[0:TS, 2, :], ALU.add).then_inc(out_s_pool, 1)
            pool.wait_ge(late_loaded, 16)
            pool.wait_ge(norm_act, 1)
            w = moe_out[0]
            link(nc.gpsimd.tensor_tensor(w, w, ln2b[:, 0, :], ALU.mult))
            nc.gpsimd.tensor_tensor(w, w, ln2b[:, 1, :], ALU.add).then_inc(fin_pool, 1)
        @block.tensor
        def _(pe):
            mm = nc.tensor.matmul

            def ada_chunk(slot, is_loaded, t, freed):
                pe.wait_ge(slot_loaded[slot], is_loaded)
                if t == 0 and freed is not None:
                    pe.wait_ge(rows_copied, freed)
                for j in range(4):
                    last = mm(ps[32 * j:32 * j + 32, 0, :], silu_c[:, t, :], ring[:, slot, 512 * j:512 * (j + 1)],
                              start=(t == 0), stop=(t == KC - 1))
                last.then_inc(ring_used, 1)

            def ada_turn(copied, freed):
                pe.wait_ge(rows_copied, copied)
                if freed is not None:
                    pe.wait_ge(ada_ready, freed)
                for c in range(4):
                    last = nc.tensor.transpose(ps[:, 1, P * c:P * (c + 1)], ada_rows[:, P * c:P * (c + 1)], ident[:])
                last.then_inc(rows_turned, 1)

            def head_chunk(slot, bank):
                for t in range(KC):
                    last = mm(ps[:, bank, 0:T], ring[:, slot, P * t:P * (t + 1)], uT[:, t, :],
                              start=(t == 0), stop=(t == KC - 1))
                last.then_inc(ring_used, 1)

            def row_chunk(slot, c):
                for t in range(4):
                    for i, (t0, tn) in enumerate(TILES):
                        last = mm(ps[0:tn, 4 + i, :], uT[:, 4 * (c % 4) + t, t0:t0 + tn],
                                  ring[:, slot, 512 * t:512 * (t + 1)],
                                  start=(c % 4 == 0 and t == 0), stop=(c % 4 == 3 and t == 3))
                last.then_inc(ring_used, 1)

            pe.sem_inc(ring_used, SLOTS)
            pe.sem_inc(comb_pe, 5)
            pe.sem_inc(hT_pe, 1)
            pe.wait_ge(silu_c_ready, 1)
            pe.wait_ge(consts_ready, 1)
            for six in range(2):
                for t in range(KC):
                    n = six * KC + t
                    ada_chunk(n % SLOTS, loaded(n), t, six if six else None)
                ada_turn(six + 1, six if six else None)

            pe.wait_ge(u_ready, 1)
            with pe.Fori(0, 3) as g:
                for c in range(SLOTS):
                    for t in (2 * c, 2 * c + 1):
                        n = N_MIX + 3 * c + t % 2
                        ada_chunk(n % SLOTS, g * 48 + loaded(n), t, g + 2)
                    n = N_MIX + 3 * c + 2
                    pe.wait_ge(slot_loaded[n % SLOTS], g * 48 + loaded(n))
                    pe.wait_ge((evac_act, evac_dve)[c % 2], g * 4 + (2 + c // 2 - 1))
                    head_chunk(n % SLOTS, 4 + c % 4)
                ada_turn(g + 3, g + 2)

            def chunk_scores(tt):
                for h in range(H):
                    last = mm(ps[:, 2 + h // 4, P * (h % 4):P * (h % 4 + 1)],
                              khat[:, h, P * tt:P * (tt + 1)], qhat[:, h, P * tt:P * (tt + 1)], start=True, stop=True)
                return last

            for c in range(SLOTS):
                for t in (2 * c, 2 * c + 1):
                    n = N_MIX + 3 * MIX + 3 * c + t % 2
                    ada_chunk(n % SLOTS, loaded(n), t, 5)
                n = N_MIX + 3 * MIX + 3 * c + 2
                pe.wait_ge(slot_loaded[n % SLOTS], loaded(n))
                if c == 0:
                    pe.wait_ge(evac_act, 14)
                    pe.wait_ge(evac_dve, 14)
                if c == 4:
                    pe.wait_ge(evac_act, 15)
                row_chunk(n % SLOTS, c)
                if c == 2:
                    pe.wait_ge(hg_dve, 3)
                    for h in range(H):
                        mm(ps[0:TS, 7, TS * h:TS * (h + 1)], khat[:, h, TP:T], qhat[:, h, TP:T], start=True, stop=True)
                    chunk_scores(0).then_inc(hg_pe, 1)
                if c == 5:
                    pe.wait_ge(hg_dve, 7)
                    chunk_scores(1).then_inc(hg_pe, 1)

            pe.wait_ge(evac_dve, 15)
            for half in range(2):
                heads = range(4 * half, 4 * half + 4)
                if half == 0:
                    pe.wait_ge(rows_copied, 6)
                    pe.wait_ge(ada_ready, 5)
                    pe.wait_ge(hg_dve, 8)
                else:
                    pe.wait_ge(us_dve, 12)
                    pe.wait_ge(osm_dve, 1)
                    pe.wait_ge(hgo_act, 2)
                for tt in range(2):
                    for h in range(4):
                        nc.tensor.transpose(ps[:, tt, P * h:P * (h + 1)],
                                            hf[:, heads[h], P * tt:P * (tt + 1)], ident[:])
                for h in range(4):
                    last = nc.tensor.transpose(ps[0:TS, 7, P * h:P * (h + 1)], hf[:, heads[h], TP:T], ident[:])
                last.then_inc(kd_pe, 1)
                for c in range(8):
                    n = N_SQ + 8 * half + c
                    pe.wait_ge(slot_loaded[c], loaded(n))
                    pe.wait_ge((evac_act, evac_dve)[c % 2], 15 + 4 * half + c // 2)
                    head_chunk(c, 4 + c % 2)
                    if c == 0:
                        pe.wait_ge(kd_act, half + 1)
                        pe.wait_ge(qpad_ready, half + 1)
                    if 8 * half + c >= 1:
                        pe.wait_ge(u_dve, 8 * half + c)
                    tt, r0 = c // 4, CH * (c % 4)
                    for h in range(4):
                        k = heads[h]
                        last = mm(ps[:, 2, P * h:P * (h + 1)], kdt[r0:r0 + CH, tt, h, :],
                                  tok[r0:r0 + CH, 3 + tt, P * k:P * (k + 1)], start=True, stop=True,
                                  tile_position=(r0, 0))
                    last.then_inc(u_pe, 1)
                    if c % 2 == 0:
                        continue
                    h = c // 2
                    k = heads[h]
                    pe.wait_ge(s0_loaded[k % 2], 16 * (k // 2 + 1))
                    for b in range(NSEQ):
                        mm(ps[32 * h:32 * h + 32, 3, 0:P], qpad[:, h, b, :], s0[k % 2][:, b, :],
                           start=(b == 0), stop=False)
                    mm(ps[32 * h:32 * h + 32, 3, 0:P], abufs[:, k, :], tok[0:TS, 5, P * k:P * (k + 1)],
                       start=False, stop=True).then_inc(os_pe, 1)
                    pe.wait_ge(vblk_ready, k + 1)
                    for part in range(2):
                        if k >= 1:
                            pe.wait_ge(us_dve, 3 * k - 1 + part)
                        mm(ps[:, part, :], kdts[:, h, :],
                           vblk[:, 4 * part:4 * part + 4, :].rearrange("p b v -> p (b v)"), start=True, stop=True
                           ).then_inc(us_pe, 1)
                pe.wait_ge(u_dve, 8 * half + 7)
                for pair in range(2):
                    if pair == 1:
                        pe.wait_ge(osr_dve, half + 1)
                        nc.tensor.transpose(ps[:, 3, P:2 * P], osr, ident[:]).then_inc(osr_pe, 1)
                        pe.wait_ge(hgo_act, 2 * half + 1)
                    for tt in range(2):
                        for h in (2 * pair, 2 * pair + 1):
                            k = heads[h]
                            o = ps[:, 7, 256 * (h % 2) + P * tt:256 * (h % 2) + P * (tt + 1)]
                            mm(o, tok[:, 3 + tt, P * k:P * (k + 1)], abuf[:, tt, k, :], start=True, stop=False)
                            for c4 in range(4):
                                c = 4 * tt + c4
                                if c == 0:
                                    continue
                                last = mm(o[:, CH * c4:CH * (c4 + 1)], shist[:, c - 1, h, :],
                                          hq[:, k, CH * c:CH * (c + 1)], start=False, stop=(c4 == 3))
                    last.then_inc(hgo_pe, 1)

            pe.wait_ge(evac_act, 23)
            pe.wait_ge(evac_dve, 23)
            pe.wait_ge(us_dve, 3 * H)
            pe.wait_ge(u_dve, 16)
            pe.wait_ge(osm_dve, 2)
            for i, (t0, tn) in enumerate(TILES):
                if i == 2:
                    pe.wait_ge(kout_evac, 1)
                for h in range(H):
                    last = nc.tensor.transpose(ps[0:tn, 2 * (i % 2) + h // 4, P * (h % 4):P * (h % 4 + 1)],
                                               skT[:, h, t0:t0 + tn], ident[:])
                last.then_inc(kout_pe, 1)

            for c in range(SLOTS + 1):
                if c < SLOTS:
                    n = N_SV + 2 * c
                    pe.wait_ge(slot_loaded[n % SLOTS], loaded(n))
                    if c == 4:
                        pe.wait_ge(evac_act, 24)
                    row_chunk(n % SLOTS, c)
                if c >= 1:
                    pe.wait_ge(kT_act, c)
                    pe.wait_ge(kT_dve, c)
                    pe.wait_ge(hgo_act, 4)
                    if c >= 2:
                        pe.wait_ge(zt_dve, c - 1)
                    for h in range(H):
                        i, j = h // 4, h % 4
                        last = mm(ps[32 * j:32 * j + 32, 7, 256 * i:256 * (i + 1)], sqT[:, h, TP:T], keyT[:, h, :],
                                  start=True, stop=True)
                    last.then_inc(zr_pe, 1)
                if c < SLOTS:
                    n = N_SV + 2 * c + 1
                    pe.wait_ge(slot_loaded[n % SLOTS], loaded(n))
                    if c == 0:
                        pe.wait_ge(kout_evac, 3)
                    for pg in range(NPG):
                        for h in range(H):
                            last = nc.tensor.transpose(ps[:, 2 * pg + h // 4, P * (h % 4):P * (h % 4 + 1)],
                                                       ring[:, n % SLOTS, 1024 * pg + P * h:1024 * pg + P * (h + 1)],
                                                       ident[:])
                        last.then_inc((kT_pe, ring_used)[pg], 1)
                if c >= 1:
                    pe.wait_ge(zr_dve, c)
                    for pg in range(NPG):
                        for i in range(2):
                            q = 2 * pg + i
                            last = nc.tensor.transpose(ps[:, 7, P * q:P * (q + 1)],
                                                       zrow[:, 256 * i + P * pg:256 * i + P * (pg + 1)], ident[:])
                    last.then_inc(zt_pe, 1)
            pe.wait_ge(evac_act, 24)
            pe.wait_ge(evac_dve, 24)
            pe.wait_ge(zt_dve, NSEQ)

            for h in range(H + 2):
                if h < H:
                    if h >= 2:
                        pe.wait_ge(z_dve, h - 1)
                    z = ps[:, 2 + h % 2, :]
                    mm(z[:, 0:256], skT[:, h, 0:128], sqT[:, h, 0:256], start=True, stop=True)
                    mm(z[:, 256:384], skT[:, h, 128:256], sqT[:, h, 128:256], start=True, stop=True
                       ).then_inc(z_pe, 1)
                if 1 <= h <= H:
                    k = h - 1
                    pe.wait_ge(sp_ready, k + 1)
                    if k >= 2:
                        pe.wait_ge(d_dve, k - 1)
                    c, s = ps[:, 4 + k % 2, :], spl[k % 2]
                    mm(c[:, 0:256], tri[:], s[:, 0:256], start=True, stop=False)
                    mm(c[:, 128:256], ones[:], s[:, 256:384], start=False, stop=True)
                    mm(c[:, 256:384], tri[:], s[:, 256:384], start=True, stop=True).then_inc(c_pe, 1)
                if h >= 2:
                    k = h - 2
                    pe.wait_ge(a_ready, k + 1)
                    if k >= 2:
                        pe.wait_ge(o_evac, k - 1)
                    o, a = ps[:, 6 + k % 2, :], aa[k % 2]
                    mm(o[:, 0:256], tok[:, 0, P * k:P * (k + 1)], a[:, 0:256], start=True, stop=False)
                    mm(o[:, 128:256], tok[:, 1, P * k:P * (k + 1)], a[:, 256:384], start=False, stop=True
                       ).then_inc(o_pe, 1)
                if h == 0:
                    pe.wait_ge(kT_act, NSEQ)
                    pe.wait_ge(kT_dve, NSEQ)
                    for k in range(H):
                        last = mm(ps[0:TS, 0, TS * k:TS * (k + 1)], skT[:, k, TP:T], sqT[:, k, TP:T],
                                  start=True, stop=True)
                    last.then_inc(ss_pe, 1)
                if h == 3:
                    pe.wait_ge(ss_dve, 2)
                    c = ps[:, 1, :].rearrange("p (g b h t) -> p g b h t", g=NPG, b=NSEQ, h=H)
                    s_new = sN.rearrange("p h (b t) -> p b h t", t=SS)
                    s_past = sP.rearrange("p (g b) h t -> p g (b h t)", g=NPG)
                    cf = ps[:, 1, :].rearrange("p (g n) -> p g n", g=NPG)
                    mm(cf[:, 1], tri[:], s_past[:, 1], start=True, stop=False)
                    mm(c[:, 1], ones[0:TS, :], s_new, start=False, stop=True)
                    mm(cf[:, 0], tri[:], s_past[:, 0], start=True, stop=False)
                    mm(cf[:, 0], ones[:], s_past[:, 1], start=False, stop=False)
                    mm(c[:, 0], ones[0:TS, :], s_new, start=False, stop=True)
                    mm(ps[0:TS, 0, 0:TS * H], tri[0:TS, 0:TS], sN.rearrange("p h t -> p (h t)"), start=True, stop=True
                       ).then_inc(ss_pe, 1)
                if h == 5:
                    pe.wait_ge(ss_act, 2)
                    for b in range(NSEQ):
                        pe.wait_ge(slot_loaded[b], loaded(N_V + b))
                        for pg in range(NPG):
                            for k in range(H):
                                i, j = k // 4, k % 4
                                last = mm(ps[32 * j:32 * j + 32, i, 0:P], apad[:, pg, b, k, :],
                                          ring[:, b, 1024 * pg + P * k:1024 * pg + P * (k + 1)],
                                          start=(b == 0 and pg == 0), stop=False)
                        last.then_inc(ring_used, 1)
                    for k in range(H):
                        i, j = k // 4, k % 4
                        last = mm(ps[32 * j:32 * j + 32, i, 0:P], aN[:, k, :], tok[0:TS, 2, P * k:P * (k + 1)],
                                  start=False, stop=True)
                    last.then_inc(ss_pe, 1)
                if h == 8:
                    pe.wait_ge(ss_dve, 4)
                    for i in range(2):
                        last = nc.tensor.transpose(ps[:, 0, P * i:P * (i + 1)], orow[:, i, :], ident[:])
                    last.then_inc(ss_pe, 1)

            pe.wait_ge(d_dve, H)
            pe.wait_ge(o_evac, H)
            pe.wait_ge(ss_dve, 5)
            for n in range(4):
                group, half = n // 2, n % 2
                if group == 0:
                    pe.wait_ge(nsq_pool, 1)
                else:
                    pe.wait_ge(nsq_act, half + 1)
                    pe.wait_ge(nln_act, n - 1)
                for k in range(4):
                    last = mm(ps[:, (2 + 4 * half + k) % 8, 0:T], ones[:], sqo[group][:, 4 * half + k, :],
                              start=True, stop=True)
                last.then_inc(nm_pe, 1)

            pe.wait_ge(nm_dve, 2)

            def sums(m):
                pe.wait_ge(wo_act, m + 1)
                mm(ps[:, 2, 0:T], ones[:], rT[:, m, :], start=(m == 0), stop=(m == KC - 1))
                mm(ps[:, 3, 0:T], ones[:], r2[m % 4], start=(m == 0), stop=(m == KC - 1)).then_inc(st_pe, 1)

            for m in range(KC):
                n = N_WO + m
                pe.wait_ge(slot_loaded[n % SLOTS], loaded(n))
                if m >= 4:
                    pe.wait_ge(wo_dve, m - 3)
                for k in range(KC):
                    last = mm(ps[:, 4 + m % 4, 0:T], ring[:, n % SLOTS, P * k:P * (k + 1)], mixT[:, k, :],
                              start=(k == 0), stop=(k == KC - 1))
                last.then_inc(ring_used, 1)
                if m >= 2:
                    sums(m - 2)
            sums(KC - 2)
            sums(KC - 1)

            pe.sem_inc(moe_used, SLOTS)
            pe.wait_ge(wo_dve, KC)
            for m in range(KC):
                if m % 4 == 0:
                    pe.wait_ge(u2_dve, m // 4 + 1)
                last = mm(ps[0:NL, 4, 0:T], wr[:, m, :], u2T[:, m, :], start=(m == 0), stop=(m == KC - 1))
            last.then_inc(rt_pe, 1)

            def turn_tokens(n, src):
                i, q = n // 4 % 3, n % 4
                t0, tn = TILES[i]
                if n >= 2:
                    pe.wait_ge(tt_act, n - 1)
                for m in range(4):
                    last = nc.tensor.transpose(ps[0:tn, 6 + n % 2, P * m:P * (m + 1)],
                                               src[:, 4 * q + m, t0:t0 + tn], ident[:])
                last.then_inc(tt_pe, 1)

            pe.wait_ge(rt_act, 1)
            for i, (t0, tn) in enumerate(TILES):
                last = nc.tensor.transpose(ps[0:tn, 5, 64 * i:64 * i + NL], lgT[:, t0:t0 + tn], ident[0:NL, 0:NL])
            last.then_inc(rt_pe, 1)
            for n in range(12):
                turn_tokens(n, u2T)
            pe.wait_ge(rt_dve, 1)
            for i in range(3):
                mm(ps[:, 2, NE * i:NE * (i + 1)], causal[:, 0:P], both[:, i, :], start=True, stop=(i == 0))
                for k in range(i):
                    mm(ps[:, 2, NE * i:NE * (i + 1)], ones[:], both[:, k, :], start=False, stop=(k == i - 1))
            for i in range(3):
                last = mm(ps[:, 3, 0:NE], ones[:], both[:, i, :], start=(i == 0), stop=(i == 2))
            last.then_inc(rt_pe, 1)
            for n in range(12, 24):
                turn_tokens(n, rT)
            def select_g2(j):
                if j >= 2:
                    pe.wait_ge(g2_act, j - 1)
                a, b = ((0, 1), (6, 7))[j % 2]
                r = slice(32 * j, 32 * j + 32)
                mm(ps[:, a, :], rowsel[r, 0:P], ada_rows[r, :], start=True, stop=True, tile_position=(32 * j, 0))
                mm(ps[0:TS, b, :], rowsel[r, P:P + TS], ada_rows[r, :], start=True, stop=True,
                   tile_position=(32 * j, 0)).then_inc(g2_pe, 1)

            pe.wait_ge(tt_act, 24)
            for j in range(2):
                select_g2(j)
            pe.wait_ge(rt_dve, 2)
            for k in range(2):
                for i in range(3):
                    last = mm(ps[0:B, 4, 0:NB1], rsel[k][:, i, :], bsel[k][:, i, :],
                              start=(k == 0 and i == 0), stop=(k == 1 and i == 2))
            last.then_inc(rt_pe, 1)
            for j in range(2, 4):
                select_g2(j)

            pe.sem_inc(moe_used, MOE_CHUNKS - SLOTS)
            pe.wait_ge(ss_dve, 5)
            pe.wait_ge(plan_ready, 2)
            nblocks = pe.value_load(plan[0:1, NB1:NB1 + 1], min_val=0, max_val=NBLK)

            def turn_rows(n):
                pe.wait_ge(gathered, n * 16)
                pe.sem_inc(wait_carrier, 1)
                for m in range(KC):
                    last = nc.tensor.transpose(ps[:, m // 8, B * (m % 8):B * (m % 8 + 1)], xg[:, P * m:P * (m + 1)],
                                               ident[0:B, 0:B])
                last.then_inc(x_turned, 1)

            pe.wait_ge(g2_act, 3)
            turn_rows(1)
            pe.wait_ge(diag_ready, 1)
            for v in range(4):
                for i, (t0, tn) in enumerate(TILES):
                    last = mm(ps[:, 2 + v, t0:t0 + tn], ones[0:tn, :], diag[0:tn, v, i, 0:tn], start=True, stop=True)
            last.then_inc(where_pe, 1)
            pe.wait_ge(spread_ready, 1)
            pe.wait_ge(g2_act, 4)

            def combine(n):
                pe.wait_ge(y_evac, n * 2 + 2)
                pe.wait_ge(spread_ready, n + 1)
                for j in range(5):
                    pe.wait_ge(sum_dve, n * 5 + max(j, 1))
                    pe.sem_inc(wait_carrier, 1)
                    if j < 4:
                        t0, tn = TILES[j // 2]
                        for r in range(2):
                            rows = slice(B * r, B * (r + 1))
                            last = mm(ps[0:tn, ((7, 4), (5, 6))[j % 2][r], :], spread[rows, t0:t0 + tn],
                                      yout[rows, 512 * (j % 2):512 * (j % 2 + 1)], start=True, stop=True,
                                      tile_position=(B * r, 0))
                    else:
                        for q in range(4):
                            rows = slice(B * (q // 2), B * (q // 2 + 1))
                            last = mm(ps[32 * q:32 * q + 32, 7, :], spread[rows, TP:T],
                                      yout[rows, 512 * (q % 2):512 * (q % 2 + 1)], start=True, stop=True,
                                      tile_position=(B * (q // 2), 32 * q))
                    last.then_inc(comb_pe, 1)

            with pe.Fori(0, NBLK) as i:
                with pe.If(i < nblocks):
                    pe.wait_ge(x_copied, i + 1)
                    for c in range(8):
                        pe.wait_ge(moe_loaded[c], i * 16 + 16)
                        for t in range(4):
                            for s in range(2):
                                last = mm(ps[B * s:B * (s + 1), 2 + c // 4, 0:256], xgT[:, 4 * (c % 4) + t, :],
                                          ring[:, c, 512 * t + 256 * s:512 * t + 256 * (s + 1)],
                                          start=(c % 4 == 0 and t == 0), stop=(c % 4 == 3 and t == 3))
                        last.then_inc(moe_used, 1)
                    turn_rows(i + 2)
                    with pe.If(i > 0):
                        combine(i)
                    pe.wait_ge(hid_dve, i + 2)
                    pe.wait_ge(sum_dve, i * 5 + 4)
                    pe.sem_inc(wait_carrier, 1)
                    for cb in range(2):
                        last = nc.tensor.transpose(ps[:, 4, P * cb:P * (cb + 1)], hid[:, P * cb:P * (cb + 1)], ident[:])
                    last.then_inc(hT_pe, 1)
                    pe.wait_ge(hT_dve, i + 1)
                    pe.wait_ge(sum_dve, i * 5 + 5)
                    for q in range(4):
                        pe.wait_ge(moe_loaded[8 + q], i * 16 + 16)
                        for nn in range(2):
                            for s in range(2):
                                last = mm(ps[B * s:B * (s + 1), 5 + nn, :], hT[:, q % 2, B * (q // 2):B * (q // 2 + 1)],
                                          mslot[q][:, 1024 * s + 512 * nn:1024 * s + 512 * (nn + 1)],
                                          start=(q == 0), stop=(q == 3))
                        last.then_inc(moe_used, 1)
            combine(nblocks)
        @block.scalar
        def _(act):
            A = nc.scalar.activation
            count = [0]

            def link(ins):
                count[0] += 1
                ins.then_inc(act_step, 1)
                act.wait_ge(act_step, count[0])

            act.sem_inc(evac_act, 2)
            act.wait_ge(c_loaded, 16)
            A(ctmp[:], cin[:], ACT.Exp, scale=-1.0).then_inc(expc_ready, 1)

            with act.Fori(0, 2) as g:
                for c in range(0, SLOTS, 2):
                    act.wait_ge(ring_used, g * MIX + used(N_MIX + 3 * c + 2))
                    nc.scalar.copy(hf_hq[:, bass.ds(g * H + c, 1), :].rearrange("p a t -> p (a t)"),
                                   ps[:, 4 + c % 4, 0:T]).then_inc(evac_act, 1)

            def evacuate_head(dst, n, bank):
                act.wait_ge(ring_used, used(n))
                nc.scalar.copy(dst, ps[:, bank, 0:T]).then_inc(evac_act, 1)

            def evacuate_rows(n, slot):
                act.wait_ge(ring_used, used(n))
                for i, (t0, tn) in enumerate(TILES):
                    last = nc.scalar.copy(tok[0:tn, slot + i, 0:512], ps[0:tn, 4 + i, :])
                last.then_inc(evac_act, 1)

            act.wait_ge(lb_dve, 1)
            A(lbt[:, 2, :], lbt[:, 2, :], ACT.Exp).then_inc(lb_act, 1)
            act.wait_ge(evac_act, 2 + 8)
            act.wait_ge(evac_dve, 2 + 8)
            A(qhat, hq, ACT.Exp, scale=-1.0)
            A(t1, hf, ACT.Exp, scale=-1.0).then_inc(hg_act, 1)
            N_G = N_MIX + 2 * MIX + 2
            evacuate_head(hg[:, 0, :], N_G, 4)
            act.wait_ge(hg_dve, 1)
            A(t1, t1, ACT.Ln).then_inc(hg_act, 1)
            evacuate_head(hg[:, 2, :], N_G + 3 * 2, 6)
            act.wait_ge(hg_dve, 2)
            A(qhat, t1, ACT.Exp)
            A(khat, t1, ACT.Exp, scale=-1.0).then_inc(hg_act, 1)
            act.wait_ge(hg_act, 3)
            A(t1, bcum, ACT.Exp)
            bp = bcum[:, :, 0:TP].rearrange("p h (c t) -> p h c t", t=CH)
            bs = bcum[:, :, TP:T].rearrange("p h (c t) -> p h c t", t=SS)
            A(dec[:, :, 0:8], bp[:, :, :, CH - 1], ACT.Exp)
            A(dec[:, :, 8:16], bs[:, :, :, SS - 1], ACT.Exp).then_inc(hg_act, 1)
            evacuate_head(hg[:, 4, :], N_G + 3 * 4, 4)
            act.wait_ge(hg_dve, 4)
            A(t1, t1, ACT.Exp).then_inc(hg_act, 1)
            evacuate_head(hg[:, 6, :], N_G + 3 * 6, 6)
            act.wait_ge(hg_dve, 5)
            act.wait_ge(evac_act, 2 + 12)
            act.wait_ge(evac_dve, 2 + 12)
            A(t1, hg, ACT.Exp, scale=-1.0).then_inc(hg_act, 1)
            evacuate_rows(N_MIX + 3 * MIX + 3 * 3 + 2, 3)

            for half in range(2):
                act.wait_ge(kd_pe, half + 1)
                if half == 0:
                    act.wait_ge(hg_dve, 6)
                    act.wait_ge(hg_pe, 2)
                else:
                    act.wait_ge(us_pe, 8)
                nc.scalar.copy(kdt, ps[:, 0:2, :].rearrange("p a (h s) -> p a h s", s=P))
                nc.scalar.copy(kdts, ps[0:TS, 7, :].rearrange("p (h s) -> p h s", s=P)).then_inc(kd_act, 1)
                for c in range(0, SLOTS, 2):
                    evacuate_head(projT[:, 8 * half + c, :], N_SQ + 8 * half + c, 4)
                for pair in range(2):
                    act.wait_ge(hgo_pe, 2 * half + pair + 1)
                    k = 4 * half + 2 * pair
                    nc.scalar.copy(hout[:, k:k + 2, 0:TP], ps[:, 7, :].rearrange("p (h t) -> p h t", h=2)
                                   ).then_inc(hgo_act, 1)

            act.wait_ge(sprompt_stored, 2 * 16)
            for c in range(SLOTS):
                if c == 3:
                    act.wait_ge(ssample_stored, H * 16)
                    act.wait_ge(os_pe, H)
                    evacuate_rows(N_SV + 2 * 3, 0)
                act.wait_ge(kT_pe, c + 1)
                if c >= 1:
                    act.wait_ge(zr_pe, c)
                nc.scalar.copy(keyT[:, :, 0:P], ps[:, 0:2, :].rearrange("p a (h s) -> p (a h) s", s=P)
                               ).then_inc(kT_act, 1)

            act.wait_ge(small_loaded, 16 * 11)
            for h in range(H + 1):
                if h < H:
                    act.wait_ge(z_dve, h + 1)
                    if h >= 2:
                        act.wait_ge(sp_ready, h - 1)
                    e = ee[h % 2]
                    link(A(e, zz[h % 2], ACT.Abs))
                    link(A(e, e, ACT.Exp, scale=-1.0))
                    A(e, e, ACT.Ln, bias=1.0).then_inc(soft_act, 1)
                if h >= 1:
                    k = h - 1
                    act.wait_ge(d_dve, k + 1)
                    if k >= 2:
                        act.wait_ge(o_pe, k - 1)
                    A(aa[k % 2], zn[k % 2], ACT.Exp).then_inc(a_ready, 1)
                if h == 1:
                    act.wait_ge(ss_dve, 1)
                    A(eP, zP, ACT.Abs)
                    link(A(eN, zN, ACT.Abs))
                    A(eP, eP, ACT.Exp, scale=-1.0)
                    link(A(eN, eN, ACT.Exp, scale=-1.0))
                    A(eP, eP, ACT.Ln, bias=1.0)
                    A(eN, eN, ACT.Ln, bias=1.0).then_inc(ss_act, 1)
                if h == 4:
                    act.wait_ge(ss_dve, 3)
                    d4 = dP.rearrange("p (g b) h t -> p g b h t", g=NPG)
                    for b in range(NSEQ):
                        A(apad[:, :, b, :, SS * b:SS * (b + 1)], d4[:, :, b], ACT.Exp)
                    A(aN, dN, ACT.Exp).then_inc(ss_act, 1)

            act.wait_ge(hgo_act, 4)
            act.wait_ge(osm_dve, 2)
            act.wait_ge(ss_dve, 5)
            act.wait_ge(o_evac, H)
            act.wait_ge(consts_ready, 1)
            for half in range(2):
                heads = slice(4 * half, 4 * half + 4)
                A(sqo[1][:, heads, :], mixT[:, H + 4 * half:H + 4 * half + 4, :], ACT.Square).then_inc(nsq_act, 1)
            for group in range(2):
                act.wait_ge(nm_pe, 2 * group + 1)
                A(rst[group][:, 0:4, :], ps[:, 2:6, 0:T], ACT.Ln, bias=epsr[:, 0:1], scale=1.0 / P
                  ).then_inc(nln_act, 1)
                act.wait_ge(nm_pe, 2 * group + 2)
                A(rst[group][:, 4:6, :], ps[:, 6:8, 0:T], ACT.Ln, bias=epsr[:, 0:1], scale=1.0 / P)
                A(rst[group][:, 6:8, :], ps[:, 0:2, 0:T], ACT.Ln, bias=epsr[:, 0:1], scale=1.0 / P
                  ).then_inc(nln_act, 1)
                act.wait_ge(nln_act, 2 * group + 2)
                A(rst[group], rst[group], ACT.Exp, scale=-0.5).then_inc(nrs_act, 1)

            for m in range(KC):
                act.wait_ge(wo_dve, m + 1)
                if m >= 4:
                    act.wait_ge(st_pe, m - 3)
                A(r2[m % 4], rT[:, m, :], ACT.Square).then_inc(wo_act, 1)
            act.wait_ge(ln_dve, 1)
            link(A(lt1, lt1, ACT.Ln, bias=epsr[:, 1:2]))
            A(rstd, lt1, ACT.Exp, scale=-0.5).then_inc(rstd_act, 1)
            for m in range(KC):
                if m < 12:
                    act.wait_ge(ln_dve, 2 + m // 4)
                else:
                    act.wait_ge(ln_pool, 1)
                A(rT[:, m, :], rT[:, m, :], ACT.Identity, bias=ln1t[:, 1, m:m + 1], scale=ln1t[:, 0, m:m + 1]
                  ).then_inc(x1_act, 1)

            act.wait_ge(v_stored, 3 * 16)
            act.wait_ge(rt_pe, 1)
            nc.scalar.copy(lgT[:], ps[0:NL, 4, 0:T]).then_inc(rt_act, 1)
            for n in range(12):
                t0, tn = TILES[n // 4]
                act.wait_ge(tt_pe, n + 1)
                nc.scalar.copy(urow[n // 4][0:tn, 512 * (n % 4):512 * (n % 4 + 1)], ps[0:tn, 6 + n % 2, :]
                               ).then_inc(tt_act, 1)
            act.wait_ge(rt_dve, 1)
            A(gexp, gexp, ACT.Exp)
            A(m2, m2, ACT.Exp).then_inc(rt_act, 1)
            for n in range(12, 24):
                i, q = n // 4 - 3, n % 4
                tn = TILES[i][1]
                act.wait_ge(tt_pe, n + 1)
                A(xres[0:tn, i, :].rearrange("t (p m) -> t m p", m=KC)[:, 4 * q:4 * q + 4, :],
                  ps[0:tn, 6 + n % 2, :].rearrange("t (m p) -> t m p", m=4), ACT.Copy, scale=ALPHA
                  ).then_inc(tt_act, 1)

            act.wait_ge(plan_ready, 1)
            act.wait_ge(u2_stored, 3 * 16)
            for j in range(4):
                a, b = ((0, 1), (6, 7))[j % 2]
                act.wait_ge(g2_pe, j + 1)
                nc.scalar.copy(g2p[:, 512 * j:512 * (j + 1)], ps[:, a, :])
                nc.scalar.copy(g2s[0:TS, 512 * j:512 * (j + 1)], ps[0:TS, b, :]).then_inc(g2_act, 1)

            act.wait_ge(plan_ready, 2)
            nblocks = act.value_load(plan[0:1, NB1:NB1 + 1], min_val=0, max_val=NBLK)

            def copy_rows(n):
                act.wait_ge(x_turned, n)
                nc.scalar.copy(xgT, ps[:, 0:2, :].rearrange("p a (m s) -> p (a m) s", s=B)).then_inc(x_copied, 1)

            copy_rows(1)
            with act.Fori(0, NBLK) as i:
                with act.If(i < nblocks):
                    act.wait_ge(moe_used, i * MOE_CHUNKS + (MOE_CHUNKS + 4))
                    act.wait_ge(hid_dve, i + 1)
                    A(hsil, ps[:, 2, 0:256], ACT.Silu).then_inc(sil_act, 1)
                    copy_rows(i + 2)
                    act.wait_ge(moe_used, i * MOE_CHUNKS + 2 * MOE_CHUNKS)
                    nc.scalar.copy(yout[:, 0:512], ps[:, 5, :]).then_inc(y_evac, 1)

            act.wait_ge(sum_dve, nblocks * 5 + 6)
            act.wait_ge(x_turned, nblocks + 1)
            act.sem_inc(wait_carrier, 1)
            for q in range(4):
                last = nc.scalar.copy(moe_out[2][0:TS, 512 * q:512 * (q + 1)], sum_s[32 * q:32 * q + 32, :])
            last.then_inc(sum_s_act, 1)
            for i, (t0, tn) in enumerate(TILES):
                w = moe_out[i][0:tn, :]
                act.wait_ge(var_dve, i + 1)
                link(A(rs1[0:tn, i:i + 1], bnag[0:tn, i, 1:2], ACT.Ln, bias=epsr[0:tn, 1:2]))
                A(rs1[0:tn, i:i + 1], rs1[0:tn, i:i + 1], ACT.Exp, scale=-0.5).then_inc(fin_act, 1)
                act.wait_ge(fin_dve, i + 1)
                A(w, w, ACT.Identity, bias=shift[0:tn, i:i + 1], scale=rs1[0:tn, i:i + 1]).then_inc(norm_act, 1)
            for i, (t0, tn) in enumerate(TILES):
                if i == 0:
                    act.wait_ge(fin_pool, 1)
                else:
                    act.wait_ge(fin_dve, 3 + i)
                dst = y_p[t0:t0 + tn, :] if i < 2 else y_s[:]
                act.dma_start(dst, moe_out[i][0:tn, :]).then_inc(out_stored, 16)

        @block.vector
        def _(dve):
            v = nc.vector
            count = [0]

            def link(ins):
                count[0] += 1
                ins.then_inc(dve_step, 1)
                dve.wait_ge(dve_step, count[0])

            dve.sem_inc(evac_dve, 2)
            dve.sem_inc(hid_dve, 1)
            dve.sem_inc(sum_dve, 5 + 1)
            dve.sem_inc(y_evac, 2)
            link(v.memset(silu_c[:], 0.0))
            dve.wait_ge(expc_ready, 1)
            link(v.tensor_scalar(ctmp[:], ctmp[:], 1.0, None, ALU.add))
            link(v.reciprocal(ctmp[:], ctmp[:]))
            v.tensor_tensor(silu_c[:, :, 0:R], cin[:].rearrange("p (m r) -> p m r", r=R),
                            ctmp[:].rearrange("p (m r) -> p m r", r=R), ALU.mult).then_inc(silu_c_ready, 1)
            dve.wait_ge(small_loaded, 16 * 11)
            link(v.tensor_scalar(badaT[:, 1, :], badaT[:, 1, :], 1.0, None, ALU.add))
            link(v.tensor_scalar(badaT[:, 4, :], badaT[:, 4, :], 1.0, None, ALU.add))

            v.tensor_tensor(lbt[:, 2, :], lbt[:, 1, :], lbt[:, 0, :], ALU.subtract).then_inc(lb_dve, 1)

            def copy_rows_out(n_used, turned, bias=None):
                dve.wait_ge(ring_used, n_used)
                if turned is not None:
                    dve.wait_ge(rows_turned, turned)
                if bias is None:
                    v.tensor_copy(ada_rows[:], ps[:, 0, :]).then_inc(rows_copied, 1)
                else:
                    v.tensor_tensor(ada_rows[:], ps[:, 0, :], bias, ALU.add).then_inc(rows_copied, 1)

            def add_bias(six):
                dve.wait_ge(rows_turned, six + 1)
                for c in range(4):
                    src = ps[:, 1, P * c:P * (c + 1)].rearrange("p (j r) -> p j r", j=4)[:, :, 0:R]
                    dst = adaT[:, bass.ds(six, 1)].rearrange("p a (j c) r -> p c (a j) r", j=4)[:, c]
                    bias = badaT[:, bass.ds(six, 1), :].rearrange("p a (j c) -> p c (a j)", j=4)[:, c]
                    last = v.tensor_tensor(dst, src, bc(bias, 2, R), ALU.add)
                last.then_inc(ada_ready, 1)

            for six in range(2):
                copy_rows_out(used(KC * six + KC - 1), six if six else None)
                add_bias(six)
            dve.wait_ge(ada_ready, 2)
            dve.wait_ge(x_loaded, 16)

            def seq(ap):
                return bc(ap, len(ap.shape), SS)

            def samp(ap):
                return ap.rearrange("p m (b t) -> p m b t", t=SS)

            for m in range(KC):
                v.tensor_scalar(uT[:, m, 0:TP], uT[:, m, 0:TP], adaT[:, 1, m, 0:1], adaT[:, 0, m, 0:1],
                                ALU.mult, ALU.add)
            us = samp(uT[:, :, TP:T])
            link(v.tensor_tensor(us, us, seq(adaT[:, 1, :, 1:R]), ALU.mult))
            v.tensor_tensor(us, us, seq(adaT[:, 0, :, 1:R]), ALU.add).then_inc(u_ready, 1)

            with dve.Fori(0, 2) as g:
                for c in range(1, SLOTS, 2):
                    if c == 7:
                        copy_rows_out(g * MIX + used(N_MIX + 22), g + 2)
                    dve.wait_ge(ring_used, g * MIX + used(N_MIX + 3 * c + 2))
                    v.tensor_copy(hf_hq[:, bass.ds(g * H + c, 1), :].rearrange("p a t -> p (a t)"),
                                  ps[:, 4 + c % 4, 0:T]).then_inc(evac_dve, 1)
                add_bias(g + 2)

            def evacuate_head(dst, n, bank):
                dve.wait_ge(ring_used, used(n))
                v.tensor_copy(dst, ps[:, bank, 0:T]).then_inc(evac_dve, 1)

            def evacuate_rows(n, slot):
                dve.wait_ge(ring_used, used(n))
                for i, (t0, tn) in enumerate(TILES):
                    last = v.tensor_copy(tok[0:tn, slot + i, 512:1024], ps[0:tn, 4 + i, :])
                last.then_inc(evac_dve, 1)

            N_G = N_MIX + 2 * MIX + 2
            flat = lambda ap: ap.rearrange("p h t -> p (h t)")
            link(v.memset(reset, 1.0))
            r3 = reset.rearrange("p (h t) -> p h t", t=T)
            v.memset(r3[:, :, 0:TP].rearrange("p h (c t) -> p h c t", t=CH)[:, :, :, 0:1], 0.0)
            v.memset(r3[:, :, TP:T].rearrange("p h (c t) -> p h c t", t=SS)[:, :, :, 0:1], 0.0)
            v.memset(abuf, 0.0)
            v.memset(abufs, 0.0)
            dve.wait_ge(lb_act, 1)
            link(v.tensor_scalar(lbt[:, 2, :], lbt[:, 2, :], 1.0, None, ALU.add))
            link(v.reciprocal(lbt[:, 2, :], lbt[:, 2, :]))
            dve.wait_ge(hg_act, 1)
            v.tensor_scalar(qhat, qhat, 1.0, None, ALU.add)
            v.tensor_scalar(t1, t1, 1.0, None, ALU.add)
            link(v.tensor_scalar(lbt[:, 3, :], lbt[:, 2, :], -1.0, 1.0, ALU.mult, ALU.add))
            v.reciprocal(qhat, qhat)
            link(v.reciprocal(t1, t1))
            v.tensor_tensor(hq, hq, qhat, ALU.mult)
            for h in range(H):
                last = v.tensor_scalar(t1[:, h, :], t1[:, h, :], lbt[:, 3, h:h + 1], lbt[:, 2, h:h + 1],
                                       ALU.mult, ALU.add)
            link(last)
            v.tensor_scalar(hf, t1, -1.0, 1.0, ALU.mult, ALU.add).then_inc(hg_dve, 1)
            evacuate_head(hg[:, 1, :], N_G + 3 * 1, 5)
            dve.wait_ge(hg_act, 2)
            for half in range(2):
                last = v.tensor_tensor_scan(flat(bcum[:, 4 * half:4 * half + 4, :]), reset,
                                            flat(t1[:, 4 * half:4 * half + 4, :]), 0.0, ALU.mult, ALU.add)
            link(last)
            bp = bcum[:, :, 0:TP].rearrange("p h (c t) -> p h c t", t=CH)
            bs = bcum[:, :, TP:T].rearrange("p h (c t) -> p h c t", t=SS)
            tp = t1[:, :, 0:TP].rearrange("p h (c t) -> p h c t", t=CH)
            ts = t1[:, :, TP:T].rearrange("p h (c t) -> p h c t", t=SS)
            for h in range(H):
                v.tensor_tensor(tp[:, h], bp[:, h], bc(bp[:, h, :, CH // 2 - 1], 2, CH), ALU.subtract)
                last = v.tensor_tensor(ts[:, h], bs[:, h], bc(bs[:, h, :, SS // 2 - 1], 2, SS), ALU.subtract)
            link(last)
            v.tensor_scalar(t1, t1, 80.0, -80.0, ALU.min, ALU.max).then_inc(hg_dve, 1)
            evacuate_head(hg[:, 3, :], N_G + 3 * 3, 7)
            dve.wait_ge(hg_act, 3)
            dve.wait_ge(hg_dve, 2)
            v.tensor_tensor(qhat, qhat, hq, ALU.mult)
            v.tensor_tensor(khat, khat, hf, ALU.mult).then_inc(hg_dve, 1)
            dve.wait_ge(hg_act, 4)
            dve.wait_ge(hg_dve, 3)
            link(v.tensor_tensor(hq, hq, t1, ALU.mult))
            for h in range(H):
                v.tensor_tensor(tp[:, h], bc(bp[:, h, :, CH - 1], 2, CH), bp[:, h], ALU.subtract)
                last = v.tensor_tensor(ts[:, h], bc(bs[:, h, :, SS - 1], 2, SS), bs[:, h], ALU.subtract)
            last.then_inc(hg_dve, 1)
            evacuate_head(hg[:, 5, :], N_G + 3 * 5, 5)
            copy_rows_out(used(N_MIX + 2 * MIX + 22), 4)
            evacuate_head(hg[:, 7, :], N_G + 3 * 7, 7)
            add_bias(4)
            dve.wait_ge(hg_act, 5)
            v.tensor_tensor(hf, hf, t1, ALU.mult).then_inc(hg_dve, 1)
            dve.wait_ge(hg_act, 6)
            link(v.tensor_scalar(t1, t1, 1.0, None, ALU.add))
            link(v.reciprocal(t1, t1))
            v.tensor_tensor(hg, hg, t1, ALU.mult).then_inc(hg_dve, 1)

            def keep_scores(tt):
                dve.wait_ge(hg_pe, tt + 1)
                for i in range(2):
                    last = v.copy_predicated(abuf[:, tt, 4 * i:4 * i + 4, :], bc(chunkmask[:].bitcast(U32), 1, 4),
                                             ps[:, 2 + i, :].rearrange("p (h t) -> p h t", t=P))
                return last

            last = keep_scores(0)
            last = v.copy_predicated(abufs, bc(incl4[:].bitcast(U32), 1, H),
                                     ps[0:TS, 7, 0:256].rearrange("p (h t) -> p h t", t=TS))
            last.then_inc(hg_dve, 1)
            keep_scores(1).then_inc(hg_dve, 1)
            copy_rows_out(used(N_MIX + 3 * MIX + 22), 5, bg2[:])
            evacuate_rows(N_MIX + 3 * MIX + 23, 3)

            link(v.memset(qpad, 0.0))
            for half in range(2):
                heads = slice(4 * half, 4 * half + 4)
                if half == 1:
                    dve.wait_ge(os_pe, 4)
                for b in range(NSEQ):
                    last = v.tensor_copy(qpad[:, :, b, SS * b:SS * (b + 1)],
                                         hq[:, heads, TP + SS * b:TP + SS * (b + 1)])
                last.then_inc(qpad_ready, 1)

                def state_after(c):
                    dve.wait_ge(u_pe, 8 * half + c + 1)
                    upd = ps[:, 2, :].rearrange("p (h v) -> p h v", v=P)
                    if c == 0:
                        if half == 1:
                            dve.wait_ge(hgo_pe, 2)
                            dve.wait_ge(sprompt_stored, 16)
                        v.tensor_copy(shist[:, 0], upd).then_inc(u_dve, 1)
                    else:
                        dve.wait_ge(u_dve, 8 * half + c)
                        link(v.tensor_tensor(shist[:, c], shist[:, c - 1], bc(dec[:, heads, c], 2, P), ALU.mult))
                        v.tensor_tensor(shist[:, c], shist[:, c], upd, ALU.add).then_inc(u_dve, 1)

                for c in range(8):
                    if c % 2 == 1:
                        evacuate_head(projT[:, 8 * half + c, :], N_SQ + 8 * half + c, 5)
                    state_after(c)
                    if c % 2 == 0:
                        continue
                    k = 4 * half + c // 2
                    dve.wait_ge(os_pe, k + 1)
                    s_new = s0[k % 2]
                    v.tensor_tensor(s_new, s_new, bc(dec[:, k, 8:16], 2, P), ALU.mult).then_inc(us_dve, 1)
                    for i in range(2):
                        dve.wait_ge(us_pe, 2 * k + i + 1)
                        dve.wait_ge(us_dve, 3 * k + 1)
                        part = s_new[:, 4 * i:4 * i + 4, :]
                        v.tensor_tensor(part, part, ps[:, i, :].rearrange("p (b v) -> p b v", v=P), ALU.add
                                        ).then_inc(us_dve, 1)
                dve.wait_ge(os_pe, 4 * (half + 1))
                if half == 1:
                    dve.wait_ge(osr_pe, 1)
                v.tensor_copy(osr, ps[:, 3, 0:P]).then_inc(osr_dve, 1)
                dve.wait_ge(osr_pe, half + 1)
                v.tensor_copy(hout[:, heads, TP:T], ps[:, 3, P:2 * P].rearrange("p (h t) -> p h t", t=TS)
                              ).then_inc(osm_dve, 1)

            dve.wait_ge(hgo_pe, 4)
            for i, (t0, tn) in enumerate(TILES):
                dve.wait_ge(kout_pe, i + 1)
                v.tensor_copy(kstage[0:tn, i, :].rearrange("p (a n) -> p a n", a=2),
                              ps[0:tn, 2 * (i % 2):2 * (i % 2) + 2, :]).then_inc(kout_evac, 1)

            dve.wait_ge(sprompt_stored, 2 * 16)
            zP4 = zP.rearrange("p (g b) h t -> p g b h t", g=NPG)
            for c in range(SLOTS + 1):
                if c == 7:
                    dve.wait_ge(ssample_stored, H * 16)
                    evacuate_rows(N_SV + 2 * 7, 0)
                if c >= 1:
                    dve.wait_ge(zr_pe, c)
                    if c >= 2:
                        dve.wait_ge(zt_pe, c - 1)
                    v.tensor_copy(zrow, ps[:, 7, :]).then_inc(zr_dve, 1)
                if c < SLOTS:
                    dve.wait_ge(ring_used, used(N_SV + 2 * c + 1))
                    v.tensor_copy(keyT[:, :, P:2 * P], ps[:, 2:4, :].rearrange("p a (h s) -> p (a h) s", s=P)
                                  ).then_inc(kT_dve, 1)
                if c >= 1:
                    dve.wait_ge(zt_pe, c)
                    src = ps[:, 7, :].rearrange("p (g h t) -> p g h t", g=NPG, h=H)
                    v.tensor_copy(zP4[:, :, c - 1], src[:, :, :, SS * (c - 1):SS * c]).then_inc(zt_dve, 1)

            dve.wait_ge(hgo_pe, 4)
            for h in range(H + 2):
                if h < H:
                    dve.wait_ge(z_pe, h + 1)
                    if h >= 2:
                        dve.wait_ge(a_ready, h - 1)
                        dve.wait_ge(c_pe, h - 1)
                    x, s, n = zz[h % 2], spl[h % 2], zn[h % 2]
                    v.tensor_scalar(x, ps[:, 2 + h % 2, 0:384], SCALE, biasb[:, h:h + 1], ALU.mult, ALU.add
                                    ).then_inc(z_dve, 1)
                    dve.wait_ge(z_dve, h + 1)
                    v.tensor_tensor(n, x, negmask[:], ALU.add)
                    dve.wait_ge(soft_act, h + 1)
                    link(v.scalar_tensor_tensor(s, x, 0.0, ee[h % 2], ALU.max, ALU.add))
                    v.tensor_tensor(s, s, causal[:], ALU.mult).then_inc(sp_ready, 1)
                if 1 <= h <= H:
                    k = h - 1
                    dve.wait_ge(c_pe, k + 1)
                    dve.wait_ge(sp_ready, k + 1)
                    v.tensor_tensor(zn[k % 2], zn[k % 2], ps[:, 4 + k % 2, 0:384], ALU.subtract).then_inc(d_dve, 1)
                if h >= 2:
                    k = h - 2
                    dve.wait_ge(o_pe, k + 1)
                    v.tensor_copy(mixT[:, H + k, 0:TP], ps[:, 6 + k % 2, 0:TP]).then_inc(o_evac, 1)
                if h == 1:
                    dve.wait_ge(zt_dve, NSEQ)
                    dve.wait_ge(k_stored, 3 * 16)
                    bias = bc(bc(biasb[:], 1, NPG * NSEQ), 3, SS)
                    v.memset(apad, 0.0)
                    v.tensor_scalar(zP, zP, SCALE, None, ALU.mult)
                    dve.wait_ge(ss_pe, 1)
                    link(v.tensor_scalar(zN.rearrange("p h t -> p (h t)"), ps[0:TS, 0, 0:TS * H], SCALE, None,
                                         ALU.mult))
                    v.tensor_tensor(zP, zP, bias, ALU.add)
                    v.tensor_tensor(zN, zN, bc(biasb[0:TS, :], 2, TS), ALU.add).then_inc(ss_dve, 1)
                if h == 2:
                    dve.wait_ge(ss_act, 1)
                    v.scalar_tensor_tensor(sP, zP, 0.0, eP, ALU.max, ALU.add)
                    link(v.scalar_tensor_tensor(sN, zN, 0.0, eN, ALU.max, ALU.add))
                    v.tensor_tensor(zN, zN, bc(neg4[:], 1, H), ALU.add)
                    v.tensor_tensor(sN, sN, bc(strict4[:], 1, H), ALU.mult).then_inc(ss_dve, 1)
                if h == 4:
                    dve.wait_ge(ss_pe, 2)
                    dve.wait_ge(ss_dve, 2)
                    v.tensor_tensor(dP.rearrange("p g h t -> p (g h t)"), zP.rearrange("p g h t -> p (g h t)"),
                                    ps[:, 1, :], ALU.subtract)
                    v.tensor_tensor(dN.rearrange("p h t -> p (h t)"), zN.rearrange("p h t -> p (h t)"),
                                    ps[0:TS, 0, 0:TS * H], ALU.subtract).then_inc(ss_dve, 1)
                if h == 7:
                    dve.wait_ge(ss_pe, 3)
                    v.tensor_copy(orow, ps[:, 0:2, 0:P]).then_inc(ss_dve, 1)
                if h == 9:
                    dve.wait_ge(ss_pe, 4)
                    v.tensor_copy(mixT[:, H:2 * H, TP:T], ps[:, 0, 0:256].rearrange("p (h t) -> p h t", t=TS)
                                  ).then_inc(ss_dve, 1)

            for group in range(2):
                dve.wait_ge(nrs_act, group + 1)
                dst = mixT[:, H * group:H * (group + 1), :]
                ins = v.scalar_tensor_tensor(dst, (hout, dst)[group], normw[:, group:group + 1], rst[group],
                                             ALU.mult, ALU.mult)
                if group == 0:
                    link(ins)
                    ins = v.tensor_tensor(dst, dst, hg, ALU.mult)
                ins.then_inc(nm_dve, 1)

            dve.wait_ge(xa_ready, 1)
            for m in range(KC):
                dve.wait_ge(ring_used, used(N_WO + m))
                o = ps[:, 4 + m % 4, :]
                rs = rT[:, m, TP:T].rearrange("p (b t) -> p b t", t=SS)
                link(v.tensor_tensor(rs, o[:, TP:T].rearrange("p (b t) -> p b t", t=SS), seq(adaT[:, 2, m, 1:R]),
                                     ALU.mult))
                v.scalar_tensor_tensor(rT[:, m, 0:TP], o[:, 0:TP], adaT[:, 2, m, 0:1], xa[:, m, 0:TP],
                                       ALU.mult, ALU.add)
                v.tensor_tensor(rT[:, m, TP:T], rT[:, m, TP:T], xa[:, m, TP:T], ALU.add).then_inc(wo_dve, 1)
            dve.wait_ge(st_pe, KC)
            dve.wait_ge(wo_act, KC)
            v.tensor_scalar(lt1, ps[:, 3, 0:T], 1.0 / D, None, ALU.mult)
            link(v.tensor_scalar(mu, ps[:, 2, 0:T], 1.0 / D, None, ALU.mult))
            link(v.tensor_tensor(rstd, mu, mu, ALU.mult))
            link(v.tensor_tensor(lt1, lt1, rstd, ALU.subtract))
            v.tensor_scalar(lt1, lt1, 0.0, None, ALU.max).then_inc(ln_dve, 1)
            part = rT[:, 0:12, :]
            link(v.tensor_tensor(part, part, bc(mu, 1, 12), ALU.subtract))
            dve.wait_ge(rstd_act, 1)
            for q in range(3):
                part = rT[:, 4 * q:4 * q + 4, :]
                v.tensor_tensor(part, part, bc(rstd, 1, 4), ALU.mult).then_inc(ln_dve, 1)
            for q in range(4):
                ms = slice(4 * q, 4 * q + 4)
                dve.wait_ge(x1_act, 4 * q + 4)
                us, xs = samp(u2T[:, ms, TP:T]), samp(rT[:, ms, TP:T])
                link(v.tensor_tensor(us, xs, seq(adaT[:, 4, ms, 1:R]), ALU.mult))
                for m in range(4 * q, 4 * q + 4):
                    v.tensor_scalar(u2T[:, m, 0:TP], rT[:, m, 0:TP], adaT[:, 4, m, 0:1], adaT[:, 3, m, 0:1],
                                    ALU.mult, ALU.add)
                v.tensor_tensor(us, us, seq(adaT[:, 3, ms, 1:R]), ALU.add).then_inc(u2_dve, 1)

            v.memset(lg, 0.0)
            v.memset(vm, 0.0)
            link(v.memset(onesNE, 1.0))
            v.memset(vm[:, 0:2], 1.0)
            link(v.memset(vm[0:32, 2:3], 1.0))
            dve.wait_ge(rt_pe, 2)
            v.tensor_tensor(lg[:, 0:2, :], ps[:, 5, 0:128].rearrange("p (i n) -> p i n", n=64)[:, :, 0:NL],
                            bc(br[:], 1, 2), ALU.add)
            link(v.tensor_tensor(lg[0:32, 2, :], ps[0:32, 5, 128:128 + NL], br[0:32, :], ALU.add))
            gl = lg[:, :, 0:NG]
            el = lg[:, :, NG:NL].rearrange("p i (g e) -> p i g e", e=NEG)

            def first_max(out, x, m, n):
                link(v.tensor_tensor(out, x, bc(m, 2, n), ALU.is_equal))
                link(v.tensor_tensor(out, out, bc(rev4[:, 0:n], 1, 3), ALU.mult))
                link(v.tensor_reduce(tmp3, out, AX, ALU.max))
                link(v.tensor_tensor(out, out, bc(tmp3, 2, n), ALU.is_equal))

            link(v.tensor_reduce(gmax, gl, AX, ALU.max))
            first_max(gone, gl, gmax, NG)
            v.tensor_tensor(gexp, gl, bc(gmax, 2, NG), ALU.subtract)
            link(v.tensor_tensor(pick, el, bc(gone, 3, NEG), ALU.mult))
            link(v.tensor_reduce(esel, pick.rearrange("p i g e -> p i e g"), AX, ALU.add))
            link(v.tensor_reduce(m1, esel, AX, ALU.max))
            first_max(e1, esel, m1, NEG)
            link(v.tensor_scalar(cand, e1, -3.0e38, None, ALU.mult))
            link(v.tensor_tensor(cand, cand, esel, ALU.add))
            link(v.tensor_reduce(m2, cand, AX, ALU.max))
            first_max(e2, cand, m2, NEG)
            link(v.tensor_tensor(m2, m2, m1, ALU.subtract))
            link(v.tensor_tensor(gone, gone, bc(vm, 2, NG), ALU.mult))
            for k, e in enumerate((e1, e2)):
                for i in range(3):
                    last = v.tensor_tensor(oneh[k][:, i], bc(gone[:, i], 2, NEG), bc(e[:, i], 1, NG), ALU.mult)
            link(last)
            oh = [oneh[k].rearrange("p i g e -> p i (g e)") for k in range(2)]
            v.tensor_tensor(both, oh[0], oh[1], ALU.add).then_inc(rt_dve, 1)

            dve.wait_ge(rt_pe, 3)
            link(v.tensor_copy(cnt, ps[:, 3, 0:NE]))
            link(v.tensor_scalar(nb, cnt, 0.0, None, ALU.is_gt))
            for j in range(1, (T + B - 1) // B):
                link(v.scalar_tensor_tensor(nb, cnt, float(B * j), nb, ALU.is_gt, ALU.add))
            link(v.tensor_tensor_scan(cum, onesNE, nb, 0.0, ALU.mult, ALU.add))
            v.tensor_tensor(base, cum, nb, ALU.subtract)
            link(v.tensor_tensor(ecmp, bc(cum[0:1, :], 1, NB1), bc(iotab[0:1, 0:NB1], 2, NE), ALU.is_le))
            link(v.tensor_reduce(eid, ecmp, AX, ALU.add))
            link(v.tensor_scalar(eid, eid, NE - 1.0, None, ALU.min))
            v.tensor_copy(plan[0:1, 0:NB1], eid)
            v.tensor_copy(plan[0:1, NB1:NB1 + 1], cum[0:1, NE - 1:NE]).then_inc(plan_ready, 1)
            link(v.tensor_copy(rank, ps[:, 2, 0:3 * NE].rearrange("p (i e) -> p i e", e=NE)))
            v.memset(gslot[:], 0.0)
            for k in range(2):
                link(v.tensor_tensor(tmp32, oh[k], rank, ALU.mult))
                link(v.tensor_reduce(rk, tmp32, AX, ALU.add))
                link(v.tensor_scalar(blkr, rk, float(B), None, ALU.is_ge))
                for j in range(2, (T + B - 1) // B):
                    link(v.scalar_tensor_tensor(blkr, rk, float(B * j), blkr, ALU.is_ge, ALU.add))
                link(v.scalar_tensor_tensor(sl, blkr, -float(B), rk, ALU.mult, ALU.add))
                link(v.tensor_tensor(tmp32, oh[k], bc(base, 1, 3), ALU.mult))
                link(v.tensor_reduce(blk, tmp32, AX, ALU.add))
                link(v.tensor_tensor(blk, blk, blkr, ALU.add))
                link(v.scalar_tensor_tensor(gslot[:, k, :], blk, float(B), sl, ALU.mult, ALU.add))
                if k == 0:
                    link(v.tensor_tensor(tokid[:], tokid[:], vm, ALU.mult))
                for i in range(3):
                    v.tensor_scalar(rsel[k][:, i, :], iotab[:], sl[:, i:i + 1], None, ALU.is_equal)
                    last = v.tensor_scalar(bsel[k][:, i, :], iotab[:, 0:NB1], blk[:, i:i + 1], tokid[:, i:i + 1],
                                           ALU.is_equal, ALU.mult)
                if k == 0:
                    link(last)
            last.then_inc(rt_dve, 1)
            dve.wait_ge(rt_pe, 4)
            v.tensor_copy(idxs[:], ps[0:B, 4, 0:NB1]).then_inc(plan_ready, 1)
            dve.wait_ge(rt_act, 2)
            link(v.tensor_reduce(gw, gexp, AX, ALU.add))
            link(v.tensor_scalar(tmp3, m2, 1.0, None, ALU.add))
            link(v.tensor_tensor(gw, gw, tmp3, ALU.mult))
            link(v.reciprocal(gate2[:, 0, :], gw))
            link(v.tensor_tensor(gate2[:, 1, :], gate2[:, 0, :], m2, ALU.mult))
            dve.wait_ge(tt_pe, 24)
            for n, col in enumerate((gslot[:, 0, :], gslot[:, 1, :], gate2[:, 0, :], gate2[:, 1, :])):
                for i in range(3):
                    last = v.tensor_scalar(diag[:, n, i, :], ident[:], col[:, i:i + 1], None, ALU.mult)
            last.then_inc(diag_ready, 1)
            link(v.tensor_scalar(slotid[:, 1:2], tokid[:, 0:1], float(B), -float(B), ALU.is_ge, ALU.mult))
            v.tensor_tensor(slotid[:, 0:1], slotid[:, 1:2], tokid[:, 0:1], ALU.add).then_inc(spread_step, 1)
            dve.wait_ge(u2_stored, 3 * 16)
            for w in (moe_out[0], moe_out[1], sum_s):
                v.memset(w, 0.0)
            dve.wait_ge(where_pe, 1)
            v.tensor_copy(where, ps[:, 2:6, 0:T]).then_inc(spread_ready, 1)

            dve.wait_ge(plan_ready, 2)
            dve.wait_ge(spread_ready, 1)
            nblocks = dve.value_load(plan[0:1, NB1:NB1 + 1], min_val=0, max_val=NBLK)

            def add_up(n):
                for j in range(5):
                    dve.wait_ge(comb_pe, n * 5 + (j + 1))
                    if j == 4:
                        v.tensor_tensor(sum_s, sum_s, ps[:, 7, :], ALU.add).then_inc(sum_dve, 1)
                        continue
                    w = moe_out[j // 2].rearrange("p (r n) -> p r n", r=2)[:, :, 512 * (j % 2):512 * (j % 2 + 1)]
                    if j % 2 == 1:
                        v.tensor_tensor(w, w, ps[:, 5:7, :], ALU.add).then_inc(sum_dve, 1)
                    else:
                        v.tensor_tensor(w[:, 0], w[:, 0], ps[:, 7, :], ALU.add)
                        v.tensor_tensor(w[:, 1], w[:, 1], ps[:, 4, :], ALU.add).then_inc(sum_dve, 1)

            with dve.Fori(0, NBLK) as i:
                with dve.If(i < nblocks):
                    dve.wait_ge(sil_act, i + 1)
                    dve.wait_ge(moe_used, i * MOE_CHUNKS + (MOE_CHUNKS + 8))
                    dve.wait_ge(hT_pe, i + 1)
                    v.tensor_tensor(hid, hsil, ps[:, 3, 0:256], ALU.mult).then_inc(hid_dve, 1)
                    with dve.If(i > 0):
                        add_up(i)
                    dve.wait_ge(hT_pe, i + 2)
                    v.tensor_copy(hT, ps[:, 4, 0:256].rearrange("p (c s) -> p c s", s=P)).then_inc(hT_dve, 1)
                    dve.wait_ge(spread_step, i * 2 + 1)
                    v.scalar_tensor_tensor(spread1, where[:, 0, :], slotid[:, 0:1], where[:, 2, :],
                                           ALU.is_equal, ALU.mult)
                    v.scalar_tensor_tensor(spread, where[:, 1, :], slotid[:, 0:1], where[:, 3, :],
                                           ALU.is_equal, ALU.mult).then_inc(spread_step, 1)
                    dve.wait_ge(spread_step, i * 2 + 2)
                    v.tensor_scalar(slotid[:, 0:1], slotid[:, 0:1], float(B), None, ALU.add).then_inc(spread_step, 1)
                    v.tensor_tensor(spread, spread, spread1, ALU.add).then_inc(spread_ready, 1)
                    dve.wait_ge(moe_used, i * MOE_CHUNKS + 2 * MOE_CHUNKS)
                    v.tensor_copy(yout[:, 512:1024], ps[:, 6, :]).then_inc(y_evac, 1)
            add_up(nblocks)

            dve.wait_ge(g2_act, 4)
            dve.wait_ge(sum_dve, nblocks * 5 + 6)
            dve.sem_inc(wait_carrier, 1)

            def shift_of(i):
                tn = TILES[i][1]
                dve.wait_ge(fin_act, i + 1)
                v.scalar_tensor_tensor(shift[0:tn, i:i + 1], bnag[0:tn, i, 0:1], -1.0, rs1[0:tn, i:i + 1],
                                       ALU.mult, ALU.mult).then_inc(fin_dve, 1)

            for i, (t0, tn) in enumerate(TILES):
                w = moe_out[i][0:tn, :]
                if i < 2:
                    link(v.tensor_tensor(w, w, g2p, ALU.mult))
                    if i == 1:
                        shift_of(0)
                    link(v.tensor_tensor(w, w, xres[:, i, :], ALU.add))
                else:
                    dve.wait_ge(out_s_pool, 1)
                for q in range(4):
                    last = v.bn_stats(bnst[0:tn, q, :], w[:, 512 * q:512 * (q + 1)])
                link(last)
                v.bn_aggr(bnag[0:tn, i, :], bnst[0:tn, :, :].rearrange("p q s -> p (q s)")).then_inc(var_dve, 1)
                if i >= 1:
                    shift_of(i)
            dve.wait_ge(late_loaded, 16)
            for i, (t0, tn) in enumerate(TILES[1:], 1):
                dve.wait_ge(norm_act, i + 1)
                w = moe_out[i][0:tn, :]
                link(v.tensor_tensor(w, w, ln2b[0:tn, 0, :], ALU.mult))
                v.tensor_tensor(w, w, ln2b[0:tn, 1, :], ALU.add).then_inc(fin_dve, 1)

def kernel(**inputs):
    import numpy as np
    import concourse.bacc as bacc
    from concourse.bass_utils import run_bass_kernel_spmd

    a = {k: np.asarray(x) for k, x in inputs.items()}

    def feature_major(x):
        return np.ascontiguousarray(x.reshape(-1, P, KC).transpose(1, 2, 0))

    w_ada = a["w_ada"][0].reshape(P, KC, 6, D)
    perm = w_ada.reshape(P, KC, 6, P, KC).transpose(2, 1, 0, 4, 3).reshape(6, KC, P, D)
    ada = np.concatenate([perm[:5], w_ada[:, :, 5].transpose(1, 0, 2)[None]])
    b_ada = a["b_ada"][0].reshape(6, D)
    w_in = a["w_in"][0].reshape(P, KC, 7, 1024)
    groups = []
    for n, g in enumerate((1, 0, 3, 2, 4, 5, 6)):
        w = w_in[:, :, g]
        if n in (3, 6):
            w = w.reshape(P, 4, 4, 2, 512).transpose(3, 1, 0, 2, 4)
        else:
            w = w.reshape(P, KC, H, P).transpose(2, 0, 1, 3)
        groups.append(w.reshape(SLOTS, P, D))
    w_o = a["w_o"][0].reshape(KC, P, P, KC).transpose(3, 1, 0, 2).reshape(2, SLOTS, P, D)
    arrays = {
        "xT": feature_major(np.concatenate([a["x_prompt"].reshape(-1, D), a["x_sample"].reshape(-1, D)])),
        "cT": feature_major(np.concatenate([a["c_prompt"], a["c_sample"]])),
        "w_ada": ada,
        "b_adaT": b_ada[:5].reshape(5, P, KC).transpose(1, 0, 2),
        "b_g2": b_ada[5].reshape(4, 512),
        "w_in": np.stack(groups),
        "w_o": w_o,
        "w_r": np.concatenate([a["w_gr"][0], a["w_er"][0].reshape(D, NE)], axis=1).reshape(P, KC, NL),
        "b_r": np.concatenate([a["b_gr"][0], a["b_er"][0].reshape(NE)]),
        "lb_logits": a["hg_lb_logits"].reshape(2, H, P).transpose(2, 0, 1),
        "norms": np.stack([a["hg_norm"][0], a["sb_norm"][0]], axis=1),
        "sb_bias": a["sb_bias"][0],
        "ln1": np.stack([a["ln1_g"][0], a["ln1_b"][0]]).reshape(2, P, KC).transpose(1, 0, 2),
        "ln2": np.stack([a["ln2_g"][0], a["ln2_b"][0]]),
        "cache_k": a["cache_k"][0].reshape(NPHYS, PAGE, 1024),
        "cache_v": a["cache_v"][0].reshape(NPHYS, PAGE, 1024),
        "page_table": a["page_table"].reshape(1, NSEQ * NPG),
        "state": a["state_hgrn"][0],
        "w_gate": a["w_gate"][0], "w_up": a["w_up"][0], "w_down": a["w_down"][0],
    }
    arrays = {k: np.ascontiguousarray(x) for k, x in arrays.items()}
    outs = {"y_p": (TP, D), "y_s": (TS, D), "k_p": (TP, 1024), "v_p": (TP, 1024), "s_p": (H, P, P),
            "k_s": (TS, 1024), "v_s": (TS, 1024), "s_s": (NSEQ, H, P, P)}
    nc = bacc.Bacc("TRN2", target_bir_lowering=False, num_devices=1)
    aps = {k: nc.dram_tensor(k, x.shape, mybir.dt.from_np(x.dtype), kind="ExternalInput").ap()
           for k, x in arrays.items()}
    aps |= {k: nc.dram_tensor(k, s, F32, kind="ExternalOutput").ap() for k, s in outs.items()}
    aps["u2_rows"] = nc.dram_tensor("u2_rows", (T, D), F32, kind="Internal").ap()
    layer(nc, **aps)
    r = run_bass_kernel_spmd(nc, [arrays], core_ids=[0]).results[0]
    return (r["y_p"].reshape(1, TP, D), r["y_s"].reshape(NSEQ, SS, D),
            r["k_p"].reshape(1, 1, TP, H, P), r["v_p"].reshape(1, 1, TP, H, P), r["s_p"].reshape(1, 1, H, P, P),
            r["k_s"].reshape(1, NSEQ, SS, H, P), r["v_s"].reshape(1, NSEQ, SS, H, P),
            r["s_s"].reshape(1, NSEQ, H, P, P))
```
